# Optimizing a Trainium2 kernel written in Bass

```python
import math
import jax, jax.numpy as jnp
from jax import lax
import numpy as np

D_MODEL = 1024
BATCH = 1
SEQ = 1024
DEPTH = 2
DEC_BATCH = 8
DEC_SEQ = 4
PAST_LEN = 4096
PAGE_SIZE = 128

N_MIXERS = 2
N_ATTN_LAYERS = (DEPTH + 1) // 2
N_MLSTM_LAYERS = DEPTH // 2
N_META = 16
EPS = 1e-6
ATT_HEADS = 16
ATT_KV_HEADS = 4
ATT_GROUP = ATT_HEADS // ATT_KV_HEADS
ATT_HEAD_DIM = D_MODEL // ATT_HEADS
WINDOW = 128
ATT_BLOCK = 128
NUM_BUCKETS = 32
MAX_DISTANCE = 128
ML_HEADS = 4
ML_DK = (D_MODEL // 2) // ML_HEADS
ML_DV = D_MODEL // ML_HEADS
ML_CHUNK = 64
GATE_SOFTCAP = 15.0
D_FF = 4 * D_MODEL

kernel_name = "hybrid_swa_sink_mlstm_decoder_step"

def rms_norm(x, g):
    xf = x.astype(jnp.float32)
    y = xf * lax.rsqrt(jnp.mean(xf * xf, axis=-1, keepdims=True) + EPS)
    return (y * g.astype(jnp.float32)).astype(x.dtype)

def t5_bucket(dist):
    n = jnp.maximum(dist, 0)
    max_exact = NUM_BUCKETS // 2
    nf = jnp.maximum(n, max_exact).astype(jnp.float32)
    large = max_exact + (jnp.log(nf / max_exact) / math.log(MAX_DISTANCE / max_exact)
                         * (NUM_BUCKETS - max_exact)).astype(jnp.int32)
    large = jnp.minimum(large, NUM_BUCKETS - 1)
    return jnp.where(n < max_exact, n, large)

def rel_bias(dist, rel_table):
    b = rel_table[t5_bucket(dist)].astype(jnp.float32)
    q_len, k_len = dist.shape
    return jnp.transpose(b, (2, 0, 1)).reshape(ATT_KV_HEADS, ATT_GROUP, q_len, k_len)

def window_attention(q, k, v, dist, key_valid, sinks, rel_table):
    *lead, q_len, _, hd = q.shape
    qg = q.reshape(*lead, q_len, ATT_KV_HEADS, ATT_GROUP, hd)
    s = jnp.einsum('...qkgd,...skd->...kgqs', qg, k, preferred_element_type=jnp.float32)
    s = s * (hd ** -0.5) + rel_bias(dist, rel_table)
    mask = ((dist >= 0) & (dist <= WINDOW)) & key_valid[..., None, None, None, :]
    s = jnp.where(mask, s, -jnp.inf)
    sink = sinks.astype(jnp.float32).reshape(ATT_KV_HEADS, ATT_GROUP, 1, 1)
    m = jnp.maximum(jnp.max(s, axis=-1, keepdims=True), sink)
    p = jnp.exp(s - m)
    den = jnp.sum(p, axis=-1, keepdims=True) + jnp.exp(sink - m)
    o = jnp.einsum('...kgqs,...skd->...qkgd', (p / den).astype(v.dtype), v)
    return o.reshape(*lead, q_len, ATT_HEADS * hd)

def attn_project(h, w_qkv, g_q, g_k):
    b, l, _ = h.shape
    qkv = h @ w_qkv
    nq = ATT_HEADS * ATT_HEAD_DIM
    nk = ATT_KV_HEADS * ATT_HEAD_DIM
    q = rms_norm(qkv[..., :nq].reshape(b, l, ATT_HEADS, ATT_HEAD_DIM), g_q)
    k = rms_norm(qkv[..., nq:nq + nk].reshape(b, l, ATT_KV_HEADS, ATT_HEAD_DIM), g_k)
    v = qkv[..., nq + nk:].reshape(b, l, ATT_KV_HEADS, ATT_HEAD_DIM)
    return q, k, v

def attn_prompt(h, w_qkv, g_q, g_k, sinks, w_o, rel_table):
    b, l, _ = h.shape
    q, k, v = attn_project(h, w_qkv, g_q, g_k)
    lead = ATT_BLOCK - N_META
    qp = jnp.pad(q, ((0, 0), (lead, 0), (0, 0), (0, 0)))
    kp = jnp.pad(k, ((0, 0), (lead + ATT_BLOCK, 0), (0, 0), (0, 0)))
    vp = jnp.pad(v, ((0, 0), (lead + ATT_BLOCK, 0), (0, 0), (0, 0)))
    nb = qp.shape[1] // ATT_BLOCK
    qb = qp.reshape(b, nb, ATT_BLOCK, ATT_HEADS, ATT_HEAD_DIM)
    kb = kp.reshape(b, nb + 1, ATT_BLOCK, ATT_KV_HEADS, ATT_HEAD_DIM)
    vb = vp.reshape(b, nb + 1, ATT_BLOCK, ATT_KV_HEADS, ATT_HEAD_DIM)
    k_band = jnp.concatenate([kb[:, :-1], kb[:, 1:]], axis=2)
    v_band = jnp.concatenate([vb[:, :-1], vb[:, 1:]], axis=2)
    dist = jnp.arange(ATT_BLOCK)[:, None] + ATT_BLOCK - jnp.arange(2 * ATT_BLOCK)[None, :]
    k_pos = (jnp.arange(nb)[:, None] * ATT_BLOCK + jnp.arange(2 * ATT_BLOCK)[None, :]
             - (lead + ATT_BLOCK))
    key_valid = k_pos >= 0
    o = window_attention(qb, k_band, v_band, dist, key_valid, sinks, rel_table)
    o = o.reshape(b, nb * ATT_BLOCK, ATT_HEADS * ATT_HEAD_DIM)[:, lead:]
    return o @ w_o, k[:, -WINDOW:], v[:, -WINDOW:]

def attn_sample(h, cache_k, cache_v, w_qkv, g_q, g_k, sinks, w_o, rel_table):
    s_len = h.shape[1]
    q, k, v = attn_project(h, w_qkv, g_q, g_k)
    win = cache_k.shape[1]
    k_all = jnp.concatenate([cache_k.astype(k.dtype), k], axis=1)
    v_all = jnp.concatenate([cache_v.astype(v.dtype), v], axis=1)
    dist = (win + jnp.arange(s_len))[:, None] - jnp.arange(win + s_len)[None, :]
    key_valid = jnp.ones((win + s_len,), dtype=bool)
    o = window_attention(q, k_all, v_all, dist, key_valid, sinks, rel_table)
    return o @ w_o, k_all[:, -win:], v_all[:, -win:]

def mlstm_chunk(carry, inputs):
    c_prev, n_prev, m_prev = carry
    q, k, v, logi, logf = inputs
    lc = q.shape[2]
    bcum = jnp.cumsum(logf, axis=-1)
    causal = jnp.tril(jnp.ones((lc, lc), dtype=bool))
    dmat = jnp.where(causal, bcum[..., :, None] - bcum[..., None, :] + logi[..., None, :], -jnp.inf)
    inter = bcum + m_prev[..., None]
    m_row = jnp.maximum(inter, jnp.max(dmat, axis=-1))
    w_inter = jnp.exp(inter - m_row)
    scores = jnp.einsum('bhtd,bhjd->bhtj', q, k) * jnp.exp(dmat - m_row[..., None])
    num = (w_inter[..., None] * jnp.einsum('bhtd,bhdv->bhtv', q, c_prev)
           + jnp.einsum('bhtj,bhjv->bhtv', scores, v))
    den = w_inter * jnp.einsum('bhtd,bhd->bht', q, n_prev) + jnp.sum(scores, axis=-1)
    h = num / jnp.maximum(jnp.abs(den), jnp.exp(-m_row))[..., None]
    b_last = bcum[..., -1]
    gk = b_last[..., None] - bcum + logi
    m_new = jnp.maximum(b_last + m_prev, jnp.max(gk, axis=-1))
    a = jnp.exp(b_last + m_prev - m_new)
    wk = jnp.exp(gk - m_new[..., None])
    c_new = a[..., None, None] * c_prev + jnp.einsum('bhj,bhjd,bhjv->bhdv', wk, k, v)
    n_new = a[..., None] * n_prev + jnp.einsum('bhj,bhjd->bhd', wk, k)
    return (c_new, n_new, m_new), h

def mlstm_project(h, w_in, w_gate, b_gate):
    b, l, _ = h.shape
    z = h @ w_in
    nqk = ML_HEADS * ML_DK
    nv = ML_HEADS * ML_DV

    def heads(t, d):
        return t.reshape(b, l, ML_HEADS, d).transpose(0, 2, 1, 3).astype(jnp.float32)

    q = heads(z[..., :nqk], ML_DK)
    k = heads(z[..., nqk:2 * nqk], ML_DK) * (ML_DK ** -0.5)
    v = heads(z[..., 2 * nqk:2 * nqk + nv], ML_DV)
    o = z[..., 2 * nqk + nv:]
    g = (h @ w_gate + b_gate).astype(jnp.float32)
    g = GATE_SOFTCAP * jnp.tanh(g / GATE_SOFTCAP)
    logi = g[..., :ML_HEADS].transpose(0, 2, 1)
    logf = jax.nn.log_sigmoid(g[..., ML_HEADS:]).transpose(0, 2, 1)
    return (q, k, v, logi, logf), o

def mlstm_output(hh, o, g_norm, w_out, dtype):
    b, _, l, _ = hh.shape
    hh = hh.transpose(0, 2, 1, 3)
    hn = hh * lax.rsqrt(jnp.mean(hh * hh, axis=-1, keepdims=True) + EPS)
    hn = hn * g_norm.astype(jnp.float32).reshape(ML_HEADS, ML_DV)
    out = (jax.nn.sigmoid(o.astype(jnp.float32)) * hn.reshape(b, l, ML_HEADS * ML_DV)).astype(dtype)
    return out @ w_out

def mlstm_prompt(h, w_in, w_gate, b_gate, g_norm, w_out):
    b = h.shape[0]
    ins, o = mlstm_project(h, w_in, w_gate, b_gate)
    state0 = (jnp.zeros((b, ML_HEADS, ML_DK, ML_DV), jnp.float32),
              jnp.zeros((b, ML_HEADS, ML_DK), jnp.float32),
              jnp.zeros((b, ML_HEADS), jnp.float32))
    meta_in = tuple(t[:, :, :N_META] for t in ins)
    rest_in = tuple(t[:, :, N_META:] for t in ins)
    state1, h_meta = mlstm_chunk(state0, meta_in)
    nc = rest_in[0].shape[2] // ML_CHUNK

    def to_chunks(t):
        return jnp.moveaxis(t.reshape(b, ML_HEADS, nc, ML_CHUNK, *t.shape[3:]), 2, 0)

    state, h_rest = lax.scan(mlstm_chunk, state1, tuple(to_chunks(t) for t in rest_in))
    h_rest = jnp.moveaxis(h_rest, 0, 2).reshape(b, ML_HEADS, nc * ML_CHUNK, ML_DV)
    hh = jnp.concatenate([h_meta, h_rest], axis=2)
    return mlstm_output(hh, o, g_norm, w_out, h.dtype), state

def mlstm_sample(h, c0, n0, m0, w_in, w_gate, b_gate, g_norm, w_out):
    ins, o = mlstm_project(h, w_in, w_gate, b_gate)
    state = (c0.astype(jnp.float32), n0.astype(jnp.float32), m0.astype(jnp.float32))
    state, hh = mlstm_chunk(state, ins)
    return mlstm_output(hh, o, g_norm, w_out, h.dtype), state

def sqrelu_mlp(h, w_up, w_down):
    return jnp.square(jax.nn.relu(h @ w_up)) @ w_down

def setup_inputs(seed: int = 0) -> dict:
    key = jax.random.key(seed)
    ks = jax.random.split(key, 24)
    nrm = jax.random.normal
    f32 = jnp.float32
    win_buf = min(WINDOW, PAST_LEN)
    qkv_w = (ATT_HEADS + 2 * ATT_KV_HEADS) * ATT_HEAD_DIM
    ml_in_w = 2 * ML_HEADS * ML_DK + 2 * ML_HEADS * ML_DV
    b_gate = jnp.concatenate([0.1 * nrm(ks[20], (N_MLSTM_LAYERS, ML_HEADS), f32),
                              3.0 + 0.1 * nrm(ks[21], (N_MLSTM_LAYERS, ML_HEADS), f32)], axis=-1)
    return {
        "x_prompt": nrm(ks[0], (BATCH, SEQ, D_MODEL), f32),
        "x_sample": nrm(ks[1], (DEC_BATCH, DEC_SEQ, D_MODEL), f32),
        "cache_k": nrm(ks[2], (N_ATTN_LAYERS, DEC_BATCH, win_buf, ATT_KV_HEADS, ATT_HEAD_DIM), f32),
        "cache_v": nrm(ks[3], (N_ATTN_LAYERS, DEC_BATCH, win_buf, ATT_KV_HEADS, ATT_HEAD_DIM), f32),
        "state_C": nrm(ks[4], (N_MLSTM_LAYERS, DEC_BATCH, ML_HEADS, ML_DK, ML_DV), f32),
        "state_n": nrm(ks[5], (N_MLSTM_LAYERS, DEC_BATCH, ML_HEADS, ML_DK), f32),
        "state_m": nrm(ks[6], (N_MLSTM_LAYERS, DEC_BATCH, ML_HEADS), f32),
        "meta_tokens": nrm(ks[7], (N_META, D_MODEL), f32),
        "rel_table": 0.5 * nrm(ks[8], (NUM_BUCKETS, ATT_HEADS), f32),
        "norm_mix": 1.0 + 0.02 * nrm(ks[9], (DEPTH, D_MODEL), f32),
        "norm_mlp": 1.0 + 0.02 * nrm(ks[10], (DEPTH, D_MODEL), f32),
        "attn_w_qkv": nrm(ks[11], (N_ATTN_LAYERS, D_MODEL, qkv_w), f32) * D_MODEL ** -0.5,
        "attn_q_norm": 1.0 + 0.02 * nrm(ks[12], (N_ATTN_LAYERS, ATT_HEAD_DIM), f32),
        "attn_k_norm": 1.0 + 0.02 * nrm(ks[13], (N_ATTN_LAYERS, ATT_HEAD_DIM), f32),
        "attn_sinks": 0.5 * nrm(ks[14], (N_ATTN_LAYERS, ATT_HEADS), f32),
        "attn_w_o": nrm(ks[15], (N_ATTN_LAYERS, ATT_HEADS * ATT_HEAD_DIM, D_MODEL), f32) * (ATT_HEADS * ATT_HEAD_DIM) ** -0.5,
        "mlstm_w_in": nrm(ks[16], (N_MLSTM_LAYERS, D_MODEL, ml_in_w), f32) * D_MODEL ** -0.5,
        "mlstm_w_gate": nrm(ks[17], (N_MLSTM_LAYERS, D_MODEL, 2 * ML_HEADS), f32) * D_MODEL ** -0.5,
        "mlstm_b_gate": b_gate,
        "mlstm_out_norm": 1.0 + 0.02 * nrm(ks[18], (N_MLSTM_LAYERS, ML_HEADS * ML_DV), f32),
        "mlstm_w_out": nrm(ks[19], (N_MLSTM_LAYERS, ML_HEADS * ML_DV, D_MODEL), f32) * (ML_HEADS * ML_DV) ** -0.5,
        "mlp_w_up": nrm(ks[22], (DEPTH, D_MODEL, D_FF), f32) * D_MODEL ** -0.5,
        "mlp_w_down": nrm(ks[23], (DEPTH, D_FF, D_MODEL), f32) * D_FF ** -0.5,
    }

def reference(x_prompt, x_sample, cache_k, cache_v, state_C, state_n, state_m,
              meta_tokens, rel_table, norm_mix, norm_mlp,
              attn_w_qkv, attn_q_norm, attn_k_norm, attn_sinks, attn_w_o,
              mlstm_w_in, mlstm_w_gate, mlstm_b_gate, mlstm_out_norm, mlstm_w_out,
              mlp_w_up, mlp_w_down):
    b = x_prompt.shape[0]
    meta = jnp.broadcast_to(meta_tokens.astype(x_prompt.dtype)[None], (b, N_META, D_MODEL))
    xp = jnp.concatenate([meta, x_prompt], axis=1)
    xs = x_sample
    kp_l, vp_l, ks_l, vs_l = [], [], [], []
    cp_l, np_l, mp_l, cs_l, ns_l, ms_l = [], [], [], [], [], []
    for i in range(DEPTH):
        hp = rms_norm(xp, norm_mix[i])
        hs = rms_norm(xs, norm_mix[i])
        j = i // N_MIXERS
        if i % N_MIXERS == 0:
            op, kp, vp = attn_prompt(hp, attn_w_qkv[j], attn_q_norm[j], attn_k_norm[j],
                                     attn_sinks[j], attn_w_o[j], rel_table)
            os_, kn, vn = attn_sample(hs, cache_k[j], cache_v[j], attn_w_qkv[j], attn_q_norm[j],
                                      attn_k_norm[j], attn_sinks[j], attn_w_o[j], rel_table)
            kp_l.append(kp); vp_l.append(vp)
            ks_l.append(kn.astype(cache_k.dtype)); vs_l.append(vn.astype(cache_v.dtype))
        else:
            op, (cp, n_p, mp) = mlstm_prompt(hp, mlstm_w_in[j], mlstm_w_gate[j], mlstm_b_gate[j],
                                             mlstm_out_norm[j], mlstm_w_out[j])
            os_, (cs, n_s, ms) = mlstm_sample(hs, state_C[j], state_n[j], state_m[j],
                                              mlstm_w_in[j], mlstm_w_gate[j], mlstm_b_gate[j],
                                              mlstm_out_norm[j], mlstm_w_out[j])
            cp_l.append(cp.astype(x_prompt.dtype)); np_l.append(n_p.astype(x_prompt.dtype))
            mp_l.append(mp.astype(x_prompt.dtype))
            cs_l.append(cs.astype(state_C.dtype)); ns_l.append(n_s.astype(state_n.dtype))
            ms_l.append(ms.astype(state_m.dtype))
        xp = xp + op
        xs = xs + os_
        xp = xp + sqrelu_mlp(rms_norm(xp, norm_mlp[i]), mlp_w_up[i], mlp_w_down[i])
        xs = xs + sqrelu_mlp(rms_norm(xs, norm_mlp[i]), mlp_w_up[i], mlp_w_down[i])
    y_prompt = xp[:, N_META:]
    y_sample = xs
    return (y_prompt, y_sample,
            jnp.stack(kp_l), jnp.stack(vp_l), jnp.stack(ks_l), jnp.stack(vs_l),
            jnp.stack(cp_l), jnp.stack(np_l), jnp.stack(mp_l),
            jnp.stack(cs_l), jnp.stack(ns_l), jnp.stack(ms_l))


_drawn_inputs = setup_inputs


def setup_inputs(seed=0):
    import zlib

    import numpy as np

    out = dict(_drawn_inputs(seed))
    spreads = {}
    factors = {'attn_q_norm': 8.0, 'attn_k_norm': 2.831, 'attn_sinks': 64.0, 'mlstm_out_norm': 24.536}
    for name, (base, spread) in spreads.items():
        noise = np.random.default_rng([zlib.crc32(name.encode()), seed]).standard_normal(out[name].shape)
        drawn = base * np.exp(spread * noise) if base else spread * noise
        out[name] = __import__('jax').numpy.asarray(drawn.astype(out[name].dtype))
    for name, factor in factors.items():
        out[name] = (out[name] * factor).astype(out[name].dtype)
    return out
```

```python
from contextlib import ExitStack

import numpy as np

import concourse.bass as bass
from concourse import mybir

F32 = mybir.dt.float32
F32R = mybir.dt.float32r
ACT = mybir.ActivationFunctionType
ALU = mybir.AluOpType
AX = mybir.AxisListType.X

P = 128
D = 1024
KC = D // P
SEQ, META, NB, NS = 1024, 16, 8, 4
SAMPLE = NB * NS
BLK = 128
NBLK = SEQ // BLK
COL_S = SEQ
COL_M = SEQ + SAMPLE
T = SEQ + SAMPLE + META
TG = 358
TP = 3 * TG
TILES = NBLK + 1
LAST = SAMPLE + META
EPS = 1e-6
QH, KH, HD, WIN = 16, 4, 64, 128
MH, DK, DV = 4, 128, 256
VH = DV + 1
FF = 4096
SLICES = 8
NEG = -1e30
CAP = 15.0
BUCKETS, MAX_DISTANCE = 32, 128
LINE = 384

U_QKV, U_WO, U_MLP0 = 0, 12, 20
U_IN = U_MLP0 + 8 * SLICES
U_OUT = U_IN + 24
U_MLP1 = U_OUT + 8
U_END = U_MLP1 + 8 * SLICES
N_QKV, N_WO, N_MLP0 = 0, 12, 20
N_IN = N_MLP0 + 12 * SLICES
N_OUT = N_IN + 25
N_MLP1 = N_OUT + 8
AHEAD = 2


def outs_through(u):
    if u < U_MLP0:
        return u + 1
    if u < U_IN:
        i, j = divmod(u - U_MLP0, 8)
        return N_MLP0 + 12 * i + (j + 1 if j < 4 else 2 * j - 2)
    if u < U_OUT:
        return N_IN + 1 + (u - U_IN) + 1
    if u < U_MLP1:
        return N_OUT + (u - U_OUT) + 1
    i, j = divmod(u - U_MLP1, 8)
    return N_MLP1 + 12 * i + (j + 1 if j < 4 else 2 * j - 2)


def is_down(u):
    for u0 in (U_MLP0, U_MLP1):
        if u0 <= u < u0 + 8 * SLICES:
            return (u - u0) % 8 >= 4
    return False


def shape_constants():
    c = {}
    c["ident"] = np.eye(P, dtype=np.float32)
    c["ones"] = np.ones((P, P), np.float32)
    two = np.zeros((P, P), np.float32)
    two[:HD, :HD] = 1.0
    two[HD:, HD:] = 1.0
    c["head_ones"] = two
    j, t = np.arange(P)[:, None], np.arange(P)[None, :]
    c["causal"] = np.where(j <= t, 0.0, NEG).astype(np.float32)
    js, ts = j[:SAMPLE], t[:, :SAMPLE]
    own = (js // NS == ts // NS) & (js <= ts)
    c["own_causal"] = np.zeros((P, SAMPLE), np.float32)
    c["own_causal"][:SAMPLE] = np.where(own, 0.0, NEG)
    return c


def selector_constants():
    sel = np.zeros((P, 8, P), np.float32)
    for h in range(MH):
        sel[64 + h, h, :] = 1.0
        sel[96 + h, 4 + h, :] = 1.0
    pair = np.zeros((P, MH), np.float32)
    for h in range(MH):
        pair[h, h] = pair[32 + h, h] = 1.0
    return np.concatenate([sel.reshape(P, -1), pair], axis=1)


def bucket_constant():
    out = np.zeros((BUCKETS + 1, LINE), np.float32)
    exact = BUCKETS // 2
    for e in range(LINE):
        dist = 2 * BLK - 1 - e
        if 0 <= dist <= WIN:
            b = dist if dist < exact else exact + int(
                np.log(dist / exact) / np.log(MAX_DISTANCE / exact) * (BUCKETS - exact) + 1e-6)
            out[min(b, BUCKETS - 1), e] = 1.0
        else:
            out[BUCKETS, e] = NEG
    return out


def scan_constant():
    keep = np.ones((MH, TP), np.float32)
    keep[:, 0:SEQ:BLK] = 0.0
    keep[:, COL_S:COL_M:NS] = 0.0
    keep[:, COL_M] = 0.0
    return keep


CONST = shape_constants()
CONST_AT, _n = {}, 0
for _k, _v in CONST.items():
    CONST_AT[_k] = (_n, _n + _v.shape[1])
    _n += _v.shape[1]
CONST_COLS = _n


def build(nc, a, out, scratch):
    with ExitStack() as ctx:
        R0 = 16512
        R1 = R0 + 37024
        R2 = R1 + 34368
        R3 = R2 + 34368
        RAW = R3 + 34368
        WHI = RAW + 16384
        WLO = WHI + 16384
        R4 = WLO + 16384
        BUF = 4320
        RC = R4 + 4 * BUF

        def at(name, offset, shape, dt=F32):
            return nc.alloc_sbuf_tensor_at(name, shape, dt, offset=offset)

        x = at("x", R0, [P, KC, TP])
        x_tok = at("x_tok", R1, [P, TILES, D])
        h_hi = at("h_hi", R1, [P, KC, TP], F32R)
        h_lo = at("h_lo", R2, [P, KC, TP], F32R)
        act_hi = at("act_hi", R3, [P, 4, TP], F32R)
        act_lo = at("act_lo", R3 + 4 * TP * 4, [P, 4, TP], F32R)
        raw = at("raw", RAW, [P, 2, 2048])
        w_hi = at("w_hi", WHI, [P, 4, 1024], F32R)
        w_lo = at("w_lo", WLO, [P, 4, 1024], F32R)
        sq = [at(f"sq{i}", R4 + i * BUF, [P, TP]) for i in range(2)]
        h32 = [at(f"h32_{i}", R4 + i * BUF, [P, TP]) for i in range(2)]
        relu = [at(f"relu{i}", R4 + i * BUF, [P, TP]) for i in range(2)]
        rstd = at("rstd", R4 + 2 * BUF, [P, 3, TG])
        relu_sq = at("relu_sq", R4 + 2 * BUF, [P, TP])
        q = at("q", R3, [P, KC, TP])
        kn = at("kn", R0, [P, 2, TP])
        v_tok = at("v_tok", R0 + 8608, [P, TILES, KH * HD])
        bias = at("bias", R0 + 8608 + 9216, [P, QH, 2 * BLK])
        v_meta = at("v_meta", R0 + 8608 + 9216 + 16384, [META, KH * HD])
        vT = [at("vT0", R4 + 3 * BUF, [P, TP]), at("vT1", R4, [P, TP])]
        cst = at("cst", RC, [P, CONST_COLS])
        at_c = RC + (CONST_COLS * 4 + 31) // 32 * 32
        gain = at("gain", at_c, [P, 4, KC])
        qk_gain = at("qk_gain", at_c + 128, [P, 2])
        sinks = at("sinks", at_c + 160, [P, QH])
        nsinks = at("nsinks", at_c + 224, [P, QH])
        eps = at("eps", at_c + 288, [P, 1])
        tokout = [at(f"tokout{i}", at_c + 320 + i * 1024, [P, 256]) for i in range(2)]
        ident = cst[:, slice(*CONST_AT["ident"])]
        ones = cst[:, slice(*CONST_AT["ones"])]
        head_ones = cst[:, slice(*CONST_AT["head_ones"])]

        ps = ctx.enter_context(nc.psum_tensor("ps", [P, 8, 512], F32))

        def grp(ap):
            return ap.rearrange("p (g n) -> p g n", g=3)

        def sem(name):
            return ctx.enter_context(nc.semaphore(name))

        x_in = [sem(f"x_in{c}") for c in range(TILES)]
        const_in = sem("const_in")
        consts_ready = sem("consts_ready")
        xt_ready = sem("xt_ready")
        x_by_act, x_by_dve = sem("x_by_act"), sem("x_by_dve")
        raw_in = [sem("raw_in0"), sem("raw_in1")]
        w_hi_ready, w_lo_ready = sem("w_hi_ready"), sem("w_lo_ready")
        out_ready = sem("out_ready")
        free_act, free_dve = sem("free_act"), sem("free_dve")
        norm_sq, norm_summed = sem("norm_sq"), sem("norm_summed")
        norm_ln, norm_rstd = sem("norm_ln"), sem("norm_rstd")
        norm_h, norm_hi, norm_lo = sem("norm_h"), sem("norm_hi"), sem("norm_lo")
        x_saved, x_back = sem("x_saved"), sem("x_back")
        qk_sum, qk_ln, qk_rstd, qk_normed = sem("qk_sum"), sem("qk_ln"), sem("qk_rstd"), sem("qk_normed")
        vt_ready, v_taken = sem("vt_ready"), sem("v_taken")
        up_done, act_split, sq_done = sem("up_done"), sem("act_split"), sem("sq_done")
        line_out = sem("line_out")
        cache_t, cache_c, stored = sem("cache_t"), sem("cache_c"), sem("stored")

        raw_k8 = raw[:, :, :].rearrange("p s (k n) -> p s k n", k=8)
        raw_k4 = raw[:, :, :].rearrange("p s (k n) -> p s k n", k=4)
        raw_per = [64] * 4 + [16] * 2 + [64] * 4 + [16] * 200

        def raw_target(r):
            return sum(raw_per[r % 2:r + 1:2])

        def raw_unit(j, slot, down):
            if down:
                return raw_k4[:, slot, :, 256 * j:256 * j + 256]
            return raw_k8[:, slot, :, 128 * j:128 * j + 128]

        def unit_view(w, slot, down):
            return w[:, slot, :].rearrange("p (k n) -> p k n", k=4 if down else 8)

        def split_hi(act, slot, rslot, j, down, raw_wait, outs_wait):
            act.wait_ge(raw_in[rslot], raw_wait)
            if outs_wait is not None:
                act.wait_ge(out_ready, outs_wait)
            nc.scalar.activation(unit_view(w_hi, slot, down), raw_unit(j, rslot, down),
                                 ACT.Copy).then_inc(w_hi_ready, 1)

        def split_lo(dve, slot, rslot, j, down, hi_wait):
            dve.wait_ge(w_hi_ready, hi_wait)
            nc.vector.tensor_tensor(unit_view(w_lo, slot, down), raw_unit(j, rslot, down),
                                    unit_view(w_hi, slot, down).bitcast(F32), ALU.subtract
                                    ).then_inc(w_lo_ready, 1)

        def split_hi_static(act, u):
            if u < U_END:
                split_hi(act, u % 4, (u // 2) % 2, u % 2, is_down(u), raw_target(u // 2),
                         outs_through(u - 4) if u >= 4 else None)

        def split_lo_static(dve, u):
            if u < U_END:
                split_lo(dve, u % 4, (u // 2) % 2, u % 2, is_down(u), u + 1)

        def freed(n):
            if n < N_WO:
                return free_act, n + 1
            if n < N_MLP0:
                return free_dve, n - N_WO + 1
            if n < N_IN:
                i, o = divmod(n - N_MLP0, 12)
                return (free_act, 12 + 4 * i + o + 1) if o < 4 else (free_dve, 8 + 8 * i + o - 3)
            if n < N_OUT:
                return free_act, 12 + 4 * SLICES + n - N_IN + 1
            if n < N_MLP1:
                return free_dve, 8 + 8 * SLICES + n - N_OUT + 1
            raise AssertionError

        FA_MLP = {N_MLP0: 12, N_MLP1: 12 + 4 * SLICES + 25}
        FD_MLP = {N_MLP0: 8, N_MLP1: 16 + 8 * SLICES}

        def out_banks(n):
            return 3 * (n % 2)

        def chunk_mms(slot, k, kc, cols, bank, hi, lo, k_of, start, stop, groups=None):
            wh = w_hi[:, slot, :].rearrange("p (k n) -> p k n", k=kc)[:, k, cols]
            wl = w_lo[:, slot, :].rearrange("p (k n) -> p k n", k=kc)[:, k, cols]
            for g in range(3):
                o = ps[:, bank + g, 0:TG]
                c = slice(g * TG, g * TG + TG)
                nc.tensor.matmul(o, wh, hi[:, k_of, c], start=start, stop=False)
                nc.tensor.matmul(o, wh, lo[:, k_of, c], start=False, stop=False)
            for g in range(3):
                last = nc.tensor.matmul(ps[:, bank + g, 0:TG], wl, hi[:, k_of, g * TG:g * TG + TG],
                                        start=False, stop=stop)
            return last

        def pe_unit(pe, u, n, hi, lo, sides=None, first_norm=None):
            pe.wait_ge(w_lo_ready, u + 1)
            if n >= 2:
                pe.wait_ge(*freed(n - 2))
            for k in range(KC):
                if first_norm is not None:
                    pe.wait_ge(norm_lo, KC * first_norm + k + 1)
                if sides and k in (2, 4, 6):
                    sides(k // 2 - 1)
                last = chunk_mms(u % 4, k, 8, slice(0, P), out_banks(n), hi, lo, k, k == 0, k == KC - 1)
            last.then_inc(out_ready, 1)

        def norm_pe(pe, m, before):
            before()
            for f in range(KC):
                pe.wait_ge(norm_sq, KC * m + f + 1)
                for g in range(3):
                    last = nc.tensor.matmul(ps[:, g, 0:TG], ones, sq[f % 2][:, g * TG:g * TG + TG],
                                            start=f == 0, stop=f == KC - 1)
                last.then_inc(norm_summed, 1)

        def norm_act(act, m, x=x):
            for f in range(KC):
                if KC * m + f >= 2:
                    act.wait_ge(norm_summed, KC * m + f - 1)
                nc.scalar.activation(sq[f % 2][:, :], x[:, f, :], ACT.Square).then_inc(norm_sq, 1)
            act.wait_ge(norm_summed, KC * m + KC)
            nc.scalar.activation(rstd[:, :, :], ps[:, 0:3, 0:TG], ACT.Ln, scale=1.0 / D,
                                 bias=eps[:, 0:1]).then_inc(norm_ln, 1)
            act.wait_ge(norm_ln, m + 1)
            nc.scalar.activation(rstd[:, :, :], rstd[:, :, :], ACT.Exp, scale=-0.5).then_inc(norm_rstd, 1)
            for f in range(KC):
                act.wait_ge(norm_h, KC * m + f + 1)
                nc.scalar.activation(h_hi[:, f, :], h32[f % 2][:, :], ACT.Copy).then_inc(norm_hi, 1)

        def norm_dve(dve, m, x=x, h_lo=h_lo):
            dve.wait_ge(norm_rstd, m + 1)
            for f in range(KC + 1):
                if f < KC:
                    if KC * m + f >= 2:
                        dve.wait_ge(norm_lo, KC * m + f - 1)
                    nc.vector.scalar_tensor_tensor(out=h32[f % 2][:, :], in0=x[:, f, :],
                                                   scalar=gain[:, m, f:f + 1],
                                                   in1=rstd[:, :, :].rearrange("p g n -> p (g n)"),
                                                   op0=ALU.mult, op1=ALU.mult).then_inc(norm_h, 1)
                if f:
                    dve.wait_ge(norm_hi, KC * m + f)
                    nc.vector.tensor_tensor(h_lo[:, f - 1, :], h32[(f - 1) % 2][:, :],
                                            h_hi[:, f - 1, :].bitcast(F32), ALU.subtract
                                            ).then_inc(norm_lo, 1)

        def x_rows(c):
            return BLK if c < NBLK else LAST

        small = [(cst[:, :], a["const"]),
                 (gain[:, 0, :], a["norm_mix"][0].rearrange("(k p) -> p k", p=P)),
                 (gain[:, 1, :], a["norm_mlp"][0].rearrange("(k p) -> p k", p=P)),
                 (gain[:, 2, :], a["norm_mix"][1].rearrange("(k p) -> p k", p=P)),
                 (gain[:, 3, :], a["norm_mlp"][1].rearrange("(k p) -> p k", p=P))]
        for half in range(2):
            small += [(qk_gain[HD * half:HD * half + HD, 0:1], a["attn_q_norm"].rearrange("a d -> d a")),
                      (qk_gain[HD * half:HD * half + HD, 1:2], a["attn_k_norm"].rearrange("a d -> d a"))]
        for s in range(4):
            gp, ip = divmod(s, 2)
            small += [(sinks[:, 4 * s:4 * s + 4].rearrange("p (a b) -> p a b", a=2),
                       bass.AP(a["attn_sinks"].tensor, 8 * gp + 2 * ip, [[0, P], [4, 2], [1, 2]]))]

        def load_x(sp):
            for c in range(TILES):
                if c < NBLK:
                    sp.dma_start(x_tok[:, c, :], a["x_prompt"][0, c * P:c * P + P, :]).then_inc(x_in[c], 16)
                else:
                    sp.dma_start(x_tok[0:SAMPLE, c, :], a["x_sample"].rearrange("b s d -> (b s) d")
                                 ).then_inc(x_in[c], 16)
                    sp.dma_start(x_tok[SAMPLE:LAST, c, :], a["meta_tokens"]).then_inc(x_in[c], 16)

        def x_tile_wait(eng, c):
            eng.wait_ge(x_in[c], 16 if c < NBLK else 32)

        def load_pe(pe):
            pe.wait_ge(const_in, 16 * len(small))
            for c in range(TILES):
                x_tile_wait(pe, c)
                n = x_rows(c)
                for half in range(2):
                    i = 2 * c + half
                    if i >= 8:
                        pe.wait_ge((x_by_act, x_by_dve)[half], (i - 8) // 2 + 1)
                    for f in range(4):
                        last = nc.tensor.transpose(ps[:, i % 8, f * P:f * P + n],
                                                   x_tok[0:n, c, (4 * half + f) * P:(4 * half + f + 1) * P],
                                                   ident[0:n, 0:n])
                    last.then_inc(xt_ready, 1)

        def take_x(eng, c, half):
            n = x_rows(c)
            eng.wait_ge(xt_ready, 2 * c + half + 1)
            src = ps[:, (2 * c + half) % 8, :].rearrange("p (f n) -> p f n", f=4)[:, :, 0:n]
            return x[:, 4 * half:4 * half + 4, c * P:c * P + n], src

        def load_qkv(sp, r):
            w = a["attn_w_qkv"][0].rearrange("(k p) n -> p k n", p=P)
            if r < 4:
                gp, i = r // 2, 2 * (r % 2)
                dst = raw_k8[:, r % 2, :, :].rearrange("p k (c g d) -> p k c g d", c=2, g=2)
                for g in range(2):
                    for c in range(2):
                        c0 = gp * 512 + g * 256 + (i + c) * HD
                        sp.dma_start(dst[:, :, c, g, :], w[:, :, c0:c0 + HD]).then_inc(raw_in[r % 2], 16)
            else:
                sp.dma_start(raw_k8[:, r % 2, :, :], w[:, :, 256 * r:256 * r + 256]).then_inc(raw_in[r % 2], 16)

        def load_wo(sp, r):
            w = a["attn_w_o"][0].rearrange("(gp g i d) n -> gp g d i n", gp=2, g=2, i=4)
            c0 = 256 * (r - U_WO // 2)
            for gp in range(2):
                for g in range(2):
                    sp.dma_start(raw_k8[HD * g:HD * g + HD, r % 2, 4 * gp:4 * gp + 4, :],
                                 w[gp, g][:, :, c0:c0 + 256]).then_inc(raw_in[r % 2], 16)

        def load_cols(sp, w, r, c0):
            sp.dma_start(raw_k8[:, r % 2, :, :],
                         w.rearrange("(k p) n -> p k n", p=P)[:, :, c0:c0 + 256]).then_inc(raw_in[r % 2], 16)

        def qk_dst(c):
            return q[:, c, :] if c < 8 else kn[:, c - 8, :]

        def side_bank(s):
            return 6 + s % 2

        def qkv_side_pe(pe, c, g):
            s = 3 * c + g
            if s >= 2:
                t = s - 2
                pe.wait_ge(qk_ln, t + 1) if t < 30 else pe.wait_ge(v_taken, t - 29)
            if c < 10:
                if g == 0:
                    pe.wait_ge(free_act, c + 1)
                nc.tensor.matmul(ps[:, side_bank(s), 0:TG], head_ones, sq[c % 2][:, g * TG:g * TG + TG],
                                 start=True, stop=True).then_inc(qk_sum, 1)
            else:
                if g == 0:
                    pe.wait_ge(free_act, c + 1)
                src = vT[c - 10]
                for t in range(4 * g, min(4 * g + 4, TILES)):
                    n = x_rows(t)
                    last = nc.tensor.transpose(ps[0:n, side_bank(s), (t % 4) * P:(t % 4) * P + P],
                                               src[:, t * P:t * P + n], ident)
                last.then_inc(vt_ready, 1)

        def qkv_pe(pe):
            for c in range(12):
                sides = (lambda g, c=c: qkv_side_pe(pe, c - 1, g)) if c else None
                pe_unit(pe, c, c, h_hi, h_lo, sides, 0 if c == 0 else None)
            for g in range(3):
                qkv_side_pe(pe, 11, g)

        def qkv_side_act(act, c):
            if c < 10:
                for g in range(3):
                    s = 3 * c + g
                    act.wait_ge(qk_sum, s + 1)
                    if c:
                        act.wait_ge(qk_normed, s - 2)
                    nc.scalar.activation(rstd[:, g, :], ps[:, side_bank(s), 0:TG], ACT.Ln,
                                         scale=1.0 / HD, bias=eps[:, 0:1]).then_inc(qk_ln, 1)
                    act.wait_ge(qk_ln, s + 1)
                    nc.scalar.activation(rstd[:, g, :], rstd[:, g, :], ACT.Exp, scale=-0.5
                                         ).then_inc(qk_rstd, 1)

        def qkv_act(act):
            for c in range(12):
                split_hi_static(act, c + AHEAD)
                if c:
                    qkv_side_act(act, c - 1)
                act.wait_ge(out_ready, c + 1)
                src = ps[:, out_banks(c):out_banks(c) + 3, 0:TG]
                if c < 10:
                    if c == 0:
                        act.wait_ge(norm_lo, KC)
                    if c == 8:
                        act.wait_ge(x_saved, 16)
                    nc.scalar.activation(grp(sq[c % 2][:, :]), src, ACT.Square)
                    nc.scalar.activation(grp(qk_dst(c)), src, ACT.Copy).then_inc(free_act, 1)
                else:
                    if c == 10:
                        act.wait_ge(line_out, 16 * QH)
                    nc.scalar.activation(grp(vT[c - 10][:, :]), src, ACT.Copy).then_inc(free_act, 1)

        def qkv_side_dve(dve, c):
            for g in range(3):
                s = 3 * c + g
                if c < 10:
                    dve.wait_ge(qk_rstd, s + 1)
                    if g == 0:
                        dve.wait_ge(free_act, c + 1)
                    d = qk_dst(c)[:, g * TG:g * TG + TG]
                    nc.vector.scalar_tensor_tensor(out=d, in0=d, scalar=qk_gain[:, c // 8:c // 8 + 1],
                                                   in1=rstd[:, g, :], op0=ALU.mult, op1=ALU.mult
                                                   ).then_inc(qk_normed, 1)
                else:
                    dve.wait_ge(vt_ready, s - 29)
                    n, tiles = (P, 4) if g < 2 else (LAST, 1)
                    nc.vector.tensor_copy(
                        v_tok[0:n, 4 * g:4 * g + tiles, (c - 10) * P:(c - 9) * P],
                        ps[0:n, side_bank(s), :].rearrange("p (t n) -> p t n", t=4)[:, 0:tiles, :]
                    ).then_inc(v_taken, 1)

        def qkv_dve(dve):
            for c in range(12):
                split_lo_static(dve, c + AHEAD)
                if c:
                    qkv_side_dve(dve, c - 1)
            qkv_side_dve(dve, 11)

        cache_src = [(NBLK - 1, BLK), (NBLK, SAMPLE)]

        def caches_pe(pe):
            pe.wait_ge(qk_normed, 30)
            pe.wait_ge(v_taken, 6)
            for j, (t, n) in enumerate(cache_src):
                for gp in range(2):
                    last = nc.tensor.transpose(ps[0:n, j, gp * P:gp * P + P], kn[:, gp, t * P:t * P + n], ident)
                last.then_inc(cache_t, 1)

        def caches_dve(dve):
            for j, (t, n) in enumerate(cache_src):
                dve.wait_ge(cache_t, j + 1)
                nc.vector.tensor_copy(tokout[j][0:n, :], ps[0:n, j, 0:256]).then_inc(cache_c, 1)

        def caches_pool(pool):
            for i in range(2):
                src = a["cache_k" if i == 0 else "cache_v"][0]
                pool.dma_start(out[4 + i][0][:, 0:WIN - NS, :, :], src[:, NS:WIN, :, :]).then_inc(stored, 16)
            pool.wait_ge(v_taken, 6)
            pool.dma_start(out[3][0, 0].rearrange("s h d -> s (h d)"), v_tok[:, NBLK - 1, :]).then_inc(stored, 16)
            for b in range(NB):
                pool.dma_start(out[5][0, b, WIN - NS:WIN].rearrange("s h d -> s (h d)"),
                               v_tok[NS * b:NS * b + NS, NBLK, :]).then_inc(stored, 16)
            pool.wait_ge(cache_c, 2)
            pool.dma_start(out[2][0, 0].rearrange("s h d -> s (h d)"), tokout[0][:, :]).then_inc(stored, 16)
            for b in range(NB):
                pool.dma_start(out[4][0, b, WIN - NS:WIN].rearrange("s h d -> s (h d)"),
                               tokout[1][NS * b:NS * b + NS, :]).then_inc(stored, 16)

        rel_ext = at("rel_ext", R4 + 2 * BUF, [BUCKETS + 1, QH])
        bucket = at("bucket", R4 + 2 * BUF + 64, [BUCKETS + 1, LINE])
        line = at("line", R4 + 3 * BUF, [QH, LINE])
        s_bias = at("s_bias", R1, [P, WIN + NS])
        line_in, line_mm, line_c = sem("line_in"), sem("line_mm"), sem("line_c")
        bias_in, sbias_in = sem("bias_in"), sem("sbias_in")
        rel_one = sem("rel_one")

        def bias_pool(pool):
            pool.dma_start(bucket[:, :], a["buckets"]).then_inc(line_in, 16)
            pool.dma_start(rel_ext[0:BUCKETS, :], a["rel_table"]).then_inc(line_in, 16)
            pool.wait_ge(line_c, 1)
            for h in range(QH):
                pool.dma_start(scratch["line"][h:h + 1, :, :],
                               bass.AP(line[h:h + 1, :].tensor, line[h:h + 1, :].offset,
                                       [list(line[h:h + 1, :].ap[0]), [0, BLK], [1, LINE]])
                               ).then_inc(line_out, 16)

        def line_src(base, dims):
            return bass.AP(scratch["line"].tensor, base, dims)

        def bias_read(pool):
            pool.wait_ge(line_out, 16 * QH)
            pool.wait_ge(x_saved, 16)
            pool.wait_ge(norm_h, KC)
            for s in range(4):
                gp, ip = divmod(s, 2)
                for par in range(2):
                    pool.dma_start(bias[:, 4 * s + 2 * par:4 * s + 2 * par + 2, :],
                                   line_src((8 * gp + 4 * par + 2 * ip) * BLK * LINE + BLK - 1,
                                            [[LINE - 1, P], [BLK * LINE, 2], [1, 2 * BLK]])
                                   ).then_inc(bias_in, 16)

        NG = 4 * TILES
        P_BUFS = 3
        prob = [at(f"prob{i}", R4 + i * 4096, [P, 4, 2 * BLK]) for i in range(P_BUFS)]
        probT = at("probT", R4 + 3 * 4096, [P, 4, 2, BLK])
        at_s = at_c + 320 + 2048
        stat = at("stat", at_s, [P, P_BUFS, 5, 4])
        esink = at("esink", at_s + P_BUFS * 80 + 16, [P, P_BUFS, 4])
        o_hi = at("o_hi", R3, [P, KC, TP], F32R)
        o_lo = at("o_lo", R2, [P, KC, TP], F32R)
        s_done, s_taken, max_done = sem("s_done"), sem("s_taken"), sem("max_done")
        negm_done, logit_done, exp_done = sem("negm_done"), sem("logit_done"), sem("exp_done")
        den_done, rden_done, prob_ready = sem("den_done"), sem("rden_done"), sem("prob_ready")
        t_done, pT_ready, pv_done = sem("t_done"), sem("pT_ready"), sem("pv_done")
        o_hi_done, o_taken, vmeta_done = sem("o_hi_done"), sem("o_taken"), sem("vmeta_done")

        def block_of(n):
            b, step = divmod(n, 4)
            if b == 0:
                return (COL_M, META), (0, None, 0), BLK, BLK + META, step
            col = BLK * (b - 1)
            if b == 1:
                return (col, BLK), (COL_M, None, META), BLK - META, 2 * BLK, step
            return (col, BLK), (col - BLK, b - 2, BLK), 0, 2 * BLK, step

        def att_scores_pe(pe, n):
            (qc, nq), (pc, _, npk), k0, k1, step = block_of(n)
            gp, ip = divmod(step, 2)
            if n >= 2:
                pe.wait_ge(s_taken, n - 1)
            for par in range(2):
                rows = slice(HD * par, HD * par + HD)
                bank = 2 * (n % 2) + par
                for i in range(2):
                    lhsT = q[rows, 4 * gp + 2 * ip + i, qc:qc + nq]
                    o = ps[0:nq, bank, 2 * BLK * i:2 * BLK * i + 2 * BLK]
                    if npk == BLK:
                        last = nc.tensor.matmul(o, lhsT, kn[rows, gp, pc:pc + 2 * BLK], start=True, stop=True)
                    else:
                        if npk:
                            nc.tensor.matmul(o[:, k0:BLK], lhsT, kn[rows, gp, pc:pc + npk],
                                             start=True, stop=True)
                        last = nc.tensor.matmul(o[:, BLK:k1], lhsT, kn[rows, gp, qc:qc + nq],
                                                start=True, stop=True)
            last.then_inc(s_done, 1)

        def att_transpose_pe(pe, n):
            (qc, nq), (pc, _, npk), k0, k1, step = block_of(n)
            pe.wait_ge(prob_ready, n + 1)
            if n >= 1:
                pe.wait_ge(pT_ready, n)
            for k in range(4):
                bank = 4 + k // 2
                for part, (c0, nk) in enumerate(((k0, npk), (BLK, nq))):
                    if nk:
                        o = ps[0:nk, bank, (k % 2) * 2 * BLK + part * BLK:][:, 0:nq]
                        last = nc.tensor.transpose(o, prob[n % P_BUFS][0:nq, k, c0:c0 + nk],
                                                   ident[0:nq, 0:nq])
            last.then_inc(t_done, 1)

        def att_values_pe(pe, n):
            (qc, nq), (pc, pt, npk), k0, k1, step = block_of(n)
            b = n // 4
            gp, ip = divmod(step, 2)
            pe.wait_ge(pT_ready, n + 1)
            if n >= 2:
                pe.wait_ge(o_taken, n - 1)
            for par in range(2):
                cols = slice((2 * gp + par) * HD, (2 * gp + par) * HD + HD)
                for i in range(2):
                    k = 2 * par + i
                    o = ps[HD * par:HD * par + HD, 6 + n % 2, BLK * i:BLK * i + nq]
                    if npk:
                        v = v_tok[:, pt, cols] if pt is not None else v_meta[:, cols]
                        nc.tensor.matmul(o, v, probT[0:npk, k, 0, 0:nq], start=True, stop=False)
                    v = v_tok[:, b - 1, cols] if b else v_meta[:, cols]
                    last = nc.tensor.matmul(o, v, probT[0:nq, k, 1, 0:nq], start=npk == 0, stop=True)
            last.then_inc(pv_done, 1)

        def att_pe(pe):
            pe.wait_ge(cache_c, 2)
            pe.wait_ge(vmeta_done, 1)
            for n in range(NG + 2):
                if n >= 2:
                    att_transpose_pe(pe, n - 2)
                if n < NG:
                    att_scores_pe(pe, n)
                if n >= 2:
                    att_values_pe(pe, n - 2)

        def att_softmax_dve(dve, n):
            (qc, nq), (pc, _, npk), k0, k1, step = block_of(n)
            b3 = n % P_BUFS
            st = stat[0:nq, b3, :, :]
            dve.wait_ge(s_done, n + 1)
            if n >= P_BUFS:
                dve.wait_ge(t_done, n - P_BUFS + 1)
            src = ps[0:nq, 2 * (n % 2):2 * (n % 2) + 2, :].rearrange("p b (i s) -> p (b i) s", i=2)
            pr = prob[b3][0:nq, :, k0:k1]
            nc.vector.scalar_tensor_tensor(out=pr, in0=src[:, :, k0:k1], scalar=HD ** -0.5,
                                           in1=bias[0:nq, 4 * step:4 * step + 4, k0:k1],
                                           op0=ALU.mult, op1=ALU.add).then_inc(s_taken, 1)
            dve.wait_ge(s_taken, n + 1)
            nc.vector.tensor_reduce(st[:, 0, :], pr, AX, ALU.max).then_inc(max_done, 1)
            dve.wait_ge(max_done, n + 1)
            nc.vector.scalar_tensor_tensor(out=st[:, 1, :], in0=st[:, 0, :], scalar=-1.0,
                                           in1=nsinks[0:nq, 4 * step:4 * step + 4],
                                           op0=ALU.mult, op1=ALU.min).then_inc(negm_done, 1)
            dve.wait_ge(negm_done, n + 1)
            nc.vector.tensor_tensor(st[:, 2, :], sinks[0:nq, 4 * step:4 * step + 4], st[:, 1, :], ALU.add
                                    ).then_inc(logit_done, 1)

        def att_exp_act(act, n):
            (qc, nq), (pc, _, npk), k0, k1, step = block_of(n)
            b3 = n % P_BUFS
            st = stat[0:nq, b3, :, :]
            act.wait_ge(logit_done, n + 1)
            for k in range(4):
                pr = prob[b3][0:nq, k, k0:k1]
                nc.scalar.activation(pr, pr, ACT.Exp, bias=st[:, 1, k:k + 1], accum_out=st[:, 3, k:k + 1])
            nc.scalar.activation(esink[0:nq, b3, :], st[:, 2, :], ACT.Exp).then_inc(exp_done, 1)

        def att_den_dve(dve, n):
            nq = block_of(n)[0][1]
            b3 = n % P_BUFS
            st = stat[0:nq, b3, :, :]
            dve.wait_ge(exp_done, n + 1)
            nc.vector.tensor_tensor(st[:, 3, :], st[:, 3, :], esink[0:nq, b3, :], ALU.add).then_inc(den_done, 1)
            dve.wait_ge(den_done, n + 1)
            nc.vector.reciprocal(st[:, 4, :], st[:, 3, :]).then_inc(rden_done, 1)

        def att_scale_pool(pool, n):
            (qc, nq), (pc, _, npk), k0, k1, step = block_of(n)
            b3 = n % P_BUFS
            pool.wait_ge(rden_done, n + 1)
            pr = prob[b3][0:nq, :, k0:k1]
            nc.gpsimd.tensor_tensor(pr, pr, stat[0:nq, b3, 4, :].unsqueeze(2).to_broadcast([nq, 4, k1 - k0]),
                                    ALU.mult).then_inc(prob_ready, 1)

        def att_pT_act(act, n):
            (qc, nq), (pc, _, npk), k0, k1, step = block_of(n)
            act.wait_ge(t_done, n + 1)
            if n >= 1:
                act.wait_ge(pv_done, n)
            src = ps[:, 4:6, :].rearrange("p b (i c s) -> p (b i) c s", i=2, c=2)
            if npk == BLK:
                nc.scalar.activation(probT[:, :, :, :], src, ACT.Copy).then_inc(pT_ready, 1)
            else:
                if npk:
                    nc.scalar.activation(probT[0:npk, :, 0, 0:nq], src[0:npk, :, 0, 0:nq], ACT.Copy)
                nc.scalar.activation(probT[0:nq, :, 1, 0:nq], src[0:nq, :, 1, 0:nq], ACT.Copy
                                     ).then_inc(pT_ready, 1)

        def o_views(n):
            (qc, nq), _, _, _, step = block_of(n)
            gp, ip = divmod(step, 2)
            c = 4 * gp + 2 * ip
            src = ps[:, 6 + n % 2, 0:2 * BLK].rearrange("p (i s) -> p i s", i=2)[:, :, 0:nq]
            return src, o_hi[:, c:c + 2, qc:qc + nq], o_lo[:, c:c + 2, qc:qc + nq]

        def att_o_act(act, n):
            src, hi, lo = o_views(n)
            act.wait_ge(pv_done, n + 1)
            nc.scalar.activation(hi, src, ACT.Copy).then_inc(o_hi_done, 1)

        def att_o_dve(dve, n):
            src, hi, lo = o_views(n)
            dve.wait_ge(o_hi_done, n + 1)
            nc.vector.tensor_tensor(lo, src, hi.bitcast(F32), ALU.subtract).then_inc(o_taken, 1)

        def att_act(act):
            for n in range(NG + 2):
                if n >= 2:
                    att_pT_act(act, n - 2)
                if n < NG:
                    att_exp_act(act, n)
                if n >= 2:
                    att_o_act(act, n - 2)

        def att_dve(dve):
            dve.wait_ge(v_taken, 6)
            nc.vector.tensor_copy(v_meta[:, :], v_tok[SAMPLE:LAST, NBLK, :]).then_inc(vmeta_done, 1)
            dve.wait_ge(bias_in, 16 * 8)
            for n in range(NG + 3):
                if 1 <= n <= NG:
                    att_den_dve(dve, n - 1)
                if n < NG:
                    att_softmax_dve(dve, n)
                if n >= 3:
                    att_o_dve(dve, n - 3)

        SK = WIN + SAMPLE
        k_raw = at("k_raw", R1 + 544, [P, NB, KH * HD])
        kcT = at("kcT", R1 + 544 + 8192, [P, 2, NB, WIN])
        v_c = at("v_c", R1 + 544 + 16384, [P, NB, KH * HD])
        q_big = at("q_big", R1 + 544 + 24576, [P, 2, NB, 2 * P // NS])
        sb_new = at("sb_new", R4, [P, 4, SK])
        s_prob = at("s_prob", R4 + 2560, [P, 4, SK])
        pcT = at("pcT", R4 + 5120, [P, 4, P])
        pnT = at("pnT", R4 + 5120 + 2048, [SAMPLE, 4, P])
        s_sink = at("s_sink", R4 + 5120 + 4096, [P, 2])
        s_stat = at("s_stat", R4 + 5120 + 4096 + 32, [P, 6, 4])
        kc_in, sq_steps, sa_steps, sp_steps = sem("kc_in"), sem("sample_dve"), sem("sample_act"), sem("sample_pe")

        def sample_loads(pool):
            pool.wait_ge(out_ready, 12)
            pool.dma_start(k_raw[:, :, :], a["cache_k"][0].rearrange("b s h d -> s b (h d)")).then_inc(kc_in, 16)
            pool.dma_start(v_c[:, :, :], a["cache_v"][0].rearrange("b s h d -> s b (h d)")).then_inc(kc_in, 16)
            pool.wait_ge(line_out, 16 * QH)
            for half in range(2):
                pool.dma_start(s_bias[64 * half:64 * half + 64, :],
                               line_src(BLK - 1, [[BLK * LINE, QH], [LINE - 1, NS], [1, WIN + NS]])
                               ).then_inc(kc_in, 16)

        def sink_rows(pool):
            pool.wait_ge(prob_ready, NG)
            pool.wait_ge(t_done, NG)
            for half in range(2):
                pool.dma_start(s_sink[64 * half:64 * half + 64, 0:1],
                               bass.AP(a["attn_sinks"].tensor, 0, [[1, QH], [0, NS], [1, 1]]),
                               allow_slow_non_contiguous=True).then_inc(sbias_in, 16)

        def sample_dve(dve):
            step = [0]

            def inc(ins):
                step[0] += 1
                ins.then_inc(sq_steps, 1)
                return step[0]

            def after(k):
                dve.wait_ge(sq_steps, k)

            dve.wait_ge(out_ready, 12)
            z = inc(nc.vector.memset(q_big[:, :, :, :], 0.0))
            after(z)
            for gp in range(2):
                for par in range(2):
                    g = 2 * gp + par
                    rows = slice(HD * par, HD * par + HD)
                    dst = q_big[rows, gp, :, 16 * g:16 * g + 16].rearrange("p b (c i) -> p b c i", i=NS)
                    src = q[rows, 4 * gp:4 * gp + 4, COL_S:COL_M].rearrange("p c (b i) -> p b c i", i=NS)
                    inc(nc.vector.tensor_copy(dst, src))
            assert step[0] == 5

        def sample_dve2(dve):
            step = [5]

            def inc(ins):
                step[0] += 1
                ins.then_inc(sq_steps, 1)
                return step[0]

            def after(k):
                dve.wait_ge(sq_steps, k)

            for j in range(4):
                dve.wait_ge(sp_steps, j + 1)
                dst = kcT[:, j // 2, 4 * (j % 2):4 * (j % 2) + 4, :]
                inc(nc.vector.tensor_copy(dst, ps[:, j, :].rearrange("p (b s) -> p b s", b=4)))
            dve.wait_ge(kc_in, 64)
            dve.wait_ge(t_done, NG)
            m = inc(nc.vector.memset(sb_new[:, :, WIN:SK], NEG))
            inc(nc.vector.tensor_copy(sb_new[:, :, 0:WIN],
                                      s_bias[:, 0:WIN].unsqueeze(1).to_broadcast([P, 4, WIN])))
            after(m)
            for b in range(NB):
                rows = slice(64 * (b % 2), 64 * (b % 2) + 64)
                inc(nc.vector.tensor_copy(sb_new[rows, b // 2, WIN + NS * b:WIN + NS * b + NS],
                                          s_bias[rows, WIN:WIN + NS]))
            after(step[0])
            dve.wait_ge(sp_steps, 5)
            sc = ps[:, 4:6, :].rearrange("p b (i s) -> p (b i) s", i=2)[:, :, 0:SK]
            k = inc(nc.vector.scalar_tensor_tensor(out=s_prob[:, :, :], in0=sc, scalar=HD ** -0.5,
                                                   in1=sb_new[:, :, :], op0=ALU.mult, op1=ALU.add))
            after(k)
            k = inc(nc.vector.tensor_reduce(s_stat[:, 0, :], s_prob[:, :, :], AX, ALU.max))
            after(k)
            dve.wait_ge(sbias_in, 32)
            sink4 = s_sink[:, 0:1].to_broadcast([P, 4])
            k = inc(nc.vector.tensor_tensor(s_stat[:, 0, :], s_stat[:, 0, :], sink4, ALU.max))
            after(k)
            k = inc(nc.vector.tensor_scalar(s_stat[:, 1, :], s_stat[:, 0, :], -1.0, None, ALU.mult))
            after(k)
            k = inc(nc.vector.tensor_tensor(s_stat[:, 2, :], s_stat[:, 1, :], sink4, ALU.add))
            assert k == 24, k
            dve.wait_ge(sa_steps, 1)
            k = inc(nc.vector.tensor_tensor(s_stat[:, 3, :], s_stat[:, 3, :], s_stat[:, 4, :], ALU.add))
            after(k)
            k = inc(nc.vector.reciprocal(s_stat[:, 5, :], s_stat[:, 3, :]))
            after(k)
            k = inc(nc.vector.tensor_tensor(s_prob[:, :, :], s_prob[:, :, :],
                                            s_stat[:, 5, :].unsqueeze(2).to_broadcast([P, 4, SK]), ALU.mult))
            assert k == 27, k
            dve.wait_ge(sp_steps, 6)
            k = inc(nc.vector.tensor_copy(pnT[:, :, :], ps[0:SAMPLE, 7, :].rearrange("p (t r) -> p t r", t=4)))
            assert k == 28
            dve.wait_ge(sa_steps, 3)
            for gp in range(2):
                src, hi, lo = sample_o(gp)
                inc(nc.vector.tensor_tensor(lo, src, hi.bitcast(F32), ALU.subtract))
            assert step[0] == 30

        def sample_o(gp):
            src = ps[:, 0, P * gp:P * gp + P].rearrange("p (b c i) -> p b c i", b=NB, i=NS)
            hi, lo = (o[:, 4 * gp:4 * gp + 4, COL_S:COL_M].rearrange("p c (b i) -> p b c i", i=NS)
                      for o in (o_hi, o_lo))
            return src, hi, lo

        def sample_act(act):
            act.wait_ge(sq_steps, 24)
            for t in range(4):
                nc.scalar.activation(s_prob[:, t, :], s_prob[:, t, :], ACT.Exp, bias=s_stat[:, 1, t:t + 1],
                                     accum_out=s_stat[:, 3, t:t + 1])
            nc.scalar.activation(s_stat[:, 4, :], s_stat[:, 2, :], ACT.Exp).then_inc(sa_steps, 1)
            act.wait_ge(sp_steps, 6)
            nc.scalar.activation(pcT[:, :, :], ps[:, 6, :].rearrange("p (t r) -> p t r", t=4), ACT.Copy
                                 ).then_inc(sa_steps, 1)
            act.wait_ge(sp_steps, 7)
            for gp in range(2):
                src, hi, lo = sample_o(gp)
                last = nc.scalar.activation(hi, src, ACT.Copy)
            last.then_inc(sa_steps, 1)

        def sample_pe(pe):
            pe.wait_ge(kc_in, 64)
            pe.wait_ge(o_taken, NG)
            for j in range(4):
                for i in range(4):
                    b = 4 * (j % 2) + i
                    last = nc.tensor.transpose(ps[:, j, P * i:P * i + P],
                                               k_raw[:, b, P * (j // 2):P * (j // 2) + P], ident)
                last.then_inc(sp_steps, 1)
            pe.wait_ge(sq_steps, 9)
            for b in range(NB):
                o = ps[64 * (b % 2):64 * (b % 2) + 64, 4 + b // 4, 256 * (b // 2 % 2):256 * (b // 2 % 2) + SK]
                for c, ncol, keys in ((0, WIN, lambda gp: kcT[:, gp, b, :]),
                                      (WIN, SAMPLE, lambda gp: kn[:, gp, COL_S:COL_M])):
                    for gp in range(2):
                        last = nc.tensor.matmul(o[:, c:c + ncol], q_big[:, gp, b, :], keys(gp),
                                                start=gp == 0, stop=gp == 1)
            last.then_inc(sp_steps, 1)
            pe.wait_ge(sq_steps, 27)
            for t in range(4):
                nc.tensor.transpose(ps[:, 6, P * t:P * t + P], s_prob[:, t, 0:WIN], ident)
                last = nc.tensor.transpose(ps[0:SAMPLE, 7, P * t:P * t + P], s_prob[:, t, WIN:SK], ident)
            last.then_inc(sp_steps, 1)
            pe.wait_ge(sq_steps, 28)
            pe.wait_ge(sa_steps, 2)
            for g in range(KH):
                gp, par = divmod(g, 2)
                for b in range(NB):
                    r = 64 * (b % 2) + 16 * g
                    o = ps[HD * par:HD * par + HD, 0, P * gp + 16 * b:P * gp + 16 * b + 16]
                    cols = slice(HD * g, HD * g + HD)
                    nc.tensor.matmul(o, v_c[:, b, cols], pcT[:, b // 2, r:r + 16], start=True, stop=False)
                    last = nc.tensor.matmul(o, v_tok[0:SAMPLE, NBLK, cols], pnT[:, b // 2, r:r + 16],
                                            start=False, stop=True)
            last.then_inc(sp_steps, 1)

        def add_x_dve(dve, n, f, x=x):
            dve.wait_ge(out_ready, n + 1)
            nc.vector.tensor_tensor(grp(x[:, f, :]), grp(x[:, f, :]), ps[:, out_banks(n):out_banks(n) + 3, 0:TG],
                                    ALU.add).then_inc(free_dve, 1)

        def reload_x(pool, which, count):
            for f in range(KC):
                pool.dma_start(x[:, f, :], scratch[which][:, f, :]).then_inc(x_back, 16)

        def wo_pe(pe):
            pe.wait_ge(sq_steps, 30)
            for c in range(KC):
                pe_unit(pe, U_WO + c, N_WO + c, o_hi, o_lo)

        def wo_act(act):
            for c in range(KC):
                split_hi_static(act, U_WO + c + AHEAD)

        def wo_dve(dve):
            for c in range(KC):
                split_lo_static(dve, U_WO + c + AHEAD)
                if c == 0:
                    dve.wait_ge(x_back, 16 * KC)
                add_x_dve(dve, N_WO + c, c)

        def mlp_slice_sp(sp, layer, u0, i):
            r0 = u0 // 2
            up = a["mlp_w_up"][layer].rearrange("(k p) n -> p k n", p=P)
            down = a["mlp_w_down"][layer].rearrange("(s p) n -> p s n", p=P)
            for j in range(4):
                slot = (r0 + j) % 2
                sp.wait_ge(w_lo_ready, i * 8 + (2 * (r0 + j) - 2))
                if j < 2:
                    src = up[:, :, bass.ds(i * 512 + 256 * j, 256)]
                    sp.dma_start(raw_k8[:, slot, :, :], src).then_inc(raw_in[slot], 16)
                else:
                    src = down[:, bass.ds(i * 4, 4), 512 * (j - 2):512 * (j - 2) + 512]
                    sp.dma_start(raw_k4[:, slot, :, :], src).then_inc(raw_in[slot], 16)

        def local_outs(j):
            return j + 1 if j < 4 else 2 * j - 2

        def mlp_raw_wait(u0, i, j):
            r = u0 // 2 + j // 2
            base = raw_target(u0 // 2 + (j // 2) % 2 - 2)
            return r % 2, i * 32 + (base + 16 * (j // 4 + 1))

        def mlp_split_hi(act, u0, n0, i, j):
            jj = j + AHEAD
            rslot, rwait = mlp_raw_wait(u0, i, jj)
            done = (n0 - 1, n0)[j] if j < 2 else n0 + local_outs(j - 2)
            split_hi(act, (u0 + jj) % 4, rslot, jj % 2, 4 <= jj < 8, rwait, i * 12 + done)

        def mlp_split_lo(dve, u0, i, j):
            jj = j + AHEAD
            split_lo(dve, (u0 + jj) % 4, (u0 // 2 + jj // 2) % 2, jj % 2, 4 <= jj < 8, i * 8 + (u0 + jj + 1))

        def mlp_slice_act(act, layer, u0, n0, i, prefetch=8):
            for j in range(8):
                if j < prefetch:
                    mlp_split_hi(act, u0, n0, i, j)
                if j < 4:
                    m = 4 * SLICES * layer
                    act.wait_ge(out_ready, i * 12 + (n0 + j + 1))
                    if layer or j >= 2:
                        act.wait_ge(act_split, i * 4 + (m + j - 1))
                    src = ps[:, out_banks(n0 + j):out_banks(n0 + j) + 3, 0:TG]
                    nc.scalar.activation(grp(relu[j % 2][:, :]), src, ACT.Relu).then_inc(free_act, 1)
                    act.wait_ge(free_act, i * 4 + (FA_MLP[n0] + j + 1))
                    nc.scalar.activation(act_hi[:, j, :], relu[j % 2][:, :], ACT.Square).then_inc(up_done, 1)

        def mlp_slice_dve(dve, layer, u0, n0, i, prefetch=8, x=x):
            for j in range(8):
                if j < prefetch:
                    mlp_split_lo(dve, u0, i, j)
                if j < 4:
                    m = 4 * SLICES * layer
                    dve.wait_ge(up_done, i * 4 + (m + j + 1))
                    dve.wait_ge(act_split, i * 4 + (m + j))
                    nc.vector.tensor_tensor(relu_sq[:, :], relu[j % 2][:, :], relu[j % 2][:, :], ALU.mult
                                            ).then_inc(sq_done, 1)
                    dve.wait_ge(sq_done, i * 4 + (m + j + 1))
                    nc.vector.tensor_tensor(act_lo[:, j, :], relu_sq[:, :], act_hi[:, j, :].bitcast(F32),
                                            ALU.subtract).then_inc(act_split, 1)
                else:
                    for c in range(2):
                        o = 2 * (j - 4) + c
                        n = n0 + 4 + o
                        dve.wait_ge(out_ready, i * 12 + (n + 1))
                        dve.wait_ge(free_dve, i * 8 + (FD_MLP[n0] + o - 7))
                        nc.vector.tensor_tensor(grp(x[:, o, :]), grp(x[:, o, :]),
                                                ps[:, out_banks(n):out_banks(n) + 3, 0:TG], ALU.add
                                                ).then_inc(free_dve, 1)

        def mlp_slice_pe(pe, layer, u0, n0, i, h_lo=h_lo):
            m = 4 * SLICES * layer
            for j in range(8):
                pe.wait_ge(w_lo_ready, i * 8 + (u0 + j + 1))
                for c in range(1 if j < 4 else 2):
                    o = j if j < 4 else 4 + 2 * (j - 4) + c
                    if o < 2:
                        pe.wait_ge(free_dve, i * 8 + (FD_MLP[n0] - 1 + o))
                    elif o < 6:
                        pe.wait_ge(free_act, i * 4 + (FA_MLP[n0] + o - 1))
                    else:
                        pe.wait_ge(free_dve, i * 8 + (FD_MLP[n0] + o - 5))
                    deep, hi, lo = (8, h_hi, h_lo) if j < 4 else (4, act_hi, act_lo)
                    for k in range(deep):
                        if o == 4:
                            pe.wait_ge(act_split, i * 4 + (m + k + 1))
                        last = chunk_mms((u0 + j) % 4, k, deep, slice(P * c, P * c + P), out_banks(n0 + o),
                                         hi, lo, k, k == 0, k == deep - 1)
                    last.then_inc(out_ready, 1)

        ROWB = 4320
        t_i, t_f, b_row, jump, m_rel, m_abs, m_prev, keep = (
            at(nm, R0 + i * ROWB, [MH, TP]) for i, nm in enumerate(
                ["t_i", "t_f", "b_row", "jump", "m_rel", "m_abs", "m_prev", "keep"]))
        u_s = at("u_s", R0 + 8 * ROWB, [MH, SAMPLE])
        m0 = at("m0", R0 + 8 * ROWB + 128, [MH, NB])
        wg_raw = at("wg_raw", R3, [P, KC, 100])
        wg_hi = at("wg_hi", R3 + 3200, [P, KC, 100], F32R)
        wg_lo = at("wg_lo", R3 + 6400, [P, KC, 100], F32R)
        rows_u = at("rows_u", R4, [P, TP])
        rows_m = at("rows_m", R4 + BUF, [P, TP])
        stage = [at(f"stage{i}", R4 + (2 + i) * BUF, [P, TP]) for i in range(2)]
        selw = at("selw", R4 + 2 * BUF, [P, 8 * P + MH])
        v_m = at("v_m", R4 + 3 * BUF, [META, MH, VH])
        qk = at("qk", R3, [P, KC, TP])
        v = at("v", R0, [P, TILES, MH, VH])
        c0 = at("c0", R0, [P, NB, MH, VH])
        og = at("og", R1, [P, KC, TP])
        y_hi = at("y_hi", R3, [P, KC, TP], F32R)
        y_lo = at("y_lo", R1, [P, KC, TP], F32R)
        x2 = at("x2", R2, [P, KC, TP])
        h_lo2 = at("h_lo2", R0, [P, KC, TP], F32R)
        names = ["rr", "decay", "sw", "kts", "qs", "e_sb", "dd", "zr"]
        rr, decay, sw, kts, qs, e_sb, dd, zr = (at(nm, R2 + 2048 * i, [P, MH, P]) for i, nm in enumerate(names))
        nsq = at("nsq", R2 + 16384, [P, MH, 2, P])
        numr = at("numr", R2 + 16384 + 4096, [P, MH, 2, P])
        cst_ = at("c_state", R2 + 16384 + 8192, [P, MH, VH])
        a_sb = at("a_sb", R2 + 16384 + 8192 + 4128, [P, MH])
        a_s = at("a_s", R2 + 16384 + 8192 + 4128 + 32, [P, MH, SAMPLE])
        at_g = at_s + P_BUFS * 80 + 16 + P_BUFS * 16 + 48
        at_g = (at_g + 31) // 32 * 32
        bgate = at("bgate", at_g, [P, 1])
        bg15 = at("bg15", at_g + 32, [P, 1])
        ogain = at("ogain", at_g + 64, [P, KC])
        causal = cst[:, slice(*CONST_AT["causal"])]
        own_causal = cst[:, slice(*CONST_AT["own_causal"])]
        small += [(bgate[0:MH, :], a["mlstm_b_gate"][:, 0:MH].rearrange("a h -> h a")),
                  (bgate[96:96 + MH, :], a["mlstm_b_gate"][:, MH:2 * MH].rearrange("a h -> h a")),
                  (ogain[:, :], a["mlstm_out_norm"][0].rearrange("(k p) -> p k", p=P))]

        wg_zero, wg_in, wg_split_hi, wg_split = sem("wg_zero"), sem("wg_in"), sem("wg_split_hi"), sem("wg_split")
        keep_in, gate_dve, gate_act = sem("keep_in"), sem("gate_dve"), sem("gate_act")
        vt2_ready, v2_taken, og_done, og_out, og_in = (sem(s) for s in
            ("vt2_ready", "v2_taken", "og_done", "og_out", "og_in"))
        v_ones, sel_in, vm_done = sem("v_ones"), sem("sel_in"), sem("vm_done")
        (rr_ready, kT_ready, st_ready, d_ready, decay_ready, sw_ready, kts_ready, bc_ready, qs_ready, e_ready,
         num_ready, dd_step, nsq_ready, ss_ready, z_ready, ln_z, r_ready, numr_ready, y_ready, yhi_ready, ylo_ready,
         cup_ready, c_new) = (sem(s) for s in (
             "rr_ready", "kT_ready", "st_ready", "d_ready", "decay_ready", "sw_ready", "kts_ready", "bc_ready",
             "qs_ready", "e_ready", "num_ready", "dd_step", "nsq_ready", "ss_ready", "z_ready", "ln_z", "r_ready",
             "numr_ready", "y_ready", "yhi_ready", "ylo_ready", "cup_ready", "c_new"))
        abs_ready = sem("abs_ready")
        c0_in, sm_pe, sm_dve, sm_act, c0_out = (sem(s) for s in ("c0_in", "sm_pe", "sm_dve", "sm_act", "c0_out"))
        x2_back = sem("x2_back")
        MLP0_ADDS = 8 + 8 * SLICES
        OUT_ADDS = MLP0_ADDS + 8

        def gates_pool(pool):
            pool.wait_ge(wg_zero, 1)
            w = a["mlstm_w_gate"][0].rearrange("(k p) n -> p k n", p=P)
            pool.dma_start(wg_raw[:, :, 0:MH], w[:, :, 0:MH]).then_inc(wg_in, 16)
            pool.dma_start(wg_raw[:, :, 96:96 + MH], w[:, :, MH:2 * MH]).then_inc(wg_in, 16)
            pool.wait_ge(free_dve, MLP0_ADDS)
            pool.dma_start(scratch["x1"], x[:, :, :]).then_inc(x_saved, 16)
            pool.wait_ge(x_saved, 32)
            pool.wait_ge(norm_h, 3 * KC)
            pool.dma_start(keep[:, :], a["keep"]).then_inc(keep_in, 16)
            pool.dma_start(m0[:, :], a["state_m"][0].rearrange("b h -> h b"),
                           allow_slow_non_contiguous=True).then_inc(keep_in, 16)

        def gates_pe(pe):
            n = N_IN
            pe.wait_ge(wg_split, 1)
            pe.wait_ge(*freed(n - 2))
            for k in range(KC):
                pe.wait_ge(norm_lo, 2 * KC + k + 1)
                for g in range(3):
                    o = ps[0:100, out_banks(n) + g, 0:TG]
                    c = slice(g * TG, g * TG + TG)
                    nc.tensor.matmul(o, wg_hi[:, k, :], h_hi[:, k, c], start=k == 0, stop=False)
                    nc.tensor.matmul(o, wg_hi[:, k, :], h_lo[:, k, c], start=False, stop=False)
                    last = nc.tensor.matmul(o, wg_lo[:, k, :], h_hi[:, k, c], start=False, stop=k == KC - 1)
            last.then_inc(out_ready, 1)

        def gates_act1(act):
            n = N_IN
            act.wait_ge(out_ready, n + 1)
            act.wait_ge(x_saved, 32)
            act.wait_ge(norm_lo, 3 * KC)
            act.wait_ge(gate_dve, 1)
            for dst, r in ((t_i, 0), (t_f, 96)):
                last = nc.scalar.activation(grp(dst[:, :]), ps[r:r + MH, out_banks(n):out_banks(n) + 3, 0:TG],
                                            ACT.Tanh, scale=1.0 / CAP, bias=bg15[r:r + MH, :])
            last.then_inc(free_act, 1)
            act.preload_act_table_set("natural_log_exp_and_others")
            act.wait_ge(free_act, freed(n)[1])
            nc.scalar.activation(t_f[:, :], t_f[:, :], ACT.Exp, scale=-CAP).then_inc(gate_act, 1)
            act.wait_ge(gate_act, 1)
            nc.scalar.activation(t_f[:, :], t_f[:, :], ACT.Ln, bias=1.0).then_inc(gate_act, 1)

        def gates_dve(dve):
            step = [1]

            def do(ins):
                step[0] += 1
                ins.then_inc(gate_dve, 1)
                dve.wait_ge(gate_dve, step[0])

            dve.wait_ge(norm_lo, 3 * KC)
            do(nc.vector.memset(rows_u[:, :], 0.0))
            do(nc.vector.memset(rows_m[:, :], 0.0))
            do(nc.vector.memset(rows_u[32:32 + MH, :], 1.0))
            do(nc.vector.memset(rows_m[0:MH, :], 1.0))
            dve.wait_ge(x_saved, 32)
            do(nc.vector.memset(jump[:, :], 0.0))
            do(nc.vector.memset(m_prev[:, COL_M:T], 0.0))
            dve.wait_ge(keep_in, 32)
            dve.wait_ge(gate_act, 2)
            do(nc.vector.tensor_tensor_scan(b_row[:, 0:T], keep[:, 0:T], t_f[:, 0:T], 0.0, ALU.mult, ALU.subtract))
            u = rows_u[0:MH, 0:T]
            do(nc.vector.scalar_tensor_tensor(out=u, in0=t_i[:, 0:T], scalar=CAP, in1=b_row[:, 0:T],
                                              op0=ALU.mult, op1=ALU.subtract))
            do(nc.vector.tensor_copy(jump[:, BLK:SEQ:BLK], b_row[:, BLK - 1:SEQ - 1:BLK]))
            do(nc.vector.tensor_copy(jump[:, 0:1], b_row[:, T - 1:T]))
            do(nc.vector.memset(jump[:, COL_S:COL_M:NS], NEG))
            do(nc.vector.tensor_copy(u_s[:, :], rows_u[0:MH, COL_S:COL_M]))
            do(nc.vector.tensor_tensor(u_s[:, 0:SAMPLE:NS], u_s[:, 0:SAMPLE:NS], m0[:, :], ALU.max))
            do(nc.vector.tensor_tensor_scan(m_rel[:, COL_M:T], jump[:, COL_M:T], rows_u[0:MH, COL_M:T], 0.0,
                                            ALU.add, ALU.max))
            do(nc.vector.tensor_tensor_scan(m_rel[:, 0:SEQ], jump[:, 0:SEQ], rows_u[0:MH, 0:SEQ],
                                            m_rel[:, T - 1:T], ALU.add, ALU.max))
            do(nc.vector.tensor_tensor_scan(m_rel[:, COL_S:COL_M], jump[:, COL_S:COL_M], u_s[:, :], 0.0,
                                            ALU.add, ALU.max))
            do(nc.vector.tensor_tensor(m_abs[:, 0:T], m_rel[:, 0:T], b_row[:, 0:T], ALU.add))
            do(nc.vector.tensor_copy(m_prev[:, 0:BLK], m_abs[:, T - 1:T].to_broadcast([MH, BLK])))
            do(nc.vector.tensor_copy(m_prev[:, BLK:SEQ].rearrange("p (c n) -> p c n", n=BLK),
                                     m_abs[:, BLK - 1:SEQ - 1:BLK].unsqueeze(2).to_broadcast([MH, NBLK - 1, BLK])))
            do(nc.vector.tensor_copy(m_prev[:, COL_S:COL_M].rearrange("p (b n) -> p b n", n=NS),
                                     m0[:, :].unsqueeze(2).to_broadcast([MH, NB, NS])))
            do(nc.vector.tensor_tensor(m_prev[:, 0:T], m_prev[:, 0:T], m_rel[:, 0:T], ALU.subtract))
            do(nc.vector.tensor_scalar(rows_m[32:32 + MH, 0:T], m_rel[:, 0:T], -1.0, None, ALU.mult))
            return step[0]
        GATE_STEPS = 23

        def gates_act2(act):
            act.wait_ge(gate_dve, GATE_STEPS)
            nc.scalar.activation(rows_m[64:64 + MH, 0:T], m_prev[:, 0:T], ACT.Exp)
            nc.scalar.activation(rows_m[96:96 + MH, 0:T], m_abs[:, 0:T], ACT.Exp, scale=-1.0).then_inc(gate_act, 1)

        def gates_out(pool):
            pool.wait_ge(gate_dve, GATE_STEPS)
            pool.dma_start(out[8][0].rearrange("b h -> h b"), m_abs[:, SEQ - 1:SEQ],
                           allow_slow_non_contiguous=True).then_inc(stored, 16)
            pool.dma_start(out[11][0].rearrange("b h -> h b"), m_abs[:, COL_S + NS - 1:COL_M:NS],
                           allow_slow_non_contiguous=True).then_inc(stored, 16)

        def in_side_pe(pe, vc, g):
            s = 3 * vc + g
            if s >= 2:
                pe.wait_ge(v2_taken, s - 1)
            if g == 0:
                pe.wait_ge(*freed(N_IN + 1 + 8 + vc))
            for t in range(4 * g, min(4 * g + 4, TILES)):
                n = x_rows(t)
                last = nc.tensor.transpose(ps[0:n, side_bank(s), (t % 4) * P:(t % 4) * P + P],
                                           stage[vc % 2][:, t * P:t * P + n], ident)
            last.then_inc(vt2_ready, 1)

        def in_pe(pe):
            for c in range(24):
                sides = (lambda g, c=c: in_side_pe(pe, c - 9, g)) if 9 <= c < 17 else None
                pe_unit(pe, U_IN + c, N_IN + 1 + c, h_hi, h_lo, sides)

        def in_side_dve(dve, vc):
            if vc == 0:
                dve.wait_ge(gate_act, 3)
                dve.wait_ge(stored, 16 * 22)
                nc.vector.memset(v[:, :, :, DV:VH], 1.0).then_inc(v_ones, 1)
            for g in range(3):
                dve.wait_ge(vt2_ready, 3 * vc + g + 1)
                n, tiles = (P, 4) if g < 2 else (LAST, 1)
                nc.vector.tensor_copy(
                    v[0:n, 4 * g:4 * g + tiles, vc // 2, P * (vc % 2):P * (vc % 2) + P],
                    ps[0:n, side_bank(3 * vc + g), :].rearrange("p (t n) -> p t n", t=4)[:, 0:tiles, :]
                ).then_inc(v2_taken, 1)

        def in_act(act):
            for c in range(24):
                n = N_IN + 1 + c
                split_hi_static(act, U_IN + c + AHEAD)
                if c == 1:
                    gates_act2(act)
                act.wait_ge(out_ready, n + 1)
                src = ps[:, out_banks(n):out_banks(n) + 3, 0:TG]
                if c < 8:
                    nc.scalar.activation(grp(qk[:, c, :]), src, ACT.Copy,
                                         scale=1.0 if c < MH else DK ** -0.5).then_inc(free_act, 1)
                elif c < 16:
                    vc = c - 8
                    if vc >= 2:
                        act.wait_ge(vt2_ready, 3 * (vc - 1))
                    nc.scalar.activation(grp(stage[vc % 2][:, :]), src, ACT.Copy).then_inc(free_act, 1)
                else:
                    oc = c - 16
                    if oc == 0:
                        act.wait_ge(vt2_ready, 24)
                    if oc >= 2:
                        act.wait_ge(og_out, 16 * (oc - 1))
                    nc.scalar.activation(grp(stage[oc % 2][:, :]), src, ACT.Sigmoid).then_inc(free_act, 1)

        def in_dve(dve):
            for c in range(24):
                split_lo_static(dve, U_IN + c + AHEAD)
                if c == 0:
                    got = gates_dve(dve)
                    assert got == GATE_STEPS, got
                if 9 <= c < 17:
                    in_side_dve(dve, c - 9)
                if c >= 16:
                    oc = c - 16
                    dve.wait_ge(*freed(N_IN + 1 + c))
                    nc.vector.tensor_scalar(stage[oc % 2][:, :], stage[oc % 2][:, :], ogain[:, oc:oc + 1], None,
                                            ALU.mult).then_inc(og_done, 1)

        def og_pool(pool):
            for oc in range(KC):
                pool.wait_ge(og_done, oc + 1)
                if oc:
                    pool.wait_ge(og_out, 16 * oc)
                pool.dma_start(scratch["og"][:, oc, :], stage[oc % 2][:, :]).then_inc(og_out, 16)
            pool.wait_ge(og_out, 16 * KC)
            pool.dma_start(selw[:, :], a["select"]).then_inc(sel_in, 16)
            pool.wait_ge(out_ready, N_OUT)
            for f in range(KC):
                pool.dma_start(og[:, f, :], scratch["og"][:, f, :]).then_inc(og_in, 16)

        def chunk_of(c):
            return (COL_M, META) if c == 0 else (BLK * (c - 1), BLK)

        def hview(bank, n, rows=P):
            return ps[0:rows, bank, 0:MH * n].rearrange("p (h n) -> p h n", h=MH)

        CB = (0, 1, 3, 4)

        def chunk_pe(pe, c):
            col, n = chunk_of(c)
            cs = slice(col, col + n)
            vals = (lambda h, k0, k1: v_m[:, h, k0:k1]) if c == 0 else (lambda h, k0, k1: v[:, c - 1, h, k0:k1])
            if c:
                pe.wait_ge(c_new, 4 * c)
            for h in range(MH):
                last = nc.tensor.transpose(ps[0:n, 0, P * h:P * h + P], qk[:, MH + h, cs], ident)
            last.then_inc(kT_ready, 1)
            for h in range(MH):
                last = nc.tensor.matmul(ps[0:n, 1, n * h:n * h + n], qk[:, MH + h, cs], qk[:, h, cs],
                                        start=True, stop=True)
            last.then_inc(st_ready, 1)
            if c:
                pe.wait_ge(z_ready, c)
            pe.wait_ge(rr_ready, c + 1)
            nc.tensor.matmul(ps[0:n, 2, 0:MH * n], ident[0:n, 0:n],
                             causal[0:n, 0:n].unsqueeze(1).to_broadcast([n, MH, n]), start=True, stop=False)
            for h in range(MH):
                last = nc.tensor.matmul(ps[0:n, 2, n * h:n * h + n], rows_u[0:64, cs], rr[0:64, h, 0:n],
                                        start=False, stop=h == MH - 1)
            last.then_inc(d_ready, 1)
            for w in range(2):
                for h in range(MH):
                    last = nc.tensor.matmul(ps[:, 3 + w, n * h:n * h + n], selw[:, P * (MH * w + h):][:, 0:P],
                                            rows_m[:, cs], start=True, stop=True)
            last.then_inc(bc_ready, 1)
            pe.wait_ge(sw_ready, c + 1)
            if c:
                pe.wait_ge(numr_ready, c)
                pe.wait_ge(dd_step, 2 * c)
                pe.wait_ge(qs_ready, c + 1)
            for h in range(MH):
                for half in range(2):
                    o = ps[:, 5 + h // 2, (2 * (h % 2) + half) * n:][:, 0:n]
                    nc.tensor.matmul(o, vals(h, P * half, P * half + P), sw[0:n, h, 0:n],
                                     start=True, stop=c == 0)
                    if c:
                        nc.tensor.matmul(o, cst_[:, h, P * half:P * half + P], qs[:, h, 0:n],
                                         start=False, stop=True)
            if n == BLK:
                nc.tensor.matmul(ps[:, 7, :], ones[0:n, :], sw[0:n, :, :].rearrange("p h n -> p (h n)"),
                                 start=True, stop=False)
                for h in range(MH):
                    last = nc.tensor.matmul(ps[:, 7, n * h:n * h + n], cst_[:, h, DV:VH].to_broadcast([P, P]),
                                            qs[:, h, :], start=False, stop=h == MH - 1)
            else:
                last = nc.tensor.matmul(ps[:, 7, 0:MH * n], ones[0:n, :], sw[0:n, :, 0:n], start=True, stop=True)
            last.then_inc(num_ready, 1)
            pe.wait_ge(kts_ready, c + 1)
            pe.wait_ge(qs_ready, c + 1)
            pe.wait_ge(e_ready, c + 1)
            for h in range(MH):
                nc.tensor.matmul(ps[:, CB[h], 0:VH], kts[0:n, h, :], vals(h, 0, VH), start=True, stop=True
                                 ).then_inc(cup_ready, 1)
            pe.wait_ge(nsq_ready, c + 1)
            for half in range(2):
                last = nc.tensor.matmul(ps[:, 2, 0:MH * n], ones, nsq[:, :, half, 0:n], start=half == 0,
                                        stop=half == 1)
            last.then_inc(ss_ready, 1)

        def num_banks(bank, n):
            return ps[:, bank, 0:4 * n].rearrange("p (h c n) -> p h c n", h=2, c=2)

        def rr_dve(dve, c):
            col, n = chunk_of(c)
            if c:
                dve.wait_ge(d_ready, c)
            nc.vector.tensor_tensor(rr[0:64, :, 0:n],
                                    rows_m[0:64, col:col + n].unsqueeze(1).to_broadcast([64, MH, n]),
                                    selw[0:64, 8 * P:8 * P + MH].unsqueeze(2).to_broadcast([64, MH, n]),
                                    ALU.mult).then_inc(rr_ready, 1)

        def chunk_dve(dve, c):
            col, n = chunk_of(c)
            cs = slice(col, col + n)
            if c == 0:
                rr_dve(dve, 0)
            dve.wait_ge(st_ready, c + 1)
            dve.wait_ge(decay_ready, c + 1)
            if c:
                dve.wait_ge(num_ready, c)
                dve.wait_ge(cup_ready, 4 * c)
            nc.vector.tensor_tensor(sw[0:n, :, 0:n], hview(1, n, n), decay[0:n, :, 0:n], ALU.mult
                                    ).then_inc(sw_ready, 1)
            dve.wait_ge(bc_ready, c + 1)
            dve.wait_ge(c_new, 4 * c)
            nc.vector.tensor_copy(a_sb[:, :], hview(3, n)[:, :, n - 1])
            nc.vector.tensor_tensor(qs[:, :, 0:n], qk[:, 0:MH, cs], hview(3, n), ALU.mult).then_inc(qs_ready, 1)
            nc.vector.tensor_tensor(kts[0:n, :, :], hview(0, P, n),
                                    decay[0:n, :, n - 1:n].to_broadcast([n, MH, P]), ALU.mult
                                    ).then_inc(kts_ready, 1)
            if c < NBLK:
                rr_dve(dve, c + 1)
            dve.wait_ge(qs_ready, c + 1)
            for h in range(MH):
                dve.wait_ge(cup_ready, 4 * c + h + 1)
                if c == 0:
                    ins = nc.vector.tensor_copy(cst_[:, h, :], ps[:, CB[h], 0:VH])
                else:
                    dve.wait_ge(c_new, 4 * c - 3 + h)
                    ins = nc.vector.scalar_tensor_tensor(out=cst_[:, h, :], in0=cst_[:, h, :],
                                                         scalar=a_sb[:, h:h + 1], in1=ps[:, CB[h], 0:VH],
                                                         op0=ALU.mult, op1=ALU.add)
                ins.then_inc(c_new, 1)
            dve.wait_ge(e_ready, c + 1)
            dve.wait_ge(abs_ready, c + 1)
            nc.vector.tensor_tensor(dd[:, :, 0:n], dd[:, :, 0:n], e_sb[:, :, 0:n], ALU.max).then_inc(dd_step, 1)
            dve.wait_ge(dd_step, 2 * c + 1)
            nc.vector.tensor_tensor(dd[:, :, 0:n], dd[:, :, 0:n], dd[:, :, 0:n], ALU.mult).then_inc(dd_step, 1)
            dve.wait_ge(dd_step, 2 * c + 2)
            dve.wait_ge(ss_ready, c + 1)
            if c:
                dve.wait_ge(numr_ready, c)
            nc.vector.scalar_tensor_tensor(out=zr[:, :, 0:n], in0=dd[:, :, 0:n], scalar=EPS,
                                           in1=hview(2, n), op0=ALU.mult, op1=ALU.add).then_inc(z_ready, 1)
            dve.wait_ge(r_ready, c + 1)
            if c:
                dve.wait_ge(ylo_ready, c)
            for b in range(2):
                last = nc.vector.tensor_tensor(
                    numr[:, 2 * b:2 * b + 2, :, 0:n], num_banks(5 + b, n),
                    zr[:, 2 * b:2 * b + 2, 0:n].unsqueeze(2).to_broadcast([P, 2, 2, n]), ALU.mult)
            last.then_inc(numr_ready, 1)
            dve.wait_ge(numr_ready, c + 1)
            nf = numr[:, :, :, 0:n].rearrange("p h c n -> p (h c) n")
            if c == 0:
                dve.wait_ge(og_in, 16 * KC)
            nc.vector.tensor_tensor(nf, nf, og[:, :, cs], ALU.mult).then_inc(y_ready, 1)
            dve.wait_ge(yhi_ready, c + 1)
            nc.vector.tensor_tensor(y_lo[:, :, cs], nf, y_hi[:, :, cs].bitcast(F32), ALU.subtract
                                    ).then_inc(ylo_ready, 1)

        def chunk_act(act, c):
            col, n = chunk_of(c)
            cs = slice(col, col + n)
            act.wait_ge(d_ready, c + 1)
            if c:
                act.wait_ge(kts_ready, c)
            nc.scalar.activation(decay[0:n, :, 0:n], hview(2, n, n), ACT.Exp).then_inc(decay_ready, 1)
            act.wait_ge(bc_ready, c + 1)
            if c:
                act.wait_ge(dd_step, 2 * c)
            nc.scalar.activation(e_sb[:, :, 0:n], hview(4, n), ACT.Copy).then_inc(e_ready, 1)
            act.wait_ge(num_ready, c + 1)
            if c:
                act.wait_ge(ss_ready, c)
            if c:
                act.wait_ge(z_ready, c)
            nc.scalar.activation(dd[:, :, 0:n], hview(7, n), ACT.Abs).then_inc(abs_ready, 1)
            for b in range(2):
                last = nc.scalar.activation(nsq[:, 2 * b:2 * b + 2, :, 0:n], num_banks(5 + b, n), ACT.Square,
                                            scale=DV ** -0.5)
            last.then_inc(nsq_ready, 1)
            act.wait_ge(z_ready, c + 1)
            nc.scalar.activation(zr[:, :, 0:n], zr[:, :, 0:n], ACT.Ln).then_inc(ln_z, 1)
            act.wait_ge(ln_z, c + 1)
            nc.scalar.activation(zr[:, :, 0:n], zr[:, :, 0:n], ACT.Exp, scale=-0.5).then_inc(r_ready, 1)
            act.wait_ge(y_ready, c + 1)
            nc.scalar.activation(y_hi[:, :, cs], numr[:, :, :, 0:n].rearrange("p h c n -> p (h c) n"), ACT.Copy
                                 ).then_inc(yhi_ready, 1)

        def c0_pool(pool):
            for b in range(NB):
                pool.wait_ge(cup_ready, 4 * (b + 2))
                pool.dma_start(c0[:, b, :, 0:DV], a["state_C"][0, b].rearrange("h k v -> k h v")).then_inc(c0_in, 16)
                pool.dma_start(c0[:, b, :, DV:VH], a["state_n"][0, b].rearrange("h k -> k h").unsqueeze(2),
                               allow_slow_non_contiguous=True).then_inc(c0_in, 16)
            pool.wait_ge(c_new, 4 * TILES)
            pool.dma_start(out[6][0, 0].rearrange("h k v -> k h v"), cst_[:, :, 0:DV]).then_inc(stored, 16)
            pool.dma_start(out[7][0, 0].rearrange("h k -> k h").unsqueeze(2), cst_[:, :, DV:VH],
                           allow_slow_non_contiguous=True).then_inc(stored, 16)

        SC = slice(COL_S, COL_M)
        SN = SAMPLE

        def s_pe(pe):
            pe.wait_ge(c_new, 4 * TILES)
            pe.wait_ge(z_ready, TILES)
            for h in range(MH):
                last = nc.tensor.transpose(ps[0:SN, 0, P * h:P * h + P], qk[:, MH + h, SC], ident)
            for h in range(MH):
                last = nc.tensor.matmul(ps[0:SN, 1, SN * h:SN * h + SN], qk[:, MH + h, SC], qk[:, h, SC],
                                        start=True, stop=True)
            pe.wait_ge(sm_dve, 1)
            nc.tensor.matmul(ps[0:SN, 2, 0:MH * SN], ident[0:SN, 0:SN],
                             own_causal[0:SN, :].unsqueeze(1).to_broadcast([SN, MH, SN]), start=True, stop=False)
            for h in range(MH):
                last = nc.tensor.matmul(ps[0:SN, 2, SN * h:SN * h + SN], rows_u[0:64, SC], rr[0:64, h, 0:SN],
                                        start=False, stop=h == MH - 1)
            last.then_inc(sm_pe, 1)
            for w in range(2):
                for h in range(MH):
                    last = nc.tensor.matmul(ps[:, 3 + w, SN * h:SN * h + SN], selw[:, P * (MH * w + h):][:, 0:P],
                                            rows_m[:, SC], start=True, stop=True)
            last.then_inc(sm_pe, 1)
            pe.wait_ge(sm_dve, 3)
            pe.wait_ge(numr_ready, TILES)
            pe.wait_ge(dd_step, 2 * TILES)
            pe.wait_ge(c0_in, 32 * NB)
            for h in range(MH):
                for half in range(2):
                    f = 2 * h + half
                    o = ps[:, 5, SN * f:SN * f + SN]
                    nc.tensor.matmul(o, v[0:SN, NBLK, h, P * half:P * half + P], sw[0:SN, h, 0:SN],
                                     start=True, stop=False)
                    for b in range(NB):
                        nc.tensor.matmul(o[:, NS * b:NS * b + NS], c0[:, b, h, P * half:P * half + P],
                                         qs[:, h, NS * b:NS * b + NS], start=False, stop=b == NB - 1)
            nc.tensor.matmul(ps[:, 7, 0:MH * SN], ones[0:SN, :], sw[0:SN, :, 0:SN], start=True, stop=False)
            for h in range(MH):
                for b in range(NB):
                    c = SN * h + NS * b
                    last = nc.tensor.matmul(ps[:, 7, c:c + NS], c0[:, b, h, DV:VH].to_broadcast([P, P]),
                                            qs[:, h, NS * b:NS * b + NS], start=False,
                                            stop=h == MH - 1 and b == NB - 1)
            last.then_inc(sm_pe, 1)
            pe.wait_ge(sm_act, 2)
            pe.wait_ge(sm_dve, 4)
            for b in range(NB):
                pe.wait_ge(sm_kb, b + 1)
                if b:
                    pe.wait_ge(sm_c, 4 * b)
                for h in range(MH):
                    nc.tensor.matmul(ps[:, CB[h], 0:VH], kbs[b % 2][:, h, :], v[0:SN, NBLK, h, :],
                                     start=True, stop=True).then_inc(sm_cup, 1)
            pe.wait_ge(sm_act, 3)
            for half in range(2):
                last = nc.tensor.matmul(ps[:, 2, 0:MH * SN], ones, nsq[:, :, half, 0:SN], start=half == 0,
                                        stop=half == 1)
            last.then_inc(sm_pe, 1)

        kbs = [at(f"kb{i}", R2 + 16384 + 8192 + 4128 + 32 + 512 + 2048 * i, [SAMPLE, MH, P]) for i in range(2)]
        kt_s = at("kt_s", R2 + 2048 * 3, [SAMPLE, MH, P])
        sm_kb, sm_cup, sm_c = sem("sm_kb"), sem("sm_cup"), sem("sm_c")

        def s_dve(dve):
            step = [0]

            def inc(ins):
                step[0] += 1
                ins.then_inc(sm_dve, 1)
                return step[0]

            inc(nc.vector.tensor_tensor(rr[0:64, :, 0:SN],
                                        rows_m[0:64, SC].unsqueeze(1).to_broadcast([64, MH, SN]),
                                        selw[0:64, 8 * P:8 * P + MH].unsqueeze(2).to_broadcast([64, MH, SN]),
                                        ALU.mult))
            dve.wait_ge(sm_pe, 1)
            dve.wait_ge(sm_act, 1)
            inc(nc.vector.tensor_tensor(sw[0:SN, :, 0:SN], hview(1, SN, SN), decay[0:SN, :, 0:SN], ALU.mult))
            dve.wait_ge(sm_pe, 2)
            nc.vector.tensor_copy(a_s[:, :, :], hview(3, SN))
            inc(nc.vector.tensor_tensor(qs[:, :, 0:SN], qk[:, 0:MH, SC], hview(3, SN), ALU.mult))
            inc(nc.vector.tensor_copy(kt_s[:, :, :], hview(0, P, SN)))
            dve.wait_ge(sm_dve, 4)
            dve.wait_ge(sm_act, 2)
            for b in range(NB + 1):
                if b < NB:
                    if b >= 2:
                        dve.wait_ge(sm_cup, 4 * (b - 1))
                    nc.vector.tensor_tensor(kbs[b % 2][:, :, :], kt_s[:, :, :],
                                            decay[0:SN, :, NS * b + NS - 1:NS * b + NS].to_broadcast([SN, MH, P]),
                                            ALU.mult).then_inc(sm_kb, 1)
                if b:
                    for h in range(MH):
                        dve.wait_ge(sm_cup, 4 * (b - 1) + h + 1)
                        nc.vector.scalar_tensor_tensor(out=c0[:, b - 1, h, :], in0=c0[:, b - 1, h, :],
                                                       scalar=a_s[:, h, NS * b - 1:NS * b],
                                                       in1=ps[:, CB[h], 0:VH], op0=ALU.mult, op1=ALU.add
                                                       ).then_inc(sm_c, 1)
            dve.wait_ge(abs_ready, TILES + 1)
            inc(nc.vector.tensor_tensor(dd[:, :, 0:SN], dd[:, :, 0:SN], e_sb[:, :, 0:SN], ALU.max))
            dve.wait_ge(sm_dve, 5)
            inc(nc.vector.reciprocal(zr[:, :, 0:SN], dd[:, :, 0:SN]))
            dve.wait_ge(sm_dve, 6)
            num = ps[:, 5, 0:8 * SN].rearrange("p (h c n) -> p h c n", h=MH, c=2)
            inc(nc.vector.tensor_tensor(numr[:, :, :, 0:SN], num,
                                        zr[:, :, 0:SN].unsqueeze(2).to_broadcast([P, MH, 2, SN]), ALU.mult))
            dve.wait_ge(sm_act, 4)
            inc(nc.vector.tensor_tensor(numr[:, :, :, 0:SN], numr[:, :, :, 0:SN],
                                        zr[:, :, 0:SN].unsqueeze(2).to_broadcast([P, MH, 2, SN]), ALU.mult))
            dve.wait_ge(sm_dve, 8)
            nf = numr[:, :, :, 0:SN].rearrange("p h c n -> p (h c) n")
            inc(nc.vector.tensor_tensor(nf, nf, og[:, :, SC], ALU.mult))
            dve.wait_ge(sm_act, 5)
            inc(nc.vector.tensor_tensor(y_lo[:, :, SC], nf, y_hi[:, :, SC].bitcast(F32), ALU.subtract))

        def s_act(act):
            act.wait_ge(sm_pe, 1)
            nc.scalar.activation(decay[0:SN, :, 0:SN], hview(2, SN, SN), ACT.Exp).then_inc(sm_act, 1)
            act.wait_ge(sm_pe, 2)
            nc.scalar.activation(e_sb[:, :, 0:SN], hview(4, SN), ACT.Copy).then_inc(sm_act, 1)
            act.wait_ge(sm_pe, 3)
            nc.scalar.activation(dd[:, :, 0:SN], hview(7, SN), ACT.Abs).then_inc(abs_ready, 1)
            act.wait_ge(sm_dve, 7)
            nc.scalar.activation(nsq[:, :, :, 0:SN].rearrange("p h c n -> p (h c) n"),
                                 numr[:, :, :, 0:SN].rearrange("p h c n -> p (h c) n"), ACT.Square,
                                 scale=DV ** -0.5).then_inc(sm_act, 1)
            act.wait_ge(sm_pe, 4)
            nc.scalar.activation(zr[:, :, 0:SN], hview(2, SN), ACT.Ln, bias=eps[:, 0:1]).then_inc(ln_z, 1)
            act.wait_ge(ln_z, TILES + 1)
            nc.scalar.activation(zr[:, :, 0:SN], zr[:, :, 0:SN], ACT.Exp, scale=-0.5).then_inc(sm_act, 1)
            act.wait_ge(sm_dve, 9)
            nc.scalar.activation(y_hi[:, :, SC], numr[:, :, :, 0:SN].rearrange("p h c n -> p (h c) n"), ACT.Copy
                                 ).then_inc(sm_act, 1)

        def s_pool(pool):
            for b in range(NB):
                pool.wait_ge(sm_c, 4 * (b + 1))
                pool.dma_start(out[9][0, b].rearrange("h k v -> k h v"), c0[:, b, :, 0:DV]).then_inc(c0_out, 16)
                pool.dma_start(out[10][0, b].rearrange("h k -> k h").unsqueeze(2), c0[:, b, :, DV:VH],
                               allow_slow_non_contiguous=True).then_inc(c0_out, 16)
            pool.wait_ge(sm_dve, 10)
            pool.wait_ge(stored, 16 * 24)
            for f in range(KC):
                pool.dma_start(x2[:, f, :], scratch["x1"][:, f, :]).then_inc(x2_back, 16)

        def out_pe(pe):
            pe.wait_ge(sm_dve, 10)
            pe.wait_ge(ylo_ready, TILES)
            for c in range(KC):
                pe_unit(pe, U_OUT + c, N_OUT + c, y_hi, y_lo)

        def out_act(act):
            for c in range(KC):
                split_hi_static(act, U_OUT + c + AHEAD)

        def out_dve(dve):
            for c in range(KC):
                split_lo_static(dve, U_OUT + c + AHEAD)
                if c == 0:
                    dve.wait_ge(x2_back, 16 * KC)
                add_x_dve(dve, N_OUT + c, c, x2)

        y_st = at("y_st", R0, [P, TILES, D])
        y_t, y_act, y_dve, y_out = sem("y_t"), sem("y_by_act"), sem("y_by_dve"), sem("y_out")

        def y_pe(pe):
            pe.wait_ge(free_dve, OUT_ADDS + 8 * SLICES)
            for i in range(2 * TILES):
                half, t = divmod(i, TILES)
                n = x_rows(t)
                if i >= 8:
                    pe.wait_ge((y_act, y_dve)[i % 2], (i - 8) // 2 + 1)
                for f in range(4):
                    last = nc.tensor.transpose(ps[0:n, i % 8, P * f:P * f + P],
                                               x2[:, 4 * half + f, t * P:t * P + n], ident)
                last.then_inc(y_t, 1)

        def y_take(eng, i):
            half, t = divmod(i, TILES)
            n = x_rows(t)
            eng.wait_ge(y_t, i + 1)
            return y_st[0:n, t, 512 * half:512 * half + 512], ps[0:n, i % 8, :]

        def y_store(sp):
            for i in range(2 * TILES):
                half, t = divmod(i, TILES)
                sp.wait_ge((y_act, y_dve)[i % 2], i // 2 + 1)
                cols = slice(512 * half, 512 * half + 512)
                if t < NBLK:
                    sp.dma_start(out[0][0, t * P:t * P + P, cols], y_st[:, t, cols]).then_inc(y_out, 16)
                else:
                    sp.dma_start(out[1].rearrange("b s d -> (b s) d")[:, cols], y_st[0:SAMPLE, t, cols]
                                 ).then_inc(y_out, 16)
            sp.wait_ge(y_out, 16 * 2 * TILES)

        block = ctx.enter_context(nc.Block())

        @block.sync
        def _(sp):
            load_x(sp)
            for r in range(U_MLP0 // 2):
                if r >= 2:
                    sp.wait_ge(w_lo_ready, 2 * r - 2)
                load_qkv(sp, r) if r < 6 else load_wo(sp, r)
            with sp.Fori(0, SLICES) as i:
                mlp_slice_sp(sp, 0, U_MLP0, i)
            for r in range(U_IN // 2, U_MLP1 // 2):
                sp.wait_ge(w_lo_ready, 2 * r - 2)
                if r < U_OUT // 2:
                    load_cols(sp, a["mlstm_w_in"][0], r, 256 * (r - U_IN // 2))
                else:
                    load_cols(sp, a["mlstm_w_out"][0], r, 256 * (r - U_OUT // 2))
            with sp.Fori(0, SLICES) as i:
                mlp_slice_sp(sp, 1, U_MLP1, i)
            y_store(sp)

        @block.gpsimd
        def _(pool):
            nc.gpsimd.memset(rel_ext[BUCKETS:BUCKETS + 1, :], 1.0).then_inc(rel_one, 1)
            bias_pool(pool)
            pool.wait_ge(x_by_act, TILES)
            pool.wait_ge(x_by_dve, TILES)
            pool.dma_start(scratch["x0"], x[:, :, :]).then_inc(x_saved, 16)
            bias_read(pool)
            sample_loads(pool)
            caches_pool(pool)
            for n in range(NG):
                att_scale_pool(pool, n)
            sink_rows(pool)
            pool.wait_ge(sp_steps, 7)
            pool.wait_ge(stored, 16 * (2 + 2 + 16))
            reload_x(pool, "x0", 0)
            gates_pool(pool)
            gates_out(pool)
            og_pool(pool)
            c0_pool(pool)
            s_pool(pool)
            pool.wait_ge(c0_out, 32 * NB)
            pool.wait_ge(stored, 16 * 24)

        @block.scalar
        def _(act):
            act.preload_act_table_set("natural_log_exp_and_others")
            for dst, src in small:
                act.dma_start(dst, src, allow_slow_non_contiguous=True).then_inc(const_in, 16)
            for c in range(TILES):
                o, i = take_x(act, c, 0)
                nc.scalar.activation(o, i, ACT.Copy).then_inc(x_by_act, 1)
            act.wait_ge(x_by_act, TILES)
            act.wait_ge(x_by_dve, TILES)
            norm_act(act, 0)
            for u in range(AHEAD):
                split_hi_static(act, u)
            qkv_act(act)
            att_act(act)
            sample_act(act)
            wo_act(act)
            act.wait_ge(free_dve, 8)
            norm_act(act, 1)
            with act.Fori(0, SLICES) as i:
                mlp_slice_act(act, 0, U_MLP0, N_MLP0, i, 8)
            act.wait_ge(wg_in, 32)
            nc.scalar.activation(wg_hi[:, :, :], wg_raw[:, :, :], ACT.Copy).then_inc(wg_split_hi, 1)
            act.wait_ge(free_dve, MLP0_ADDS)
            norm_act(act, 2)
            gates_act1(act)
            in_act(act)
            act.preload_act_table_set("natural_log_exp_and_others")
            for c in range(TILES):
                chunk_act(act, c)
            s_act(act)
            out_act(act)
            act.wait_ge(free_dve, OUT_ADDS)
            norm_act(act, 3, x2)
            with act.Fori(0, SLICES - 1) as i:
                mlp_slice_act(act, 1, U_MLP1, N_MLP1, i, 8)
            mlp_slice_act(act, 1, U_MLP1, N_MLP1, SLICES - 1, 8 - AHEAD)
            for i in range(0, 2 * TILES, 2):
                o, src = y_take(act, i)
                nc.scalar.activation(o, src, ACT.Copy).then_inc(y_act, 1)

        @block.vector
        def _(dve):
            nc.vector.memset(eps[:, :], EPS)
            nc.vector.memset(x[:, :, T:TP], 0.0)
            dve.wait_ge(const_in, 16 * len(small))
            nc.vector.tensor_scalar(nsinks[:, :], sinks[:, :], -1.0, None, ALU.mult)
            nc.vector.tensor_scalar(bg15[0:MH, :], bgate[0:MH, :], 1.0 / CAP, None, ALU.mult)
            nc.vector.tensor_scalar(bg15[96:96 + MH, :], bgate[96:96 + MH, :], 1.0 / CAP, None, ALU.mult
                                    ).then_inc(gate_dve, 1)
            dve.wait_ge(line_mm, 1)
            nc.vector.tensor_copy(line[:, :], ps[0:QH, 0, 0:LINE]).then_inc(line_c, 1)
            for c in range(TILES):
                o, i = take_x(dve, c, 1)
                nc.vector.tensor_copy(o, i).then_inc(x_by_dve, 1)
            dve.wait_ge(x_by_dve, TILES)
            dve.wait_ge(x_by_act, TILES)
            norm_dve(dve, 0)
            for u in range(AHEAD):
                split_lo_static(dve, u)
            qkv_dve(dve)
            caches_dve(dve)
            dve.wait_ge(qk_normed, 30)
            nc.vector.memset(o_hi[:, :, T:TP].bitcast(F32), 0.0)
            nc.vector.memset(o_lo[:, :, T:TP].bitcast(F32), 0.0)
            att_dve(dve)
            sample_dve(dve)
            sample_dve2(dve)
            wo_dve(dve)
            dve.wait_ge(free_dve, 8)
            norm_dve(dve, 1)
            with dve.Fori(0, SLICES) as i:
                mlp_slice_dve(dve, 0, U_MLP0, N_MLP0, i, 8)
            dve.wait_ge(out_ready, N_IN)
            nc.vector.memset(wg_raw[:, :, :], 0.0).then_inc(wg_zero, 1)
            dve.wait_ge(wg_split_hi, 1)
            nc.vector.tensor_tensor(wg_lo[:, :, :], wg_raw[:, :, :], wg_hi[:, :, :].bitcast(F32), ALU.subtract
                                    ).then_inc(wg_split, 1)
            dve.wait_ge(free_dve, MLP0_ADDS)
            norm_dve(dve, 2)
            in_dve(dve)
            dve.wait_ge(v2_taken, 24)
            dve.wait_ge(og_out, 16 * KC)
            nc.vector.tensor_copy(v_m[:, :, :], v[SAMPLE:LAST, NBLK, :, :]).then_inc(vm_done, 1)
            nc.vector.memset(y_hi[:, :, T:TP].bitcast(F32), 0.0)
            dve.wait_ge(out_ready, N_OUT)
            dve.wait_ge(og_in, 16 * KC)
            nc.vector.memset(y_lo[:, :, T:TP].bitcast(F32), 0.0)
            dve.wait_ge(sel_in, 16)
            for c in range(TILES):
                chunk_dve(dve, c)
            s_dve(dve)
            out_dve(dve)
            dve.wait_ge(free_dve, OUT_ADDS)
            dve.wait_ge(c0_out, 32 * NB)
            norm_dve(dve, 3, x2, h_lo2)
            with dve.Fori(0, SLICES - 1) as i:
                mlp_slice_dve(dve, 1, U_MLP1, N_MLP1, i, 8, x2)
            mlp_slice_dve(dve, 1, U_MLP1, N_MLP1, SLICES - 1, 8 - AHEAD, x2)
            for i in range(1, 2 * TILES, 2):
                o, src = y_take(dve, i)
                nc.vector.tensor_copy(o, src).then_inc(y_dve, 1)

        @block.tensor
        def _(pe):
            pe.wait_ge(line_in, 32)
            pe.wait_ge(rel_one, 1)
            nc.tensor.matmul(ps[0:QH, 0, 0:LINE], rel_ext[:, :], bucket[:, :], start=True, stop=True
                             ).then_inc(line_mm, 1)
            pe.wait_ge(line_c, 1)
            load_pe(pe)
            def before():
                pe.wait_ge(x_by_act, TILES)
                pe.wait_ge(x_by_dve, TILES)
            norm_pe(pe, 0, before)
            qkv_pe(pe)
            caches_pe(pe)
            att_pe(pe)
            sample_pe(pe)
            wo_pe(pe)
            norm_pe(pe, 1, lambda: pe.wait_ge(free_dve, 8))
            pe.wait_ge(norm_lo, 2 * KC)
            with pe.Fori(0, SLICES) as i:
                mlp_slice_pe(pe, 0, U_MLP0, N_MLP0, i)
            norm_pe(pe, 2, lambda: pe.wait_ge(free_dve, MLP0_ADDS))
            gates_pe(pe)
            in_pe(pe)
            pe.wait_ge(vm_done, 1)
            pe.wait_ge(sel_in, 16)
            pe.wait_ge(gate_act, 3)
            pe.wait_ge(*freed(N_OUT - 1))
            for c in range(TILES):
                chunk_pe(pe, c)
            s_pe(pe)
            out_pe(pe)
            norm_pe(pe, 3, lambda: pe.wait_ge(free_dve, OUT_ADDS))
            pe.wait_ge(norm_lo, 4 * KC)
            with pe.Fori(0, SLICES) as i:
                mlp_slice_pe(pe, 1, U_MLP1, N_MLP1, i, h_lo2)
            y_pe(pe)


_INS = ["x_prompt", "x_sample", "cache_k", "cache_v", "state_C", "state_n", "state_m", "meta_tokens",
        "rel_table", "norm_mix", "norm_mlp", "attn_w_qkv", "attn_q_norm", "attn_k_norm", "attn_sinks",
        "attn_w_o", "mlstm_w_in", "mlstm_w_gate", "mlstm_b_gate", "mlstm_out_norm", "mlstm_w_out",
        "mlp_w_up", "mlp_w_down"]
_OUTS = [(1, SEQ, D), (NB, NS, D),
         (1, 1, WIN, KH, HD), (1, 1, WIN, KH, HD), (1, NB, WIN, KH, HD), (1, NB, WIN, KH, HD),
         (1, 1, MH, DK, DV), (1, 1, MH, DK), (1, 1, MH),
         (1, NB, MH, DK, DV), (1, NB, MH, DK), (1, NB, MH)]
_SCRATCH = {"x0": [P, KC, TP], "x1": [P, KC, TP], "og": [P, KC, TP], "line": [QH, BLK, LINE]}


def kernel(**inputs):
    import concourse.bacc as _bacc
    from concourse.bass_utils import run_bass_kernel_spmd as _run

    nc = _bacc.Bacc("TRN2", target_bir_lowering=False, num_devices=1)
    arrays, args = {}, {}
    for name in _INS:
        arr = np.ascontiguousarray(inputs[name])
        arrays[f"in_{name}"] = arr
        args[name] = nc.dram_tensor(f"in_{name}", arr.shape, F32, kind="ExternalInput").ap()
    consts = {"const": np.concatenate([CONST[k] for k in CONST], axis=1), "select": selector_constants(),
              "buckets": bucket_constant(), "keep": scan_constant()}
    for name, arr in consts.items():
        arr = np.ascontiguousarray(arr)
        arrays[f"in_{name}"] = arr
        args[name] = nc.dram_tensor(f"in_{name}", arr.shape, F32, kind="ExternalInput").ap()
    outs = [nc.dram_tensor(f"out_{i}", shape, F32, kind="ExternalOutput").ap() for i, shape in enumerate(_OUTS)]
    scratch = {k: nc.dram_tensor(f"scratch_{k}", s, F32, kind="Internal").ap() for k, s in _SCRATCH.items()}
    build(nc, args, outs, scratch)
    r = _run(nc, [arrays], core_ids=[0])
    return tuple(r.results[0][f"out_{i}"] for i in range(len(_OUTS)))
```

```python
from contextlib import ExitStack

import numpy as np

import concourse.bass as bass
from concourse import mybir

F32 = mybir.dt.float32
F32R = mybir.dt.float32r
ACT = mybir.ActivationFunctionType
ALU = mybir.AluOpType
AX = mybir.AxisListType.X

P = 128
D = 1024
KC = D // P
SEQ, META, NB, NS = 1024, 16, 8, 4
SAMPLE = NB * NS
BLK = 128
NBLK = SEQ // BLK
COL_S = SEQ
COL_M = SEQ + SAMPLE
T = SEQ + SAMPLE + META
TG = 358
TP = 3 * TG
TILES = NBLK + 1
LAST = SAMPLE + META
EPS = 1e-6
QH, KH, HD, WIN = 16, 4, 64, 128
MH, DK, DV = 4, 128, 256
VH = DV + 1
FF = 4096
SLICES = 8
NEG = -1e30
CAP = 15.0
BUCKETS, MAX_DISTANCE = 32, 128
LINE = 384

U_QKV, U_WO, U_MLP0 = 0, 12, 20
U_IN = U_MLP0 + 8 * SLICES
U_OUT = U_IN + 24
U_MLP1 = U_OUT + 8
U_END = U_MLP1 + 8 * SLICES
N_QKV, N_WO, N_MLP0 = 0, 12, 20
N_IN = N_MLP0 + 12 * SLICES
N_OUT = N_IN + 25
N_MLP1 = N_OUT + 8
AHEAD = 2


def outs_through(u):
    if u < U_MLP0:
        return u + 1
    if u < U_IN:
        i, j = divmod(u - U_MLP0, 8)
        return N_MLP0 + 12 * i + (j + 1 if j < 4 else 2 * j - 2)
    if u < U_OUT:
        return N_IN + 1 + (u - U_IN) + 1
    if u < U_MLP1:
        return N_OUT + (u - U_OUT) + 1
    i, j = divmod(u - U_MLP1, 8)
    return N_MLP1 + 12 * i + (j + 1 if j < 4 else 2 * j - 2)


def is_down(u):
    for u0 in (U_MLP0, U_MLP1):
        if u0 <= u < u0 + 8 * SLICES:
            return (u - u0) % 8 >= 4
    return False


def shape_constants():
    c = {}
    c["ident"] = np.eye(P, dtype=np.float32)
    c["ones"] = np.ones((P, P), np.float32)
    two = np.zeros((P, P), np.float32)
    two[:HD, :HD] = 1.0
    two[HD:, HD:] = 1.0
    c["head_ones"] = two
    j, t = np.arange(P)[:, None], np.arange(P)[None, :]
    c["causal"] = np.where(j <= t, 0.0, NEG).astype(np.float32)
    js, ts = j[:SAMPLE], t[:, :SAMPLE]
    own = (js // NS == ts // NS) & (js <= ts)
    c["own_causal"] = np.zeros((P, SAMPLE), np.float32)
    c["own_causal"][:SAMPLE] = np.where(own, 0.0, NEG)
    return c


def selector_constants():
    sel = np.zeros((P, 8, P), np.float32)
    for h in range(MH):
        sel[64 + h, h, :] = 1.0
        sel[96 + h, 4 + h, :] = 1.0
    pair = np.zeros((P, MH), np.float32)
    for h in range(MH):
        pair[h, h] = pair[32 + h, h] = 1.0
    return np.concatenate([sel.reshape(P, -1), pair], axis=1)


def bucket_constant():
    out = np.zeros((BUCKETS + 1, LINE), np.float32)
    exact = BUCKETS // 2
    for e in range(LINE):
        dist = 2 * BLK - 1 - e
        if 0 <= dist <= WIN:
            b = dist if dist < exact else exact + int(
                np.log(dist / exact) / np.log(MAX_DISTANCE / exact) * (BUCKETS - exact) + 1e-6)
            out[min(b, BUCKETS - 1), e] = 1.0
        else:
            out[BUCKETS, e] = NEG
    return out


def scan_constant():
    keep = np.ones((MH, TP), np.float32)
    keep[:, 0:SEQ:BLK] = 0.0
    keep[:, COL_S:COL_M:NS] = 0.0
    keep[:, COL_M] = 0.0
    return keep


CONST = shape_constants()
CONST_AT, _n = {}, 0
for _k, _v in CONST.items():
    CONST_AT[_k] = (_n, _n + _v.shape[1])
    _n += _v.shape[1]
CONST_COLS = _n


def build(nc, a, out, scratch):
    with ExitStack() as ctx:
        R0 = 16512
        R1 = R0 + 37024
        R2 = R1 + 34368
        R3 = R2 + 34368
        RAW = R3 + 34368
        WHI = RAW + 16384
        WLO = WHI + 16384
        R4 = WLO + 16384
        BUF = 4320
        RC = R4 + 4 * BUF

        def at(name, offset, shape, dt=F32):
            return nc.alloc_sbuf_tensor_at(name, shape, dt, offset=offset)

        x = at("x", R0, [P, KC, TP])
        x_tok = at("x_tok", R1, [P, TILES, D])
        h_hi = at("h_hi", R1, [P, KC, TP], F32R)
        h_lo = at("h_lo", R2, [P, KC, TP], F32R)
        act_hi = at("act_hi", R3, [P, 4, TP], F32R)
        act_lo = at("act_lo", R3 + 4 * TP * 4, [P, 4, TP], F32R)
        raw = at("raw", RAW, [P, 2, 2048])
        w_hi = at("w_hi", WHI, [P, 4, 1024], F32R)
        w_lo = at("w_lo", WLO, [P, 4, 1024], F32R)
        sq = [at(f"sq{i}", R4 + i * BUF, [P, TP]) for i in range(2)]
        relu = [at(f"relu{i}", R4 + i * BUF, [P, TP]) for i in range(2)]
        rstd = at("rstd", R4 + 2 * BUF, [P, 3, TG])
        acc = at("acc", R4 + 3 * BUF, [P, TP])
        relu_sq = at("relu_sq", R4 + 3 * BUF, [P, TP])
        head_rstd = at("head_rstd", R4 + 3 * BUF, [P, 3, TG])
        q = at("q", R3, [P, KC, TP])
        kn = at("kn", R0, [P, 2, TP])
        v_tok = at("v_tok", R0 + 8608, [P, TILES, KH * HD])
        bias = at("bias", R0 + 8608 + 9216, [P, QH, 2 * BLK])
        v_meta = at("v_meta", R0 + 8608 + 9216 + 16384, [META, KH * HD])
        vT = [at(f"vT{i}", R4 + i * BUF, [P, TP]) for i in range(2)]
        cst = at("cst", RC, [P, CONST_COLS])
        at_c = RC + (CONST_COLS * 4 + 31) // 32 * 32
        gains = at("gains", at_c, [P, 5, KC])
        qk_gain = at("qk_gain", at_c + 320, [P, 2])
        gain_rows = at("gain_rows", at_c + 352, [5 * KC, P])
        sinks = at("sinks", at_c + 160, [P, QH])
        nsinks = at("nsinks", at_c + 224, [P, QH])
        eps = at("eps", at_c + 288, [P, 1])
        tokout = [at(f"tokout{i}", at_c + 352 + i * 1024, [P, 256]) for i in range(2)]
        gain_of = (0, 2, 1, 3)
        ident = cst[:, slice(*CONST_AT["ident"])]
        ones = cst[:, slice(*CONST_AT["ones"])]
        head_ones = cst[:, slice(*CONST_AT["head_ones"])]

        ps = ctx.enter_context(nc.psum_tensor("ps", [P, 8, 512], F32))

        def grp(ap):
            return ap.rearrange("p (g n) -> p g n", g=3)

        def sem(name):
            return ctx.enter_context(nc.semaphore(name))

        x_in = [sem(f"x_in{c}") for c in range(TILES)]
        ident_in, gains_in, const_in = sem("ident_in"), sem("gains_in"), sem("const_in")
        gains_t, gains_ready = sem("gains_t"), sem("gains_ready")
        xt_ready = sem("xt_ready")
        x_by_act, x_by_dve = sem("x_by_act"), sem("x_by_dve")
        raw_in = [sem("raw_in0"), sem("raw_in1")]
        w_hi_ready, w_lo_ready = sem("w_hi_ready"), sem("w_lo_ready")
        out_ready = sem("out_ready")
        out_free = sem("out_free")
        norm_sq, norm_acc, norm_summed = sem("norm_sq"), sem("norm_acc"), sem("norm_summed")
        norm_ln, norm_rstd = sem("norm_ln"), sem("norm_rstd")
        norm_hi, norm_lo = sem("norm_hi"), sem("norm_lo")
        x_saved, x1_saved, x_back = sem("x_saved"), sem("x1_saved"), sem("x_back")
        head_sq = sem("head_sq")
        qk_sum, qk_ln, qk_rstd, qk_normed = sem("qk_sum"), sem("qk_ln"), sem("qk_rstd"), sem("qk_normed")
        vt_ready, v_taken = sem("vt_ready"), sem("v_taken")
        up_done, act_split, sq_done = sem("up_done"), sem("act_split"), sem("sq_done")
        line_out = sem("line_out")
        cache_t, cache_c, stored = sem("cache_t"), sem("cache_c"), sem("stored")

        raw_k8 = raw[:, :, :].rearrange("p s (k n) -> p s k n", k=8)
        raw_k4 = raw[:, :, :].rearrange("p s (k n) -> p s k n", k=4)
        raw_per = [64] * 4 + [16] * 2 + [64] * 4 + [16] * 200

        def raw_target(r):
            return sum(raw_per[r % 2:r + 1:2])

        def raw_unit(j, slot, down):
            if down:
                return raw_k4[:, slot, :, 256 * j:256 * j + 256]
            return raw_k8[:, slot, :, 128 * j:128 * j + 128]

        def unit_view(w, slot, down):
            return w[:, slot, :].rearrange("p (k n) -> p k n", k=4 if down else 8)

        def split_hi(act, slot, rslot, j, down, raw_wait, outs_wait):
            act.wait_ge(raw_in[rslot], raw_wait)
            if outs_wait is not None:
                act.wait_ge(out_ready, outs_wait)
            nc.scalar.activation(unit_view(w_hi, slot, down), raw_unit(j, rslot, down),
                                 ACT.Copy).then_inc(w_hi_ready, 1)

        def split_lo(dve, slot, rslot, j, down, hi_wait):
            dve.wait_ge(w_hi_ready, hi_wait)
            nc.vector.tensor_tensor(unit_view(w_lo, slot, down), raw_unit(j, rslot, down),
                                    unit_view(w_hi, slot, down).bitcast(F32), ALU.subtract
                                    ).then_inc(w_lo_ready, 1)

        def split_hi_static(act, u):
            if u < U_END:
                split_hi(act, u % 4, (u // 2) % 2, u % 2, is_down(u), raw_target(u // 2),
                         outs_through(u - 4) if u >= 4 else None)

        def split_lo_static(dve, u):
            if u < U_END:
                split_lo(dve, u % 4, (u // 2) % 2, u % 2, is_down(u), u + 1)

        def out_banks(n):
            return 3 * (n % 2)

        def chunk_mms(slot, k, kc, cols, bank, hi, lo, k_of, start, stop, groups=None):
            wh = w_hi[:, slot, :].rearrange("p (k n) -> p k n", k=kc)[:, k, cols]
            wl = w_lo[:, slot, :].rearrange("p (k n) -> p k n", k=kc)[:, k, cols]
            for g in range(3):
                o = ps[:, bank + g, 0:TG]
                c = slice(g * TG, g * TG + TG)
                nc.tensor.matmul(o, wh, hi[:, k_of, c], start=start, stop=False)
                nc.tensor.matmul(o, wh, lo[:, k_of, c], start=False, stop=False)
            for g in range(3):
                last = nc.tensor.matmul(ps[:, bank + g, 0:TG], wl, hi[:, k_of, g * TG:g * TG + TG],
                                        start=False, stop=stop)
            return last

        def w_block(w, slot, k, kc, cols):
            return w[:, slot, :].rearrange("p (k n) -> p k n", k=kc)[:, k, cols]

        def pass_hi(slot, k, kc, cols, bank, hi, start):
            for i, w in enumerate((w_hi, w_lo)):
                for g in range(3):
                    nc.tensor.matmul(ps[:, bank + g, 0:TG], w_block(w, slot, k, kc, cols),
                                     hi[:, k, g * TG:g * TG + TG], start=start and i == 0, stop=False)

        def pass_lo(slot, k, kc, cols, bank, lo, stop):
            for g in range(3):
                last = nc.tensor.matmul(ps[:, bank + g, 0:TG], w_block(w_hi, slot, k, kc, cols),
                                        lo[:, k, g * TG:g * TG + TG], start=False, stop=stop)
            return last

        def pe_unit(pe, u, n, hi, lo, sides=None, first_norm=None):
            pe.wait_ge(w_lo_ready, u + 1)
            if n >= 2:
                pe.wait_ge(out_free, n - 1)
            for k in range(KC):
                if first_norm is not None:
                    pe.wait_ge(norm_lo, KC * first_norm + k + 1)
                if sides and k in (2, 4, 6):
                    sides(k // 2 - 1)
                last = chunk_mms(u % 4, k, 8, slice(0, P), out_banks(n), hi, lo, k, k == 0, k == KC - 1)
            last.then_inc(out_ready, 1)

        def norm_act(act, m, f, x, h_hi):
            nc.scalar.activation(h_hi[:, f, :], x[:, f, :], ACT.Copy,
                                 scale=gains[:, gain_of[m], f:f + 1]).then_inc(norm_hi, 1)
            if f >= 2:
                act.wait_ge(norm_acc, (KC - 1) * m + f - 1)
            nc.scalar.activation(sq[f % 2][:, :], x[:, f, :], ACT.Square).then_inc(norm_sq, 1)

        def norm_lo_dve(dve, m, f, x, h_hi, h_lo):
            dve.wait_ge(norm_hi, KC * m + f + 1)
            nc.vector.scalar_tensor_tensor(out=h_lo[:, f, :], in0=x[:, f, :], scalar=gains[:, gain_of[m], f:f + 1],
                                           in1=h_hi[:, f, :].bitcast(F32), op0=ALU.mult, op1=ALU.subtract
                                           ).then_inc(norm_lo, 1)

        def norm_acc_dve(dve, m, f):
            dve.wait_ge(norm_sq, KC * m + f + 1)
            if f >= 2:
                dve.wait_ge(norm_acc, (KC - 1) * m + f - 1)
            first = sq[0] if f == 1 else acc
            nc.vector.tensor_tensor(acc[:, :], first[:, :], sq[f % 2][:, :], ALU.add).then_inc(norm_acc, 1)

        def norm_pe(pe, m, g):
            pe.wait_ge(norm_acc, (KC - 1) * (m + 1))
            if g == 2:
                pe.wait_ge(norm_ln, 3 * m + 1)
            nc.tensor.matmul(ps[:, 6 + g % 2, 0:TG], ones, acc[:, g * TG:g * TG + TG], start=True, stop=True
                             ).then_inc(norm_summed, 1)

        def norm_rstd_act(act, m):
            for g in range(3):
                act.wait_ge(norm_summed, 3 * m + g + 1)
                nc.scalar.activation(rstd[:, g, :], ps[:, 6 + g % 2, 0:TG], ACT.Ln, scale=1.0 / D,
                                     bias=eps[:, 0:1]).then_inc(norm_ln, 1)
            act.wait_ge(norm_ln, 3 * m + 3)
            nc.scalar.activation(rstd[:, :, :], rstd[:, :, :], ACT.Exp, scale=-0.5).then_inc(norm_rstd, 1)

        def times_rstd(dst, n, scale=1.0, rows=slice(0, P)):
            nc.vector.scalar_tensor_tensor(out=dst, in0=ps[rows, out_banks(n):out_banks(n) + 3, 0:TG], scalar=scale,
                                           in1=rstd[rows, :, :], op0=ALU.mult, op1=ALU.mult
                                           ).then_inc(out_free, 1)

        def x_rows(c):
            return BLK if c < NBLK else LAST

        small = []
        for half in range(2):
            small += [(qk_gain[HD * half:HD * half + HD, 0:1], a["attn_q_norm"].rearrange("a d -> d a")),
                      (qk_gain[HD * half:HD * half + HD, 1:2], a["attn_k_norm"].rearrange("a d -> d a"))]
        for s in range(4):
            gp, ip = divmod(s, 2)
            small += [(sinks[:, 4 * s:4 * s + 4].rearrange("p (a b) -> p a b", a=2),
                       bass.AP(a["attn_sinks"].tensor, 8 * gp + 2 * ip, [[0, P], [4, 2], [1, 2]]))]

        def load_x(sp):
            for c in range(TILES):
                if c < NBLK:
                    sp.dma_start(x_tok[:, c, :], a["x_prompt"][0, c * P:c * P + P, :]).then_inc(x_in[c], 16)
                else:
                    sp.dma_start(x_tok[0:SAMPLE, c, :], a["x_sample"].rearrange("b s d -> (b s) d")
                                 ).then_inc(x_in[c], 16)
                    sp.dma_start(x_tok[SAMPLE:LAST, c, :], a["meta_tokens"]).then_inc(x_in[c], 16)

        def x_tile_wait(eng, c):
            eng.wait_ge(x_in[c], 16 if c < NBLK else 32)

        def load_pe(pe):
            pe.wait_ge(ident_in, 16)
            for c in range(TILES):
                x_tile_wait(pe, c)
                n = x_rows(c)
                for half in range(2):
                    i = 2 * c + half
                    if i >= 8:
                        pe.wait_ge((x_by_act, x_by_dve)[half], (i - 8) // 2 + 1)
                    for f in range(4):
                        last = nc.tensor.transpose(ps[:, i % 8, f * P:f * P + n],
                                                   x_tok[0:n, c, (4 * half + f) * P:(4 * half + f + 1) * P],
                                                   ident[0:n, 0:n])
                    last.then_inc(xt_ready, 1)

        def take_x(eng, c, half):
            n = x_rows(c)
            eng.wait_ge(xt_ready, 2 * c + half + 1)
            src = ps[:, (2 * c + half) % 8, :].rearrange("p (f n) -> p f n", f=4)[:, :, 0:n]
            return x[:, 4 * half:4 * half + 4, c * P:c * P + n], src

        def load_qkv(sp, r):
            w = a["attn_w_qkv"][0].rearrange("(k p) n -> p k n", p=P)
            if r < 4:
                gp, i = r // 2, 2 * (r % 2)
                dst = raw_k8[:, r % 2, :, :].rearrange("p k (c g d) -> p k c g d", c=2, g=2)
                for g in range(2):
                    for c in range(2):
                        c0 = gp * 512 + g * 256 + (i + c) * HD
                        sp.dma_start(dst[:, :, c, g, :], w[:, :, c0:c0 + HD]).then_inc(raw_in[r % 2], 16)
            else:
                sp.dma_start(raw_k8[:, r % 2, :, :], w[:, :, 256 * r:256 * r + 256]).then_inc(raw_in[r % 2], 16)

        def load_wo(sp, r):
            w = a["attn_w_o"][0].rearrange("(gp g i d) n -> gp g d i n", gp=2, g=2, i=4)
            c0 = 256 * (r - U_WO // 2)
            for gp in range(2):
                for g in range(2):
                    sp.dma_start(raw_k8[HD * g:HD * g + HD, r % 2, 4 * gp:4 * gp + 4, :],
                                 w[gp, g][:, :, c0:c0 + 256]).then_inc(raw_in[r % 2], 16)

        def load_cols(sp, w, r, c0):
            sp.dma_start(raw_k8[:, r % 2, :, :],
                         w.rearrange("(k p) n -> p k n", p=P)[:, :, c0:c0 + 256]).then_inc(raw_in[r % 2], 16)

        def qk_dst(c):
            return q[:, c, :] if c < 8 else kn[:, c - 8, :]

        def side_bank(s):
            return 6 + s % 2

        def qkv_side_pe(pe, c, g):
            s = 3 * c + g
            if s >= 2:
                t = s - 2
                pe.wait_ge(qk_ln, t + 1) if t < 30 else pe.wait_ge(v_taken, t - 29)
            elif s == 0:
                pe.wait_ge(norm_ln, 3)
            if c < 10:
                pe.wait_ge(head_sq, c + 1)
                nc.tensor.matmul(ps[:, side_bank(s), 0:TG], head_ones, sq[c % 2][:, g * TG:g * TG + TG],
                                 start=True, stop=True).then_inc(qk_sum, 1)
            else:
                pe.wait_ge(out_free, c + 1)
                src = vT[c - 10]
                for t in range(4 * g, min(4 * g + 4, TILES)):
                    n = x_rows(t)
                    last = nc.tensor.transpose(ps[0:n, side_bank(s), (t % 4) * P:(t % 4) * P + P],
                                               src[:, t * P:t * P + n], ident)
                last.then_inc(vt_ready, 1)

        def qkv_pe(pe):
            for c in range(12):
                sides = (lambda g, c=c: qkv_side_pe(pe, c - 1, g)) if c else (lambda g: norm_pe(pe, 0, g))
                pe_unit(pe, c, c, h_hi, h_lo, sides, 0 if c == 0 else None)
            for g in range(3):
                qkv_side_pe(pe, 11, g)

        def qkv_side_act(act, c):
            for g in range(3):
                s = 3 * c + g
                act.wait_ge(qk_sum, s + 1)
                if c:
                    act.wait_ge(qk_normed, s - 2)
                nc.scalar.activation(head_rstd[:, g, :], ps[:, side_bank(s), 0:TG], ACT.Ln,
                                     scale=1.0 / HD, bias=eps[:, 0:1]).then_inc(qk_ln, 1)
                act.wait_ge(qk_ln, s + 1)
                nc.scalar.activation(head_rstd[:, g, :], head_rstd[:, g, :], ACT.Exp, scale=-0.5
                                     ).then_inc(qk_rstd, 1)

        def qkv_act(act):
            for c in range(12):
                split_hi_static(act, c + AHEAD)
                if c == 0:
                    norm_rstd_act(act, 0)
                elif c <= 10:
                    qkv_side_act(act, c - 1)
                if c < 10:
                    act.wait_ge(out_free, c + 1)
                    if c >= 2:
                        act.wait_ge(qk_sum, 3 * (c - 1))
                    nc.scalar.activation(sq[c % 2][:, :], qk_dst(c), ACT.Square).then_inc(head_sq, 1)

        def qkv_side_dve(dve, c):
            for g in range(3):
                s = 3 * c + g
                if c < 10:
                    dve.wait_ge(qk_rstd, s + 1)
                    d = qk_dst(c)[:, g * TG:g * TG + TG]
                    nc.vector.scalar_tensor_tensor(out=d, in0=d, scalar=qk_gain[:, c // 8:c // 8 + 1],
                                                   in1=head_rstd[:, g, :], op0=ALU.mult, op1=ALU.mult
                                                   ).then_inc(qk_normed, 1)
                else:
                    dve.wait_ge(vt_ready, s - 29)
                    n, tiles = (P, 4) if g < 2 else (LAST, 1)
                    nc.vector.tensor_copy(
                        v_tok[0:n, 4 * g:4 * g + tiles, (c - 10) * P:(c - 9) * P],
                        ps[0:n, side_bank(s), :].rearrange("p (t n) -> p t n", t=4)[:, 0:tiles, :]
                    ).then_inc(v_taken, 1)

        def qkv_dve(dve):
            for c in range(12):
                split_lo_static(dve, c + AHEAD)
                if c:
                    qkv_side_dve(dve, c - 1)
                dve.wait_ge(out_ready, c + 1)
                if c == 0:
                    dve.wait_ge(norm_rstd, 1)
                if c == 8:
                    dve.wait_ge(x_saved, 16)
                if c >= 10:
                    dve.wait_ge(qk_sum, 27 + 3 * (c - 10))
                times_rstd(grp(qk_dst(c) if c < 10 else vT[c - 10][:, :]), c)
            qkv_side_dve(dve, 11)

        cache_src = [(NBLK - 1, BLK), (NBLK, SAMPLE)]

        def caches_pe(pe):
            for j, (t, n) in enumerate(cache_src):
                for gp in range(2):
                    last = nc.tensor.transpose(ps[0:n, 6 + j, gp * P:gp * P + P], kn[:, gp, t * P:t * P + n], ident)
                last.then_inc(cache_t, 1)

        def caches_dve(dve):
            for j, (t, n) in enumerate(cache_src):
                dve.wait_ge(cache_t, j + 1)
                nc.vector.tensor_copy(tokout[j][0:n, :], ps[0:n, 6 + j, 0:256]).then_inc(cache_c, 1)

        def caches_pool1(pool):
            for i in range(2):
                src = a["cache_k" if i == 0 else "cache_v"][0]
                pool.dma_start(out[4 + i][0][:, 0:WIN - NS, :, :], src[:, NS:WIN, :, :]).then_inc(stored, 16)
            pool.wait_ge(v_taken, 6)
            pool.dma_start(out[3][0, 0].rearrange("s h d -> s (h d)"), v_tok[:, NBLK - 1, :]).then_inc(stored, 16)
            for b in range(NB):
                pool.dma_start(out[5][0, b, WIN - NS:WIN].rearrange("s h d -> s (h d)"),
                               v_tok[NS * b:NS * b + NS, NBLK, :]).then_inc(stored, 16)

        def caches_pool2(pool):
            pool.wait_ge(cache_c, 2)
            pool.dma_start(out[2][0, 0].rearrange("s h d -> s (h d)"), tokout[0][:, :]).then_inc(stored, 16)
            for b in range(NB):
                pool.dma_start(out[4][0, b, WIN - NS:WIN].rearrange("s h d -> s (h d)"),
                               tokout[1][NS * b:NS * b + NS, :]).then_inc(stored, 16)

        rel_ext = at("rel_ext", R4 + 2 * BUF, [BUCKETS + 1, QH])
        bucket = at("bucket", R4 + 2 * BUF + 64, [BUCKETS + 1, LINE])
        line = at("line", R0 + 35232, [QH, LINE])
        s_bias = at("s_bias", R1, [P, WIN + NS])
        line_in, line_mm, line_c = sem("line_in"), sem("line_mm"), sem("line_c")
        bias_in, sbias_in = sem("bias_in"), sem("sbias_in")
        rel_one = sem("rel_one")

        def bias_pool(pool):
            pool.dma_start(bucket[:, :], a["buckets"]).then_inc(line_in, 16)
            pool.dma_start(rel_ext[0:BUCKETS, :], a["rel_table"]).then_inc(line_in, 16)
        def line_src(base, dims):
            return bass.AP(scratch["line"].tensor, base, dims)

        def line_write(sp):
            sp.wait_ge(line_c, 1)
            sp.dma_start(scratch["line"][:, :, :], line[:, :].unsqueeze(1).to_broadcast([QH, BLK, LINE])
                         ).then_inc(line_out, 16)

        def bias_read(sp):
            sp.wait_ge(line_out, 16)
            sp.wait_ge(x_saved, 16)
            sp.wait_ge(norm_lo, KC)
            sp.wait_ge(norm_sq, KC)
            for s in range(4):
                gp, ip = divmod(s, 2)
                for par in range(2):
                    sp.dma_start(bias[:, 4 * s + 2 * par:4 * s + 2 * par + 2, :],
                                   line_src((8 * gp + 4 * par + 2 * ip) * BLK * LINE + BLK - 1,
                                            [[LINE - 1, P], [BLK * LINE, 2], [1, 2 * BLK]])
                                   ).then_inc(bias_in, 16)

        NG = 4 * TILES
        P_BUFS = 3
        prob = [at(f"prob{i}", R4 + i * 4096, [P, 4, 2 * BLK]) for i in range(P_BUFS)]
        probT = at("probT", R4 + 3 * 4096, [P, 4, 2, BLK])
        at_s = at_c + 352 + 2048
        stat = at("stat", at_s, [P, P_BUFS, 5, 4])
        esink = at("esink", at_s + 256, [P, P_BUFS, 4])
        o_hi = at("o_hi", R3, [P, KC, TP], F32R)
        o_lo = at("o_lo", R2, [P, KC, TP], F32R)
        s_done, s_taken, max_done = sem("s_done"), sem("s_taken"), sem("max_done")
        negm_done, logit_done, exp_done = sem("negm_done"), sem("logit_done"), sem("exp_done")
        den_done, rden_done, prob_ready = sem("den_done"), sem("rden_done"), sem("prob_ready")
        t_done, pT_ready, pv_done = sem("t_done"), sem("pT_ready"), sem("pv_done")
        o_hi_done, o_taken, vmeta_done = sem("o_hi_done"), sem("o_taken"), sem("vmeta_done")

        def block_of(n):
            b, step = divmod(n, 4)
            if b == 0:
                return (COL_M, META), (0, None, 0), BLK, BLK + META, step
            col = BLK * (b - 1)
            if b == 1:
                return (col, BLK), (COL_M, None, META), BLK - META, 2 * BLK, step
            return (col, BLK), (col - BLK, b - 2, BLK), 0, 2 * BLK, step

        def att_scores_pe(pe, n):
            (qc, nq), (pc, _, npk), k0, k1, step = block_of(n)
            gp, ip = divmod(step, 2)
            if n >= 2:
                pe.wait_ge(s_taken, n - 1)
            for par in range(2):
                rows = slice(HD * par, HD * par + HD)
                bank = 2 * (n % 2) + par
                for i in range(2):
                    lhsT = q[rows, 4 * gp + 2 * ip + i, qc:qc + nq]
                    o = ps[0:nq, bank, 2 * BLK * i:2 * BLK * i + 2 * BLK]
                    if npk == BLK:
                        last = nc.tensor.matmul(o, lhsT, kn[rows, gp, pc:pc + 2 * BLK], start=True, stop=True)
                    else:
                        if npk:
                            nc.tensor.matmul(o[:, k0:BLK], lhsT, kn[rows, gp, pc:pc + npk],
                                             start=True, stop=True)
                        last = nc.tensor.matmul(o[:, BLK:k1], lhsT, kn[rows, gp, qc:qc + nq],
                                                start=True, stop=True)
            last.then_inc(s_done, 1)

        def att_transpose_pe(pe, n):
            (qc, nq), (pc, _, npk), k0, k1, step = block_of(n)
            pe.wait_ge(prob_ready, n + 1)
            if n >= 1:
                pe.wait_ge(pT_ready, n)
            for k in range(4):
                bank = 4 + k // 2
                for part, (c0, nk) in enumerate(((k0, npk), (BLK, nq))):
                    if nk:
                        o = ps[0:nk, bank, (k % 2) * 2 * BLK + part * BLK:][:, 0:nq]
                        last = nc.tensor.transpose(o, prob[n % P_BUFS][0:nq, k, c0:c0 + nk],
                                                   ident[0:nq, 0:nq])
            last.then_inc(t_done, 1)

        def att_values_pe(pe, n):
            (qc, nq), (pc, pt, npk), k0, k1, step = block_of(n)
            b = n // 4
            gp, ip = divmod(step, 2)
            pe.wait_ge(pT_ready, n + 1)
            if n >= 2:
                pe.wait_ge(o_taken, n - 1)
            for par in range(2):
                cols = slice((2 * gp + par) * HD, (2 * gp + par) * HD + HD)
                for i in range(2):
                    k = 2 * par + i
                    o = ps[HD * par:HD * par + HD, 6 + n % 2, BLK * i:BLK * i + nq]
                    if npk:
                        v = v_tok[:, pt, cols] if pt is not None else v_meta[:, cols]
                        nc.tensor.matmul(o, v, probT[0:npk, k, 0, 0:nq], start=True, stop=False)
                    v = v_tok[:, b - 1, cols] if b else v_meta[:, cols]
                    last = nc.tensor.matmul(o, v, probT[0:nq, k, 1, 0:nq], start=npk == 0, stop=True)
            last.then_inc(pv_done, 1)

        def att_pe(pe):
            pe.wait_ge(vmeta_done, 1)
            pe.wait_ge(v_taken, 6)
            for n in range(NG + 2):
                if n >= 2:
                    att_transpose_pe(pe, n - 2)
                if n < NG:
                    att_scores_pe(pe, n)
                if n >= 2:
                    att_values_pe(pe, n - 2)

        def att_softmax_dve(dve, n):
            (qc, nq), (pc, _, npk), k0, k1, step = block_of(n)
            b3 = n % P_BUFS
            st = stat[0:nq, b3, :, :]
            dve.wait_ge(s_done, n + 1)
            if n >= P_BUFS:
                dve.wait_ge(t_done, n - P_BUFS + 1)
            src = ps[0:nq, 2 * (n % 2):2 * (n % 2) + 2, :].rearrange("p b (i s) -> p (b i) s", i=2)
            pr = prob[b3][0:nq, :, k0:k1]
            nc.vector.scalar_tensor_tensor(out=pr, in0=src[:, :, k0:k1], scalar=HD ** -0.5,
                                           in1=bias[0:nq, 4 * step:4 * step + 4, k0:k1],
                                           op0=ALU.mult, op1=ALU.add).then_inc(s_taken, 1)
            dve.wait_ge(s_taken, n + 1)
            nc.vector.tensor_reduce(st[:, 0, :], pr, AX, ALU.max).then_inc(max_done, 1)
            dve.wait_ge(max_done, n + 1)
            nc.vector.scalar_tensor_tensor(out=st[:, 1, :], in0=st[:, 0, :], scalar=-1.0,
                                           in1=nsinks[0:nq, 4 * step:4 * step + 4],
                                           op0=ALU.mult, op1=ALU.min).then_inc(negm_done, 1)
            dve.wait_ge(negm_done, n + 1)
            nc.vector.tensor_tensor(st[:, 2, :], sinks[0:nq, 4 * step:4 * step + 4], st[:, 1, :], ALU.add
                                    ).then_inc(logit_done, 1)

        def att_exp_act(act, n):
            (qc, nq), (pc, _, npk), k0, k1, step = block_of(n)
            b3 = n % P_BUFS
            st = stat[0:nq, b3, :, :]
            act.wait_ge(logit_done, n + 1)
            for k in range(4):
                pr = prob[b3][0:nq, k, k0:k1]
                nc.scalar.activation(pr, pr, ACT.Exp, bias=st[:, 1, k:k + 1], accum_out=st[:, 3, k:k + 1])
            nc.scalar.activation(esink[0:nq, b3, :], st[:, 2, :], ACT.Exp).then_inc(exp_done, 1)

        def att_den_dve(dve, n):
            nq = block_of(n)[0][1]
            b3 = n % P_BUFS
            st = stat[0:nq, b3, :, :]
            dve.wait_ge(exp_done, n + 1)
            nc.vector.tensor_tensor(st[:, 3, :], st[:, 3, :], esink[0:nq, b3, :], ALU.add).then_inc(den_done, 1)
            dve.wait_ge(den_done, n + 1)
            nc.vector.reciprocal(st[:, 4, :], st[:, 3, :]).then_inc(rden_done, 1)

        def att_scale_pool(pool, n):
            (qc, nq), (pc, _, npk), k0, k1, step = block_of(n)
            b3 = n % P_BUFS
            pool.wait_ge(rden_done, n + 1)
            pr = prob[b3][0:nq, :, k0:k1]
            nc.gpsimd.tensor_tensor(pr, pr, stat[0:nq, b3, 4, :].unsqueeze(2).to_broadcast([nq, 4, k1 - k0]),
                                    ALU.mult).then_inc(prob_ready, 1)

        def att_pT_act(act, n):
            (qc, nq), (pc, _, npk), k0, k1, step = block_of(n)
            act.wait_ge(t_done, n + 1)
            if n >= 1:
                act.wait_ge(pv_done, n)
            src = ps[:, 4:6, :].rearrange("p b (i c s) -> p (b i) c s", i=2, c=2)
            if npk == BLK:
                nc.scalar.activation(probT[:, :, :, :], src, ACT.Copy).then_inc(pT_ready, 1)
            else:
                if npk:
                    nc.scalar.activation(probT[0:npk, :, 0, 0:nq], src[0:npk, :, 0, 0:nq], ACT.Copy)
                nc.scalar.activation(probT[0:nq, :, 1, 0:nq], src[0:nq, :, 1, 0:nq], ACT.Copy
                                     ).then_inc(pT_ready, 1)

        def o_views(n):
            (qc, nq), _, _, _, step = block_of(n)
            gp, ip = divmod(step, 2)
            c = 4 * gp + 2 * ip
            src = ps[:, 6 + n % 2, 0:2 * BLK].rearrange("p (i s) -> p i s", i=2)[:, :, 0:nq]
            return src, o_hi[:, c:c + 2, qc:qc + nq], o_lo[:, c:c + 2, qc:qc + nq]

        def att_o_act(act, n):
            src, hi, lo = o_views(n)
            act.wait_ge(pv_done, n + 1)
            nc.scalar.activation(hi, src, ACT.Copy).then_inc(o_hi_done, 1)

        def att_o_dve(dve, n):
            src, hi, lo = o_views(n)
            dve.wait_ge(o_hi_done, n + 1)
            nc.vector.tensor_tensor(lo, src, hi.bitcast(F32), ALU.subtract).then_inc(o_taken, 1)

        def att_act(act):
            for n in range(NG + 2):
                if n >= 2:
                    att_pT_act(act, n - 2)
                if n < NG:
                    att_exp_act(act, n)
                if n >= 2:
                    att_o_act(act, n - 2)

        def att_dve(dve):
            dve.wait_ge(v_taken, 6)
            nc.vector.tensor_copy(v_meta[:, :], v_tok[SAMPLE:LAST, NBLK, :]).then_inc(vmeta_done, 1)
            dve.wait_ge(bias_in, 16 * 8)
            for n in range(NG + 3):
                if 1 <= n <= NG:
                    att_den_dve(dve, n - 1)
                if n < NG:
                    att_softmax_dve(dve, n)
                if n >= 3:
                    att_o_dve(dve, n - 3)

        SK = WIN + SAMPLE
        k_raw = at("k_raw", R1 + 544, [P, NB, KH * HD])
        kcT = at("kcT", R1 + 544 + 8192, [P, 2, NB, WIN])
        v_c = at("v_c", R1 + 544 + 16384, [P, NB, KH * HD])
        q_big = at("q_big", R1 + 544 + 24576, [P, 2, NB, 2 * P // NS])
        sb_new = at("sb_new", R4, [P, 4, SK])
        s_prob = at("s_prob", R4 + 2560, [P, 4, SK])
        pcT = at("pcT", R4 + 5120, [P, 4, P])
        pnT = at("pnT", R4 + 5120 + 2048, [SAMPLE, 4, P])
        s_sink = at("s_sink", R4 + 5120 + 4096, [P, 2])
        s_stat = at("s_stat", R4 + 5120 + 4096 + 32, [P, 6, 4])
        kc_in, sq_steps, sa_steps, sp_steps = sem("kc_in"), sem("sample_dve"), sem("sample_act"), sem("sample_pe")

        def sample_loads(pool):
            pool.wait_ge(out_ready, 12)
            pool.dma_start(k_raw[:, :, :], a["cache_k"][0].rearrange("b s h d -> s b (h d)")).then_inc(kc_in, 16)
            pool.dma_start(v_c[:, :, :], a["cache_v"][0].rearrange("b s h d -> s b (h d)")).then_inc(kc_in, 16)
            pool.wait_ge(line_out, 16)
            for half in range(2):
                pool.dma_start(s_bias[64 * half:64 * half + 64, :],
                               line_src(BLK - 1, [[BLK * LINE, QH], [LINE - 1, NS], [1, WIN + NS]])
                               ).then_inc(kc_in, 16)

        def sink_rows(pool):
            pool.wait_ge(prob_ready, NG)
            pool.wait_ge(t_done, NG)
            for half in range(2):
                pool.dma_start(s_sink[64 * half:64 * half + 64, 0:1],
                               bass.AP(a["attn_sinks"].tensor, 0, [[1, QH], [0, NS], [1, 1]]),
                               allow_slow_non_contiguous=True).then_inc(sbias_in, 16)

        def sample_dve(dve):
            step = [0]

            def inc(ins):
                step[0] += 1
                ins.then_inc(sq_steps, 1)
                return step[0]

            def after(k):
                dve.wait_ge(sq_steps, k)

            dve.wait_ge(out_ready, 12)
            z = inc(nc.vector.memset(q_big[:, :, :, :], 0.0))
            after(z)
            for gp in range(2):
                for par in range(2):
                    g = 2 * gp + par
                    rows = slice(HD * par, HD * par + HD)
                    dst = q_big[rows, gp, :, 16 * g:16 * g + 16].rearrange("p b (c i) -> p b c i", i=NS)
                    src = q[rows, 4 * gp:4 * gp + 4, COL_S:COL_M].rearrange("p c (b i) -> p b c i", i=NS)
                    inc(nc.vector.tensor_copy(dst, src))
            assert step[0] == 5

        def sample_dve2(dve):
            step = [5]

            def inc(ins):
                step[0] += 1
                ins.then_inc(sq_steps, 1)
                return step[0]

            def after(k):
                dve.wait_ge(sq_steps, k)

            caches_dve(dve)
            for j in range(4):
                dve.wait_ge(sp_steps, j + 1)
                dst = kcT[:, j // 2, 4 * (j % 2):4 * (j % 2) + 4, :]
                inc(nc.vector.tensor_copy(dst, ps[:, j, :].rearrange("p (b s) -> p b s", b=4)))
            dve.wait_ge(kc_in, 64)
            dve.wait_ge(t_done, NG)
            m = inc(nc.vector.memset(sb_new[:, :, WIN:SK], NEG))
            inc(nc.vector.tensor_copy(sb_new[:, :, 0:WIN],
                                      s_bias[:, 0:WIN].unsqueeze(1).to_broadcast([P, 4, WIN])))
            after(m)
            for b in range(NB):
                rows = slice(64 * (b % 2), 64 * (b % 2) + 64)
                inc(nc.vector.tensor_copy(sb_new[rows, b // 2, WIN + NS * b:WIN + NS * b + NS],
                                          s_bias[rows, WIN:WIN + NS]))
            after(step[0])
            dve.wait_ge(sp_steps, 5)
            sc = ps[:, 4:6, :].rearrange("p b (i s) -> p (b i) s", i=2)[:, :, 0:SK]
            k = inc(nc.vector.scalar_tensor_tensor(out=s_prob[:, :, :], in0=sc, scalar=HD ** -0.5,
                                                   in1=sb_new[:, :, :], op0=ALU.mult, op1=ALU.add))
            after(k)
            k = inc(nc.vector.tensor_reduce(s_stat[:, 0, :], s_prob[:, :, :], AX, ALU.max))
            after(k)
            dve.wait_ge(sbias_in, 32)
            sink4 = s_sink[:, 0:1].to_broadcast([P, 4])
            k = inc(nc.vector.tensor_tensor(s_stat[:, 0, :], s_stat[:, 0, :], sink4, ALU.max))
            after(k)
            k = inc(nc.vector.tensor_scalar(s_stat[:, 1, :], s_stat[:, 0, :], -1.0, None, ALU.mult))
            after(k)
            k = inc(nc.vector.tensor_tensor(s_stat[:, 2, :], s_stat[:, 1, :], sink4, ALU.add))
            assert k == 24, k
            dve.wait_ge(sa_steps, 1)
            k = inc(nc.vector.tensor_tensor(s_stat[:, 3, :], s_stat[:, 3, :], s_stat[:, 4, :], ALU.add))
            after(k)
            k = inc(nc.vector.reciprocal(s_stat[:, 5, :], s_stat[:, 3, :]))
            after(k)
            k = inc(nc.vector.tensor_tensor(s_prob[:, :, :], s_prob[:, :, :],
                                            s_stat[:, 5, :].unsqueeze(2).to_broadcast([P, 4, SK]), ALU.mult))
            assert k == 27, k
            dve.wait_ge(sp_steps, 6)
            k = inc(nc.vector.tensor_copy(pnT[:, :, :], ps[0:SAMPLE, 7, :].rearrange("p (t r) -> p t r", t=4)))
            assert k == 28
            dve.wait_ge(sa_steps, 3)
            for gp in range(2):
                src, hi, lo = sample_o(gp)
                inc(nc.vector.tensor_tensor(lo, src, hi.bitcast(F32), ALU.subtract))
            assert step[0] == 30

        def sample_o(gp):
            src = ps[:, 0, P * gp:P * gp + P].rearrange("p (b c i) -> p b c i", b=NB, i=NS)
            hi, lo = (o[:, 4 * gp:4 * gp + 4, COL_S:COL_M].rearrange("p c (b i) -> p b c i", i=NS)
                      for o in (o_hi, o_lo))
            return src, hi, lo

        def sample_act(act):
            act.wait_ge(sq_steps, 24)
            for t in range(4):
                nc.scalar.activation(s_prob[:, t, :], s_prob[:, t, :], ACT.Exp, bias=s_stat[:, 1, t:t + 1],
                                     accum_out=s_stat[:, 3, t:t + 1])
            nc.scalar.activation(s_stat[:, 4, :], s_stat[:, 2, :], ACT.Exp).then_inc(sa_steps, 1)
            act.wait_ge(sp_steps, 6)
            nc.scalar.activation(pcT[:, :, :], ps[:, 6, :].rearrange("p (t r) -> p t r", t=4), ACT.Copy
                                 ).then_inc(sa_steps, 1)
            act.wait_ge(sp_steps, 7)
            for gp in range(2):
                src, hi, lo = sample_o(gp)
                last = nc.scalar.activation(hi, src, ACT.Copy)
            last.then_inc(sa_steps, 1)

        def sample_pe(pe):
            pe.wait_ge(o_taken, NG)
            caches_pe(pe)
            pe.wait_ge(kc_in, 64)
            for j in range(4):
                for i in range(4):
                    b = 4 * (j % 2) + i
                    last = nc.tensor.transpose(ps[:, j, P * i:P * i + P],
                                               k_raw[:, b, P * (j // 2):P * (j // 2) + P], ident)
                last.then_inc(sp_steps, 1)
            pe.wait_ge(sq_steps, 9)
            for b in range(NB):
                o = ps[64 * (b % 2):64 * (b % 2) + 64, 4 + b // 4, 256 * (b // 2 % 2):256 * (b // 2 % 2) + SK]
                for c, ncol, keys in ((0, WIN, lambda gp: kcT[:, gp, b, :]),
                                      (WIN, SAMPLE, lambda gp: kn[:, gp, COL_S:COL_M])):
                    for gp in range(2):
                        last = nc.tensor.matmul(o[:, c:c + ncol], q_big[:, gp, b, :], keys(gp),
                                                start=gp == 0, stop=gp == 1)
            last.then_inc(sp_steps, 1)
            pe.wait_ge(sq_steps, 27)
            pe.wait_ge(cache_c, 2)
            for t in range(4):
                nc.tensor.transpose(ps[:, 6, P * t:P * t + P], s_prob[:, t, 0:WIN], ident)
                last = nc.tensor.transpose(ps[0:SAMPLE, 7, P * t:P * t + P], s_prob[:, t, WIN:SK], ident)
            last.then_inc(sp_steps, 1)
            pe.wait_ge(sq_steps, 28)
            pe.wait_ge(sa_steps, 2)
            for g in range(KH):
                gp, par = divmod(g, 2)
                for b in range(NB):
                    r = 64 * (b % 2) + 16 * g
                    o = ps[HD * par:HD * par + HD, 0, P * gp + 16 * b:P * gp + 16 * b + 16]
                    cols = slice(HD * g, HD * g + HD)
                    nc.tensor.matmul(o, v_c[:, b, cols], pcT[:, b // 2, r:r + 16], start=True, stop=False)
                    last = nc.tensor.matmul(o, v_tok[0:SAMPLE, NBLK, cols], pnT[:, b // 2, r:r + 16],
                                            start=False, stop=True)
            last.then_inc(sp_steps, 1)

        def add_x_dve(dve, n, f, x):
            dve.wait_ge(out_ready, n + 1)
            nc.vector.tensor_tensor(grp(x[:, f, :]), grp(x[:, f, :]), ps[:, out_banks(n):out_banks(n) + 3, 0:TG],
                                    ALU.add).then_inc(out_free, 1)

        def reload_x(pool):
            for f in range(KC):
                pool.dma_start(x[:, f, :], scratch["x0"][:, f, :]).then_inc(x_back, 16)

        def wo_pe(pe):
            pe.wait_ge(sq_steps, 30)
            for c in range(KC):
                pe_unit(pe, U_WO + c, N_WO + c, o_hi, o_lo)

        def project_act(act, u0, n0, m, x, h_hi):
            for c in range(KC):
                split_hi_static(act, u0 + c + AHEAD)
                act.wait_ge(out_free, n0 + c + 1)
                norm_act(act, m, c, x, h_hi)

        def project_dve(dve, u0, n0, m, x, h_hi, h_lo, back):
            for c in range(KC):
                split_lo_static(dve, u0 + c + AHEAD)
                if c >= 2:
                    norm_acc_dve(dve, m, c - 1)
                if c == 0:
                    dve.wait_ge(back, 16 * KC)
                add_x_dve(dve, n0 + c, c, x)
            norm_acc_dve(dve, m, KC - 1)
            dve.wait_ge(out_ready, n0 + KC)
            for c in range(KC):
                norm_lo_dve(dve, m, c, x, h_hi, h_lo)

        def mlp_slice_sp(sp, layer, u0, i):
            r0 = u0 // 2
            up = a["mlp_w_up"][layer].rearrange("(k p) n -> p k n", p=P)
            down = a["mlp_w_down"][layer].rearrange("(s p) n -> p s n", p=P)
            for j in range(4):
                slot = (r0 + j) % 2
                sp.wait_ge(w_lo_ready, i * 8 + (2 * (r0 + j) - 2))
                if j < 2:
                    src = up[:, :, bass.ds(i * 512 + 256 * j, 256)]
                    sp.dma_start(raw_k8[:, slot, :, :], src).then_inc(raw_in[slot], 16)
                else:
                    src = down[:, bass.ds(i * 4, 4), 512 * (j - 2):512 * (j - 2) + 512]
                    sp.dma_start(raw_k4[:, slot, :, :], src).then_inc(raw_in[slot], 16)

        def local_outs(j):
            return j + 1 if j < 4 else 2 * j - 2

        def mlp_raw_wait(u0, i, j):
            r = u0 // 2 + j // 2
            base = raw_target(u0 // 2 + (j // 2) % 2 - 2)
            return r % 2, i * 32 + (base + 16 * (j // 4 + 1))

        def mlp_split_hi(act, u0, n0, i, j):
            jj = j + AHEAD
            rslot, rwait = mlp_raw_wait(u0, i, jj)
            done = (n0 - 1, n0)[j] if j < 2 else n0 + local_outs(j - 2)
            split_hi(act, (u0 + jj) % 4, rslot, jj % 2, 4 <= jj < 8, rwait, i * 12 + done)

        def mlp_split_lo(dve, u0, i, j):
            jj = j + AHEAD
            split_lo(dve, (u0 + jj) % 4, (u0 // 2 + jj // 2) % 2, jj % 2, 4 <= jj < 8, i * 8 + (u0 + jj + 1))

        def mlp_slice_act(act, layer, u0, n0, i, prefetch=8, norm=None):
            ups = 4 * SLICES * layer
            for j in range(8):
                if j < prefetch:
                    mlp_split_hi(act, u0, n0, i, j)
                if j < 4:
                    act.wait_ge(out_free, i * 12 + (n0 + j + 1))
                    nc.scalar.activation(act_hi[:, j, :], relu[j % 2][:, :], ACT.Square).then_inc(up_done, 1)
                elif norm:
                    for o in (2 * j - 8, 2 * j - 7):
                        act.wait_ge(out_free, i * 12 + (n0 + 5 + o))
                        if o == 0:
                            act.wait_ge(act_split, i * 4 + (ups + 4))
                        norm_act(act, norm[0], o, norm[1], norm[2])

        def mlp_slice_dve(dve, layer, u0, n0, i, x, prefetch=8, norm=None):
            ups = 4 * SLICES * layer
            for j in range(8):
                if j < prefetch:
                    mlp_split_lo(dve, u0, i, j)
                if j < 4:
                    n = n0 + j
                    dve.wait_ge(out_ready, i * 12 + (n + 1))
                    nc.vector.scalar_tensor_tensor(out=grp(relu[j % 2][:, :]),
                                                   in0=ps[:, out_banks(n):out_banks(n) + 3, 0:TG], scalar=0.0,
                                                   in1=rstd[:, :, :], op0=ALU.max, op1=ALU.mult
                                                   ).then_inc(out_free, 1)
                    dve.wait_ge(out_free, i * 12 + (n + 1))
                    if j:
                        dve.wait_ge(act_split, i * 4 + (ups + j))
                    nc.vector.tensor_tensor(relu_sq[:, :], relu[j % 2][:, :], relu[j % 2][:, :], ALU.mult
                                            ).then_inc(sq_done, 1)
                    dve.wait_ge(sq_done, i * 4 + (ups + j + 1))
                    dve.wait_ge(up_done, i * 4 + (ups + j + 1))
                    nc.vector.tensor_tensor(act_lo[:, j, :], relu_sq[:, :], act_hi[:, j, :].bitcast(F32),
                                            ALU.subtract).then_inc(act_split, 1)
                else:
                    for o in (2 * j - 8, 2 * j - 7):
                        n = n0 + 4 + o
                        dve.wait_ge(out_ready, i * 12 + (n + 1))
                        dve.wait_ge(out_free, i * 12 + (n0 + o - 7))
                        nc.vector.tensor_tensor(grp(x[:, o, :]), grp(x[:, o, :]),
                                                ps[:, out_banks(n):out_banks(n) + 3, 0:TG], ALU.add
                                                ).then_inc(out_free, 1)
                        if norm and o:
                            if o >= 2:
                                norm_acc_dve(dve, norm[0], o - 1)
                            norm_lo_dve(dve, norm[0], o - 1, *norm[1:])
            if norm:
                norm_acc_dve(dve, norm[0], KC - 1)
                norm_lo_dve(dve, norm[0], KC - 1, *norm[1:])

        def mlp_slice_pe(pe, layer, u0, n0, i, h_hi, h_lo):
            ups = 4 * SLICES * layer
            for j in range(8):
                pe.wait_ge(w_lo_ready, i * 8 + (u0 + j + 1))
                slot = (u0 + j) % 4
                deep, hi, lo = (8, h_hi, h_lo) if j < 4 else (4, act_hi, act_lo)
                for c in range(1 if j < 4 else 2):
                    o = j if j < 4 else 4 + 2 * (j - 4) + c
                    pe.wait_ge(out_free, i * 12 + (n0 + o - 1))
                    for k in range(deep):
                        if o == 0:
                            pe.wait_ge(norm_hi, KC * (2 * layer + 1) + k + 1)
                        if o == 4:
                            pe.wait_ge(act_split, i * 4 + (ups + k + 1))
                        pass_hi(slot, k, deep, slice(P * c, P * c + P), out_banks(n0 + o), hi, k == 0)
                    for k in range(deep):
                        if o == 0:
                            pe.wait_ge(norm_lo, KC * (2 * layer + 1) + k + 1)
                        last = pass_lo(slot, k, deep, slice(P * c, P * c + P), out_banks(n0 + o), lo, k == deep - 1)
                    last.then_inc(out_ready, 1)

        ROWB = 4320
        t_i, t_f, b_row, jump, m_rel, m_abs, m_prev, keep = (
            at(nm, R0 + i * ROWB, [MH, TP]) for i, nm in enumerate(
                ["t_i", "t_f", "b_row", "jump", "m_rel", "m_abs", "m_prev", "keep"]))
        u_s = at("u_s", R0 + 8 * ROWB, [MH, SAMPLE])
        m0 = at("m0", R0 + 8 * ROWB + 128, [MH, NB])
        wg_raw = at("wg_raw", R3, [P, KC, 100])
        wg_hi = at("wg_hi", R3 + 3200, [P, KC, 100], F32R)
        wg_lo = at("wg_lo", R3 + 6400, [P, KC, 100], F32R)
        rows_u = at("rows_u", R4, [P, TP])
        rows_m = at("rows_m", R4 + BUF, [P, TP])
        stage = at("stage", R4 + 3 * BUF, [P, TP])
        selw = at("selw", R4 + 2 * BUF, [P, 8 * P + MH])
        v_m = at("v_m", R4 + 3 * BUF, [META, MH, VH])
        qk = at("qk", R3, [P, KC, TP])
        v = at("v", R0, [P, TILES, MH, VH])
        c0 = at("c0", R0, [P, NB, MH, VH])
        og = at("og", R1, [P, KC, TP])
        y_hi = at("y_hi", R3, [P, KC, TP], F32R)
        y_lo = at("y_lo", R1, [P, KC, TP], F32R)
        x2 = at("x2", R2, [P, KC, TP])
        h_hi2 = at("h_hi2", R0, [P, KC, TP], F32R)
        h_lo2 = at("h_lo2", R1, [P, KC, TP], F32R)
        names = ["rr", "decay", "sw", "kts", "qs", "e_sb", "dd", "zr"]
        rr, decay, sw, kts, qs, e_sb, dd, zr = (at(nm, R2 + 2048 * i, [P, MH, P]) for i, nm in enumerate(names))
        nsq = at("nsq", R2 + 16384, [P, MH, 2, P])
        numr = at("numr", R2 + 16384 + 4096, [P, MH, 2, P])
        cst_ = at("c_state", R2 + 16384 + 8192, [P, MH, VH])
        a_sb = at("a_sb", R2 + 16384 + 8192 + 4128, [P, MH])
        a_s = at("a_s", R2 + 16384 + 8192 + 4128 + 32, [P, MH, SAMPLE])
        at_g = at_s + 256 + 64
        bgate = at("bgate", at_g, [MH, 2])
        bg15 = at("bg15", at_g + 32, [MH, 2])
        causal = cst[:, slice(*CONST_AT["causal"])]
        own_causal = cst[:, slice(*CONST_AT["own_causal"])]
        small += [(bgate[:, :], a["mlstm_b_gate"][0].rearrange("(g h) -> h g", g=2))]

        wg_zero, wg_in, wg_split_hi, wg_split = sem("wg_zero"), sem("wg_in"), sem("wg_split_hi"), sem("wg_split")
        keep_in, gate_dve, gate_act = sem("keep_in"), sem("gate_dve"), sem("gate_act")
        vt2_ready, v2_taken, og_done, og_out, og_in = (sem(s) for s in
            ("vt2_ready", "v2_taken", "og_done", "og_out", "og_in"))
        o_sig = sem("o_sig")
        v_ones, sel_in, vm_done = sem("v_ones"), sem("sel_in"), sem("vm_done")
        (rr_ready, kT_ready, st_ready, d_ready, decay_ready, sw_ready, kts_ready, bc_ready, qs_ready, e_ready,
         num_ready, dd_step, nsq_ready, ss_ready, z_ready, ln_z, r_ready, numr_ready, y_ready, yhi_ready, ylo_ready,
         cup_ready, c_new) = (sem(s) for s in (
             "rr_ready", "kT_ready", "st_ready", "d_ready", "decay_ready", "sw_ready", "kts_ready", "bc_ready",
             "qs_ready", "e_ready", "num_ready", "dd_step", "nsq_ready", "ss_ready", "z_ready", "ln_z", "r_ready",
             "numr_ready", "y_ready", "yhi_ready", "ylo_ready", "cup_ready", "c_new"))
        abs_ready = sem("abs_ready")
        c0_in, sm_pe, sm_dve, sm_act, c0_out = (sem(s) for s in ("c0_in", "sm_pe", "sm_dve", "sm_act", "c0_out"))
        x2_back = sem("x2_back")

        def gates_pool(pool):
            pool.wait_ge(wg_zero, 1)
            w = a["mlstm_w_gate"][0].rearrange("(k p) n -> p k n", p=P)
            pool.dma_start(wg_raw[:, :, 0:MH], w[:, :, 0:MH]).then_inc(wg_in, 16)
            pool.dma_start(wg_raw[:, :, 96:96 + MH], w[:, :, MH:2 * MH]).then_inc(wg_in, 16)
            pool.wait_ge(out_free, N_IN)
            pool.dma_start(scratch["x1"], x[:, :, :]).then_inc(x1_saved, 16)
            pool.wait_ge(x1_saved, 16)
            pool.wait_ge(norm_lo, 3 * KC)
            pool.wait_ge(norm_sq, 3 * KC)
            pool.dma_start(keep[:, :], a["keep"]).then_inc(keep_in, 16)
            pool.dma_start(m0[:, :], a["state_m"][0].rearrange("b h -> h b"),
                           allow_slow_non_contiguous=True).then_inc(keep_in, 16)

        def gates_pe(pe):
            n = N_IN
            pe.wait_ge(wg_split, 1)
            pe.wait_ge(out_free, n - 1)
            for k in range(KC):
                pe.wait_ge(norm_lo, 2 * KC + k + 1)
                if k in (4, 5, 6):
                    norm_pe(pe, 2, k - 4)
                for g in range(3):
                    o = ps[0:100, out_banks(n) + g, 0:TG]
                    c = slice(g * TG, g * TG + TG)
                    nc.tensor.matmul(o, wg_hi[:, k, :], h_hi[:, k, c], start=k == 0, stop=False)
                    nc.tensor.matmul(o, wg_hi[:, k, :], h_lo[:, k, c], start=False, stop=False)
                    last = nc.tensor.matmul(o, wg_lo[:, k, :], h_hi[:, k, c], start=False, stop=k == KC - 1)
            last.then_inc(out_ready, 1)

        def gates_act1(act):
            act.wait_ge(gate_dve, 1)
            act.wait_ge(out_free, N_IN + 1)
            for i, t in enumerate((t_i, t_f)):
                last = nc.scalar.activation(t[:, :], t[:, :], ACT.Tanh, scale=1.0 / CAP, bias=bg15[:, i:i + 1])
            last.then_inc(gate_act, 1)
            act.preload_act_table_set("natural_log_exp_and_others")
            act.wait_ge(gate_act, 1)
            nc.scalar.activation(t_f[:, :], t_f[:, :], ACT.Exp, scale=-CAP).then_inc(gate_act, 1)
            act.wait_ge(gate_act, 2)
            nc.scalar.activation(t_f[:, :], t_f[:, :], ACT.Ln, bias=1.0).then_inc(gate_act, 1)

        def gates_dve(dve):
            dve.wait_ge(out_ready, N_IN + 1)
            dve.wait_ge(norm_rstd, 3)
            dve.wait_ge(x1_saved, 16)
            dve.wait_ge(norm_sq, 3 * KC)
            nc.vector.tensor_tensor(grp(t_i[:, :]), ps[0:MH, out_banks(N_IN):out_banks(N_IN) + 3, 0:TG],
                                    rstd[0:MH, :, :], ALU.mult).then_inc(gate_dve, 1)
            nc.vector.tensor_tensor(grp(t_f[:, :]), ps[96:96 + MH, out_banks(N_IN):out_banks(N_IN) + 3, 0:TG],
                                    rstd[96:96 + MH, :, :], ALU.mult).then_inc(out_free, 1)

        def gates_dve2(dve):
            step = [1]

            def do(ins):
                step[0] += 1
                ins.then_inc(gate_dve, 1)
                dve.wait_ge(gate_dve, step[0])

            dve.wait_ge(norm_summed, 9)
            do(nc.vector.memset(rows_u[:, :], 0.0))
            do(nc.vector.memset(rows_m[:, :], 0.0))
            do(nc.vector.memset(rows_u[32:32 + MH, :], 1.0))
            do(nc.vector.memset(rows_m[0:MH, :], 1.0))
            dve.wait_ge(x1_saved, 16)
            do(nc.vector.memset(jump[:, :], 0.0))
            do(nc.vector.memset(m_prev[:, COL_M:T], 0.0))
            dve.wait_ge(keep_in, 32)
            dve.wait_ge(gate_act, 3)
            do(nc.vector.tensor_tensor_scan(b_row[:, 0:T], keep[:, 0:T], t_f[:, 0:T], 0.0, ALU.mult, ALU.subtract))
            u = rows_u[0:MH, 0:T]
            do(nc.vector.scalar_tensor_tensor(out=u, in0=t_i[:, 0:T], scalar=CAP, in1=b_row[:, 0:T],
                                              op0=ALU.mult, op1=ALU.subtract))
            do(nc.vector.tensor_copy(jump[:, BLK:SEQ:BLK], b_row[:, BLK - 1:SEQ - 1:BLK]))
            do(nc.vector.tensor_copy(jump[:, 0:1], b_row[:, T - 1:T]))
            do(nc.vector.memset(jump[:, COL_S:COL_M:NS], NEG))
            do(nc.vector.tensor_copy(u_s[:, :], rows_u[0:MH, COL_S:COL_M]))
            do(nc.vector.tensor_tensor(u_s[:, 0:SAMPLE:NS], u_s[:, 0:SAMPLE:NS], m0[:, :], ALU.max))
            do(nc.vector.tensor_tensor_scan(m_rel[:, COL_M:T], jump[:, COL_M:T], rows_u[0:MH, COL_M:T], 0.0,
                                            ALU.add, ALU.max))
            do(nc.vector.tensor_tensor_scan(m_rel[:, 0:SEQ], jump[:, 0:SEQ], rows_u[0:MH, 0:SEQ],
                                            m_rel[:, T - 1:T], ALU.add, ALU.max))
            do(nc.vector.tensor_tensor_scan(m_rel[:, COL_S:COL_M], jump[:, COL_S:COL_M], u_s[:, :], 0.0,
                                            ALU.add, ALU.max))
            do(nc.vector.tensor_tensor(m_abs[:, 0:T], m_rel[:, 0:T], b_row[:, 0:T], ALU.add))
            do(nc.vector.tensor_copy(m_prev[:, 0:BLK], m_abs[:, T - 1:T].to_broadcast([MH, BLK])))
            do(nc.vector.tensor_copy(m_prev[:, BLK:SEQ].rearrange("p (c n) -> p c n", n=BLK),
                                     m_abs[:, BLK - 1:SEQ - 1:BLK].unsqueeze(2).to_broadcast([MH, NBLK - 1, BLK])))
            do(nc.vector.tensor_copy(m_prev[:, COL_S:COL_M].rearrange("p (b n) -> p b n", n=NS),
                                     m0[:, :].unsqueeze(2).to_broadcast([MH, NB, NS])))
            do(nc.vector.tensor_tensor(m_prev[:, 0:T], m_prev[:, 0:T], m_rel[:, 0:T], ALU.subtract))
            do(nc.vector.tensor_scalar(rows_m[32:32 + MH, 0:T], m_rel[:, 0:T], -1.0, None, ALU.mult))
            return step[0]
        GATE_STEPS = 23

        def gates_act2(act):
            act.wait_ge(gate_dve, GATE_STEPS)
            nc.scalar.activation(rows_m[64:64 + MH, 0:T], m_prev[:, 0:T], ACT.Exp)
            nc.scalar.activation(rows_m[96:96 + MH, 0:T], m_abs[:, 0:T], ACT.Exp, scale=-1.0).then_inc(gate_act, 1)

        def gates_out(pool):
            pool.wait_ge(gate_dve, GATE_STEPS)
            pool.dma_start(out[8][0].rearrange("b h -> h b"), m_abs[:, SEQ - 1:SEQ],
                           allow_slow_non_contiguous=True).then_inc(stored, 16)
            pool.dma_start(out[11][0].rearrange("b h -> h b"), m_abs[:, COL_S + NS - 1:COL_M:NS],
                           allow_slow_non_contiguous=True).then_inc(stored, 16)

        def in_side_pe(pe, vc, g):
            s = 3 * vc + g
            if s >= 2:
                pe.wait_ge(v2_taken, s - 1)
            pe.wait_ge(out_free, N_IN + 1 + 8 + vc + 1)
            for t in range(4 * g, min(4 * g + 4, TILES)):
                n = x_rows(t)
                last = nc.tensor.transpose(ps[0:n, side_bank(s), (t % 4) * P:(t % 4) * P + P],
                                           stage[:, t * P:t * P + n], ident)
            last.then_inc(vt2_ready, 1)

        def in_pe(pe):
            for c in range(24):
                sides = (lambda g, c=c: in_side_pe(pe, c - 9, g)) if 9 <= c < 17 else None
                pe_unit(pe, U_IN + c, N_IN + 1 + c, h_hi, h_lo, sides)

        def in_side_dve(dve, vc):
            if vc == 0:
                dve.wait_ge(gate_act, 4)
                dve.wait_ge(stored, 16 * 22)
                nc.vector.memset(v[:, :, :, DV:VH], 1.0).then_inc(v_ones, 1)
            for g in range(3):
                dve.wait_ge(vt2_ready, 3 * vc + g + 1)
                n, tiles = (P, 4) if g < 2 else (LAST, 1)
                nc.vector.tensor_copy(
                    v[0:n, 4 * g:4 * g + tiles, vc // 2, P * (vc % 2):P * (vc % 2) + P],
                    ps[0:n, side_bank(3 * vc + g), :].rearrange("p (t n) -> p t n", t=4)[:, 0:tiles, :]
                ).then_inc(v2_taken, 1)

        def in_act(act):
            for c in range(24):
                split_hi_static(act, U_IN + c + AHEAD)
                if c == 0:
                    gates_act1(act)
                if c == 1:
                    gates_act2(act)
                if c >= 16:
                    act.wait_ge(out_free, N_IN + c + 2)
                    nc.scalar.activation(stage[:, :], stage[:, :], ACT.Sigmoid).then_inc(o_sig, 1)

        def in_dve(dve):
            for c in range(24):
                n = N_IN + 1 + c
                split_lo_static(dve, U_IN + c + AHEAD)
                if 9 <= c < 17:
                    in_side_dve(dve, c - 9)
                dve.wait_ge(out_ready, n + 1)
                if c > 16:
                    dve.wait_ge(og_out, 16 * (c - 16))
                if c < 8:
                    times_rstd(grp(qk[:, c, :]), n, 1.0 if c < MH else DK ** -0.5)
                else:
                    times_rstd(grp(stage[:, :]), n)
                if c == 0:
                    got = gates_dve2(dve)
                    assert got == GATE_STEPS, got
                if c >= 16:
                    oc = c - 16
                    dve.wait_ge(o_sig, oc + 1)
                    nc.vector.tensor_scalar(stage[:, :], stage[:, :], gains[:, 4, oc:oc + 1], None, ALU.mult
                                            ).then_inc(og_done, 1)

        def og_pool(pool):
            for oc in range(KC):
                pool.wait_ge(og_done, oc + 1)
                if oc:
                    pool.wait_ge(og_out, 16 * oc)
                pool.dma_start(scratch["og"][:, oc, :], stage[:, :]).then_inc(og_out, 16)
            pool.wait_ge(og_out, 16 * KC)
            pool.dma_start(selw[:, :], a["select"]).then_inc(sel_in, 16)
            pool.wait_ge(out_ready, N_OUT)
            for f in range(KC):
                pool.dma_start(og[:, f, :], scratch["og"][:, f, :]).then_inc(og_in, 16)

        def chunk_of(c):
            return (COL_M, META) if c == 0 else (BLK * (c - 1), BLK)

        def hview(bank, n, rows=P):
            return ps[0:rows, bank, 0:MH * n].rearrange("p (h n) -> p h n", h=MH)

        CB = (0, 1, 3, 4)

        def chunk_pe(pe, c):
            col, n = chunk_of(c)
            cs = slice(col, col + n)
            vals = (lambda h, k0, k1: v_m[:, h, k0:k1]) if c == 0 else (lambda h, k0, k1: v[:, c - 1, h, k0:k1])
            if c:
                pe.wait_ge(c_new, 4 * c)
            for h in range(MH):
                last = nc.tensor.transpose(ps[0:n, 0, P * h:P * h + P], qk[:, MH + h, cs], ident)
            last.then_inc(kT_ready, 1)
            for h in range(MH):
                last = nc.tensor.matmul(ps[0:n, 1, n * h:n * h + n], qk[:, MH + h, cs], qk[:, h, cs],
                                        start=True, stop=True)
            last.then_inc(st_ready, 1)
            if c:
                pe.wait_ge(z_ready, c)
            pe.wait_ge(rr_ready, c + 1)
            nc.tensor.matmul(ps[0:n, 2, 0:MH * n], ident[0:n, 0:n],
                             causal[0:n, 0:n].unsqueeze(1).to_broadcast([n, MH, n]), start=True, stop=False)
            for h in range(MH):
                last = nc.tensor.matmul(ps[0:n, 2, n * h:n * h + n], rows_u[0:64, cs], rr[0:64, h, 0:n],
                                        start=False, stop=h == MH - 1)
            last.then_inc(d_ready, 1)
            for w in range(2):
                for h in range(MH):
                    last = nc.tensor.matmul(ps[:, 3 + w, n * h:n * h + n], selw[:, P * (MH * w + h):][:, 0:P],
                                            rows_m[:, cs], start=True, stop=True)
            last.then_inc(bc_ready, 1)
            pe.wait_ge(sw_ready, c + 1)
            if c:
                pe.wait_ge(numr_ready, c)
                pe.wait_ge(dd_step, 2 * c)
                pe.wait_ge(qs_ready, c + 1)
            for h in range(MH):
                for half in range(2):
                    o = ps[:, 5 + h // 2, (2 * (h % 2) + half) * n:][:, 0:n]
                    nc.tensor.matmul(o, vals(h, P * half, P * half + P), sw[0:n, h, 0:n],
                                     start=True, stop=c == 0)
                    if c:
                        nc.tensor.matmul(o, cst_[:, h, P * half:P * half + P], qs[:, h, 0:n],
                                         start=False, stop=True)
            if n == BLK:
                nc.tensor.matmul(ps[:, 7, :], ones[0:n, :], sw[0:n, :, :].rearrange("p h n -> p (h n)"),
                                 start=True, stop=False)
                for h in range(MH):
                    last = nc.tensor.matmul(ps[:, 7, n * h:n * h + n], cst_[:, h, DV:VH].to_broadcast([P, P]),
                                            qs[:, h, :], start=False, stop=h == MH - 1)
            else:
                last = nc.tensor.matmul(ps[:, 7, 0:MH * n], ones[0:n, :], sw[0:n, :, 0:n], start=True, stop=True)
            last.then_inc(num_ready, 1)
            pe.wait_ge(kts_ready, c + 1)
            pe.wait_ge(qs_ready, c + 1)
            pe.wait_ge(e_ready, c + 1)
            for h in range(MH):
                nc.tensor.matmul(ps[:, CB[h], 0:VH], kts[0:n, h, :], vals(h, 0, VH), start=True, stop=True
                                 ).then_inc(cup_ready, 1)
            pe.wait_ge(nsq_ready, c + 1)
            for half in range(2):
                last = nc.tensor.matmul(ps[:, 2, 0:MH * n], ones, nsq[:, :, half, 0:n], start=half == 0,
                                        stop=half == 1)
            last.then_inc(ss_ready, 1)

        def num_banks(bank, n):
            return ps[:, bank, 0:4 * n].rearrange("p (h c n) -> p h c n", h=2, c=2)

        def rr_dve(dve, c):
            col, n = chunk_of(c)
            if c:
                dve.wait_ge(d_ready, c)
            nc.vector.tensor_tensor(rr[0:64, :, 0:n],
                                    rows_m[0:64, col:col + n].unsqueeze(1).to_broadcast([64, MH, n]),
                                    selw[0:64, 8 * P:8 * P + MH].unsqueeze(2).to_broadcast([64, MH, n]),
                                    ALU.mult).then_inc(rr_ready, 1)

        def chunk_dve(dve, c):
            col, n = chunk_of(c)
            cs = slice(col, col + n)
            if c == 0:
                rr_dve(dve, 0)
            dve.wait_ge(st_ready, c + 1)
            dve.wait_ge(decay_ready, c + 1)
            if c:
                dve.wait_ge(num_ready, c)
                dve.wait_ge(cup_ready, 4 * c)
            nc.vector.tensor_tensor(sw[0:n, :, 0:n], hview(1, n, n), decay[0:n, :, 0:n], ALU.mult
                                    ).then_inc(sw_ready, 1)
            dve.wait_ge(bc_ready, c + 1)
            dve.wait_ge(c_new, 4 * c)
            nc.vector.tensor_copy(a_sb[:, :], hview(3, n)[:, :, n - 1])
            nc.vector.tensor_tensor(qs[:, :, 0:n], qk[:, 0:MH, cs], hview(3, n), ALU.mult).then_inc(qs_ready, 1)
            nc.vector.tensor_tensor(kts[0:n, :, :], hview(0, P, n),
                                    decay[0:n, :, n - 1:n].to_broadcast([n, MH, P]), ALU.mult
                                    ).then_inc(kts_ready, 1)
            if c < NBLK:
                rr_dve(dve, c + 1)
            dve.wait_ge(qs_ready, c + 1)
            for h in range(MH):
                dve.wait_ge(cup_ready, 4 * c + h + 1)
                if c == 0:
                    ins = nc.vector.tensor_copy(cst_[:, h, :], ps[:, CB[h], 0:VH])
                else:
                    dve.wait_ge(c_new, 4 * c - 3 + h)
                    ins = nc.vector.scalar_tensor_tensor(out=cst_[:, h, :], in0=cst_[:, h, :],
                                                         scalar=a_sb[:, h:h + 1], in1=ps[:, CB[h], 0:VH],
                                                         op0=ALU.mult, op1=ALU.add)
                ins.then_inc(c_new, 1)
            dve.wait_ge(e_ready, c + 1)
            dve.wait_ge(abs_ready, c + 1)
            nc.vector.tensor_tensor(dd[:, :, 0:n], dd[:, :, 0:n], e_sb[:, :, 0:n], ALU.max).then_inc(dd_step, 1)
            dve.wait_ge(dd_step, 2 * c + 1)
            nc.vector.tensor_tensor(dd[:, :, 0:n], dd[:, :, 0:n], dd[:, :, 0:n], ALU.mult).then_inc(dd_step, 1)
            dve.wait_ge(dd_step, 2 * c + 2)
            dve.wait_ge(ss_ready, c + 1)
            if c:
                dve.wait_ge(numr_ready, c)
            nc.vector.scalar_tensor_tensor(out=zr[:, :, 0:n], in0=dd[:, :, 0:n], scalar=EPS,
                                           in1=hview(2, n), op0=ALU.mult, op1=ALU.add).then_inc(z_ready, 1)
            dve.wait_ge(r_ready, c + 1)
            if c:
                dve.wait_ge(ylo_ready, c)
            for b in range(2):
                last = nc.vector.tensor_tensor(
                    numr[:, 2 * b:2 * b + 2, :, 0:n], num_banks(5 + b, n),
                    zr[:, 2 * b:2 * b + 2, 0:n].unsqueeze(2).to_broadcast([P, 2, 2, n]), ALU.mult)
            last.then_inc(numr_ready, 1)
            dve.wait_ge(numr_ready, c + 1)
            nf = numr[:, :, :, 0:n].rearrange("p h c n -> p (h c) n")
            if c == 0:
                dve.wait_ge(og_in, 16 * KC)
            nc.vector.tensor_tensor(nf, nf, og[:, :, cs], ALU.mult).then_inc(y_ready, 1)
            dve.wait_ge(yhi_ready, c + 1)
            nc.vector.tensor_tensor(y_lo[:, :, cs], nf, y_hi[:, :, cs].bitcast(F32), ALU.subtract
                                    ).then_inc(ylo_ready, 1)

        def chunk_act(act, c):
            col, n = chunk_of(c)
            cs = slice(col, col + n)
            act.wait_ge(d_ready, c + 1)
            if c:
                act.wait_ge(kts_ready, c)
            nc.scalar.activation(decay[0:n, :, 0:n], hview(2, n, n), ACT.Exp).then_inc(decay_ready, 1)
            act.wait_ge(bc_ready, c + 1)
            if c:
                act.wait_ge(dd_step, 2 * c)
            nc.scalar.activation(e_sb[:, :, 0:n], hview(4, n), ACT.Copy).then_inc(e_ready, 1)
            act.wait_ge(num_ready, c + 1)
            if c:
                act.wait_ge(ss_ready, c)
            if c:
                act.wait_ge(z_ready, c)
            nc.scalar.activation(dd[:, :, 0:n], hview(7, n), ACT.Abs).then_inc(abs_ready, 1)
            for b in range(2):
                last = nc.scalar.activation(nsq[:, 2 * b:2 * b + 2, :, 0:n], num_banks(5 + b, n), ACT.Square,
                                            scale=DV ** -0.5)
            last.then_inc(nsq_ready, 1)
            act.wait_ge(z_ready, c + 1)
            nc.scalar.activation(zr[:, :, 0:n], zr[:, :, 0:n], ACT.Ln).then_inc(ln_z, 1)
            act.wait_ge(ln_z, c + 1)
            nc.scalar.activation(zr[:, :, 0:n], zr[:, :, 0:n], ACT.Exp, scale=-0.5).then_inc(r_ready, 1)
            act.wait_ge(y_ready, c + 1)
            nc.scalar.activation(y_hi[:, :, cs], numr[:, :, :, 0:n].rearrange("p h c n -> p (h c) n"), ACT.Copy
                                 ).then_inc(yhi_ready, 1)

        def c0_pool(pool):
            for b in range(NB):
                pool.wait_ge(cup_ready, 4 * (b + 2))
                pool.dma_start(c0[:, b, :, 0:DV], a["state_C"][0, b].rearrange("h k v -> k h v")).then_inc(c0_in, 16)
                pool.dma_start(c0[:, b, :, DV:VH], a["state_n"][0, b].rearrange("h k -> k h").unsqueeze(2),
                               allow_slow_non_contiguous=True).then_inc(c0_in, 16)
            pool.wait_ge(c_new, 4 * TILES)
            pool.dma_start(out[6][0, 0].rearrange("h k v -> k h v"), cst_[:, :, 0:DV]).then_inc(stored, 16)
            pool.dma_start(out[7][0, 0].rearrange("h k -> k h").unsqueeze(2), cst_[:, :, DV:VH],
                           allow_slow_non_contiguous=True).then_inc(stored, 16)

        SC = slice(COL_S, COL_M)
        SN = SAMPLE

        def s_pe(pe):
            pe.wait_ge(c_new, 4 * TILES)
            pe.wait_ge(z_ready, TILES)
            for h in range(MH):
                last = nc.tensor.transpose(ps[0:SN, 0, P * h:P * h + P], qk[:, MH + h, SC], ident)
            for h in range(MH):
                last = nc.tensor.matmul(ps[0:SN, 1, SN * h:SN * h + SN], qk[:, MH + h, SC], qk[:, h, SC],
                                        start=True, stop=True)
            pe.wait_ge(sm_dve, 1)
            nc.tensor.matmul(ps[0:SN, 2, 0:MH * SN], ident[0:SN, 0:SN],
                             own_causal[0:SN, :].unsqueeze(1).to_broadcast([SN, MH, SN]), start=True, stop=False)
            for h in range(MH):
                last = nc.tensor.matmul(ps[0:SN, 2, SN * h:SN * h + SN], rows_u[0:64, SC], rr[0:64, h, 0:SN],
                                        start=False, stop=h == MH - 1)
            last.then_inc(sm_pe, 1)
            for w in range(2):
                for h in range(MH):
                    last = nc.tensor.matmul(ps[:, 3 + w, SN * h:SN * h + SN], selw[:, P * (MH * w + h):][:, 0:P],
                                            rows_m[:, SC], start=True, stop=True)
            last.then_inc(sm_pe, 1)
            pe.wait_ge(sm_dve, 3)
            pe.wait_ge(numr_ready, TILES)
            pe.wait_ge(dd_step, 2 * TILES)
            pe.wait_ge(c0_in, 32 * NB)
            for h in range(MH):
                for half in range(2):
                    f = 2 * h + half
                    o = ps[:, 5, SN * f:SN * f + SN]
                    nc.tensor.matmul(o, v[0:SN, NBLK, h, P * half:P * half + P], sw[0:SN, h, 0:SN],
                                     start=True, stop=False)
                    for b in range(NB):
                        nc.tensor.matmul(o[:, NS * b:NS * b + NS], c0[:, b, h, P * half:P * half + P],
                                         qs[:, h, NS * b:NS * b + NS], start=False, stop=b == NB - 1)
            nc.tensor.matmul(ps[:, 7, 0:MH * SN], ones[0:SN, :], sw[0:SN, :, 0:SN], start=True, stop=False)
            for h in range(MH):
                for b in range(NB):
                    c = SN * h + NS * b
                    last = nc.tensor.matmul(ps[:, 7, c:c + NS], c0[:, b, h, DV:VH].to_broadcast([P, P]),
                                            qs[:, h, NS * b:NS * b + NS], start=False,
                                            stop=h == MH - 1 and b == NB - 1)
            last.then_inc(sm_pe, 1)
            pe.wait_ge(sm_act, 2)
            pe.wait_ge(sm_dve, 4)
            for b in range(NB):
                pe.wait_ge(sm_kb, b + 1)
                if b:
                    pe.wait_ge(sm_c, 4 * b)
                for h in range(MH):
                    nc.tensor.matmul(ps[:, CB[h], 0:VH], kbs[b % 2][:, h, :], v[0:SN, NBLK, h, :],
                                     start=True, stop=True).then_inc(sm_cup, 1)
            pe.wait_ge(sm_act, 3)
            for half in range(2):
                last = nc.tensor.matmul(ps[:, 2, 0:MH * SN], ones, nsq[:, :, half, 0:SN], start=half == 0,
                                        stop=half == 1)
            last.then_inc(sm_pe, 1)

        kbs = [at(f"kb{i}", R2 + 16384 + 8192 + 4128 + 32 + 512 + 2048 * i, [SAMPLE, MH, P]) for i in range(2)]
        kt_s = at("kt_s", R2 + 2048 * 3, [SAMPLE, MH, P])
        sm_kb, sm_cup, sm_c = sem("sm_kb"), sem("sm_cup"), sem("sm_c")

        def s_dve(dve):
            step = [0]

            def inc(ins):
                step[0] += 1
                ins.then_inc(sm_dve, 1)
                return step[0]

            inc(nc.vector.tensor_tensor(rr[0:64, :, 0:SN],
                                        rows_m[0:64, SC].unsqueeze(1).to_broadcast([64, MH, SN]),
                                        selw[0:64, 8 * P:8 * P + MH].unsqueeze(2).to_broadcast([64, MH, SN]),
                                        ALU.mult))
            dve.wait_ge(sm_pe, 1)
            dve.wait_ge(sm_act, 1)
            inc(nc.vector.tensor_tensor(sw[0:SN, :, 0:SN], hview(1, SN, SN), decay[0:SN, :, 0:SN], ALU.mult))
            dve.wait_ge(sm_pe, 2)
            nc.vector.tensor_copy(a_s[:, :, :], hview(3, SN))
            inc(nc.vector.tensor_tensor(qs[:, :, 0:SN], qk[:, 0:MH, SC], hview(3, SN), ALU.mult))
            inc(nc.vector.tensor_copy(kt_s[:, :, :], hview(0, P, SN)))
            dve.wait_ge(sm_dve, 4)
            dve.wait_ge(sm_act, 2)
            for b in range(NB + 1):
                if b < NB:
                    if b >= 2:
                        dve.wait_ge(sm_cup, 4 * (b - 1))
                    nc.vector.tensor_tensor(kbs[b % 2][:, :, :], kt_s[:, :, :],
                                            decay[0:SN, :, NS * b + NS - 1:NS * b + NS].to_broadcast([SN, MH, P]),
                                            ALU.mult).then_inc(sm_kb, 1)
                if b:
                    for h in range(MH):
                        dve.wait_ge(sm_cup, 4 * (b - 1) + h + 1)
                        nc.vector.scalar_tensor_tensor(out=c0[:, b - 1, h, :], in0=c0[:, b - 1, h, :],
                                                       scalar=a_s[:, h, NS * b - 1:NS * b],
                                                       in1=ps[:, CB[h], 0:VH], op0=ALU.mult, op1=ALU.add
                                                       ).then_inc(sm_c, 1)
            dve.wait_ge(abs_ready, TILES + 1)
            inc(nc.vector.tensor_tensor(dd[:, :, 0:SN], dd[:, :, 0:SN], e_sb[:, :, 0:SN], ALU.max))
            dve.wait_ge(sm_dve, 5)
            inc(nc.vector.reciprocal(zr[:, :, 0:SN], dd[:, :, 0:SN]))
            dve.wait_ge(sm_dve, 6)
            num = ps[:, 5, 0:8 * SN].rearrange("p (h c n) -> p h c n", h=MH, c=2)
            inc(nc.vector.tensor_tensor(numr[:, :, :, 0:SN], num,
                                        zr[:, :, 0:SN].unsqueeze(2).to_broadcast([P, MH, 2, SN]), ALU.mult))
            dve.wait_ge(sm_act, 4)
            inc(nc.vector.tensor_tensor(numr[:, :, :, 0:SN], numr[:, :, :, 0:SN],
                                        zr[:, :, 0:SN].unsqueeze(2).to_broadcast([P, MH, 2, SN]), ALU.mult))
            dve.wait_ge(sm_dve, 8)
            nf = numr[:, :, :, 0:SN].rearrange("p h c n -> p (h c) n")
            inc(nc.vector.tensor_tensor(nf, nf, og[:, :, SC], ALU.mult))
            dve.wait_ge(sm_act, 5)
            inc(nc.vector.tensor_tensor(y_lo[:, :, SC], nf, y_hi[:, :, SC].bitcast(F32), ALU.subtract))

        def s_act(act):
            act.wait_ge(sm_pe, 1)
            nc.scalar.activation(decay[0:SN, :, 0:SN], hview(2, SN, SN), ACT.Exp).then_inc(sm_act, 1)
            act.wait_ge(sm_pe, 2)
            nc.scalar.activation(e_sb[:, :, 0:SN], hview(4, SN), ACT.Copy).then_inc(sm_act, 1)
            act.wait_ge(sm_pe, 3)
            nc.scalar.activation(dd[:, :, 0:SN], hview(7, SN), ACT.Abs).then_inc(abs_ready, 1)
            act.wait_ge(sm_dve, 7)
            nc.scalar.activation(nsq[:, :, :, 0:SN].rearrange("p h c n -> p (h c) n"),
                                 numr[:, :, :, 0:SN].rearrange("p h c n -> p (h c) n"), ACT.Square,
                                 scale=DV ** -0.5).then_inc(sm_act, 1)
            act.wait_ge(sm_pe, 4)
            nc.scalar.activation(zr[:, :, 0:SN], hview(2, SN), ACT.Ln, bias=eps[:, 0:1]).then_inc(ln_z, 1)
            act.wait_ge(ln_z, TILES + 1)
            nc.scalar.activation(zr[:, :, 0:SN], zr[:, :, 0:SN], ACT.Exp, scale=-0.5).then_inc(sm_act, 1)
            act.wait_ge(sm_dve, 9)
            nc.scalar.activation(y_hi[:, :, SC], numr[:, :, :, 0:SN].rearrange("p h c n -> p (h c) n"), ACT.Copy
                                 ).then_inc(sm_act, 1)

        def s_pool(pool):
            for b in range(NB):
                pool.wait_ge(sm_c, 4 * (b + 1))
                pool.dma_start(out[9][0, b].rearrange("h k v -> k h v"), c0[:, b, :, 0:DV]).then_inc(c0_out, 16)
                pool.dma_start(out[10][0, b].rearrange("h k -> k h").unsqueeze(2), c0[:, b, :, DV:VH],
                               allow_slow_non_contiguous=True).then_inc(c0_out, 16)
            pool.wait_ge(sm_dve, 10)
            pool.wait_ge(stored, 16 * 24)
            for f in range(KC):
                pool.dma_start(x2[:, f, :], scratch["x1"][:, f, :]).then_inc(x2_back, 16)

        def out_pe(pe):
            pe.wait_ge(sm_dve, 10)
            for c in range(KC):
                pe_unit(pe, U_OUT + c, N_OUT + c, y_hi, y_lo)

        y_st = at("y_st", R0, [P, TILES, D])
        y_t, y_act, y_dve, y_out = sem("y_t"), sem("y_by_act"), sem("y_by_dve"), sem("y_out")

        def y_pe(pe):
            pe.wait_ge(out_free, N_MLP1 + 12 * SLICES)
            for i in range(2 * TILES):
                half, t = divmod(i, TILES)
                n = x_rows(t)
                if i >= 8:
                    pe.wait_ge((y_act, y_dve)[i % 2], (i - 8) // 2 + 1)
                for f in range(4):
                    last = nc.tensor.transpose(ps[0:n, i % 8, P * f:P * f + P],
                                               x2[:, 4 * half + f, t * P:t * P + n], ident)
                last.then_inc(y_t, 1)

        def y_take(eng, i):
            half, t = divmod(i, TILES)
            n = x_rows(t)
            eng.wait_ge(y_t, i + 1)
            return y_st[0:n, t, 512 * half:512 * half + 512], ps[0:n, i % 8, :]

        def y_store(sp):
            for i in range(2 * TILES):
                half, t = divmod(i, TILES)
                sp.wait_ge((y_act, y_dve)[i % 2], i // 2 + 1)
                cols = slice(512 * half, 512 * half + 512)
                if t < NBLK:
                    sp.dma_start(out[0][0, t * P:t * P + P, cols], y_st[:, t, cols]).then_inc(y_out, 16)
                else:
                    sp.dma_start(out[1].rearrange("b s d -> (b s) d")[:, cols], y_st[0:SAMPLE, t, cols]
                                 ).then_inc(y_out, 16)
            sp.wait_ge(y_out, 16 * 2 * TILES)

        block = ctx.enter_context(nc.Block())

        @block.sync
        def _(sp):
            load_x(sp)
            for r in range(U_MLP0 // 2):
                if r >= 2:
                    sp.wait_ge(w_lo_ready, 2 * r - 2)
                load_qkv(sp, r) if r < 6 else load_wo(sp, r)
                if r == 1:
                    line_write(sp)
                    sp.wait_ge(x_by_act, TILES)
                    sp.wait_ge(x_by_dve, TILES)
                    sp.dma_start(scratch["x0"], x[:, :, :]).then_inc(x_saved, 16)
                if r == 3:
                    bias_read(sp)
            with sp.Fori(0, SLICES) as i:
                mlp_slice_sp(sp, 0, U_MLP0, i)
            for r in range(U_IN // 2, U_MLP1 // 2):
                sp.wait_ge(w_lo_ready, 2 * r - 2)
                if r < U_OUT // 2:
                    load_cols(sp, a["mlstm_w_in"][0], r, 256 * (r - U_IN // 2))
                else:
                    load_cols(sp, a["mlstm_w_out"][0], r, 256 * (r - U_OUT // 2))
            with sp.Fori(0, SLICES) as i:
                mlp_slice_sp(sp, 1, U_MLP1, i)
            y_store(sp)

        @block.gpsimd
        def _(pool):
            nc.gpsimd.memset(rel_ext[BUCKETS:BUCKETS + 1, :], 1.0).then_inc(rel_one, 1)
            bias_pool(pool)
            sample_loads(pool)
            caches_pool1(pool)
            for n in range(NG):
                att_scale_pool(pool, n)
            sink_rows(pool)
            caches_pool2(pool)
            pool.wait_ge(sp_steps, 7)
            pool.wait_ge(stored, 16 * (2 + 2 + 16))
            reload_x(pool)
            gates_pool(pool)
            gates_out(pool)
            og_pool(pool)
            c0_pool(pool)
            s_pool(pool)
            pool.wait_ge(c0_out, 32 * NB)
            pool.wait_ge(stored, 16 * 24)

        @block.scalar
        def _(act):
            act.preload_act_table_set("natural_log_exp_and_others")
            act.dma_start(cst[:, :], a["const"]).then_inc(ident_in, 16)
            act.dma_start(gain_rows[0:16, :], a["norm_mix"].rearrange("m (k p) -> (m k) p", p=P)).then_inc(gains_in, 16)
            act.dma_start(gain_rows[16:32, :], a["norm_mlp"].rearrange("m (k p) -> (m k) p", p=P)).then_inc(gains_in, 16)
            act.dma_start(gain_rows[32:40, :], a["mlstm_out_norm"].rearrange("m (k p) -> (m k) p", p=P)).then_inc(gains_in, 16)
            for dst, src in small:
                act.dma_start(dst, src, allow_slow_non_contiguous=True).then_inc(const_in, 16)
            for c in range(TILES):
                o, i = take_x(act, c, 0)
                nc.scalar.activation(o, i, ACT.Copy).then_inc(x_by_act, 1)
            act.wait_ge(x_by_act, TILES)
            act.wait_ge(x_by_dve, TILES)
            act.wait_ge(gains_ready, 1)
            for f in range(KC):
                norm_act(act, 0, f, x, h_hi)
                if f in (2, 3):
                    split_hi_static(act, f - 2)
            qkv_act(act)
            att_act(act)
            sample_act(act)
            project_act(act, U_WO, N_WO, 1, x, h_hi)
            norm_rstd_act(act, 1)
            with act.Fori(0, SLICES - 1) as i:
                mlp_slice_act(act, 0, U_MLP0, N_MLP0, i)
            mlp_slice_act(act, 0, U_MLP0, N_MLP0, SLICES - 1, norm=(2, x, h_hi))
            act.wait_ge(wg_in, 32)
            nc.scalar.activation(wg_hi[:, :, :], wg_raw[:, :, :], ACT.Copy).then_inc(wg_split_hi, 1)
            norm_rstd_act(act, 2)
            in_act(act)
            act.preload_act_table_set("natural_log_exp_and_others")
            for c in range(TILES):
                chunk_act(act, c)
            s_act(act)
            act.wait_ge(c0_out, 32 * NB)
            project_act(act, U_OUT, N_OUT, 3, x2, h_hi2)
            norm_rstd_act(act, 3)
            with act.Fori(0, SLICES - 1) as i:
                mlp_slice_act(act, 1, U_MLP1, N_MLP1, i)
            mlp_slice_act(act, 1, U_MLP1, N_MLP1, SLICES - 1, 8 - AHEAD)
            for i in range(0, 2 * TILES, 2):
                o, src = y_take(act, i)
                nc.scalar.activation(o, src, ACT.Copy).then_inc(y_act, 1)

        @block.vector
        def _(dve):
            nc.vector.memset(eps[:, :], EPS)
            nc.vector.memset(x[:, :, T:TP], 0.0)
            dve.wait_ge(line_mm, 1)
            nc.vector.tensor_copy(line[:, :], ps[0:QH, 0, 0:LINE]).then_inc(line_c, 1)
            for c in range(TILES):
                o, i = take_x(dve, c, 1)
                nc.vector.tensor_copy(o, i).then_inc(x_by_dve, 1)
            dve.wait_ge(gains_t, 1)
            nc.vector.tensor_copy(gains[:, :, :].rearrange("p m k -> p (m k)"), ps[:, 7, 0:5 * KC]
                                  ).then_inc(gains_ready, 1)
            dve.wait_ge(gains_ready, 1)
            dve.wait_ge(const_in, 16 * len(small))
            nc.vector.tensor_scalar(nsinks[:, :], sinks[:, :], -1.0, None, ALU.mult)
            nc.vector.tensor_scalar(bg15[:, :], bgate[:, :], 1.0 / CAP, None, ALU.mult)
            dve.wait_ge(x_by_dve, TILES)
            dve.wait_ge(x_by_act, TILES)
            for f in range(KC):
                norm_lo_dve(dve, 0, f, x, h_hi, h_lo)
                if f:
                    norm_acc_dve(dve, 0, f)
                if f in (2, 3):
                    split_lo_static(dve, f - 2)
            qkv_dve(dve)
            dve.wait_ge(qk_normed, 30)
            nc.vector.memset(o_hi[:, :, T:TP].bitcast(F32), 0.0)
            nc.vector.memset(o_lo[:, :, T:TP].bitcast(F32), 0.0)
            att_dve(dve)
            sample_dve(dve)
            sample_dve2(dve)
            project_dve(dve, U_WO, N_WO, 1, x, h_hi, h_lo, x_back)
            dve.wait_ge(norm_rstd, 2)
            with dve.Fori(0, SLICES - 1) as i:
                mlp_slice_dve(dve, 0, U_MLP0, N_MLP0, i, x)
            mlp_slice_dve(dve, 0, U_MLP0, N_MLP0, SLICES - 1, x, norm=(2, x, h_hi, h_lo))
            dve.wait_ge(out_ready, N_IN)
            nc.vector.memset(wg_raw[:, :, :], 0.0).then_inc(wg_zero, 1)
            dve.wait_ge(wg_split_hi, 1)
            nc.vector.tensor_tensor(wg_lo[:, :, :], wg_raw[:, :, :], wg_hi[:, :, :].bitcast(F32), ALU.subtract
                                    ).then_inc(wg_split, 1)
            gates_dve(dve)
            in_dve(dve)
            dve.wait_ge(v2_taken, 24)
            dve.wait_ge(og_out, 16 * KC)
            nc.vector.tensor_copy(v_m[:, :, :], v[SAMPLE:LAST, NBLK, :, :]).then_inc(vm_done, 1)
            nc.vector.memset(y_hi[:, :, T:TP].bitcast(F32), 0.0)
            dve.wait_ge(out_ready, N_OUT)
            dve.wait_ge(og_in, 16 * KC)
            nc.vector.memset(y_lo[:, :, T:TP].bitcast(F32), 0.0)
            dve.wait_ge(sel_in, 16)
            for c in range(TILES):
                chunk_dve(dve, c)
            s_dve(dve)
            project_dve(dve, U_OUT, N_OUT, 3, x2, h_hi2, h_lo2, x2_back)
            dve.wait_ge(norm_rstd, 4)
            with dve.Fori(0, SLICES - 1) as i:
                mlp_slice_dve(dve, 1, U_MLP1, N_MLP1, i, x2)
            mlp_slice_dve(dve, 1, U_MLP1, N_MLP1, SLICES - 1, x2, 8 - AHEAD)
            for i in range(1, 2 * TILES, 2):
                o, src = y_take(dve, i)
                nc.vector.tensor_copy(o, src).then_inc(y_dve, 1)

        @block.tensor
        def _(pe):
            pe.wait_ge(line_in, 32)
            pe.wait_ge(rel_one, 1)
            nc.tensor.matmul(ps[0:QH, 0, 0:LINE], rel_ext[:, :], bucket[:, :], start=True, stop=True
                             ).then_inc(line_mm, 1)
            pe.wait_ge(line_c, 1)
            load_pe(pe)
            pe.wait_ge(gains_in, 48)
            pe.wait_ge(x_by_dve, 8)
            nc.tensor.transpose(ps[:, 7, 0:5 * KC], gain_rows[:, :], ident[0:5 * KC, 0:5 * KC]
                                ).then_inc(gains_t, 1)
            qkv_pe(pe)
            att_pe(pe)
            sample_pe(pe)
            wo_pe(pe)
            for g in range(3):
                norm_pe(pe, 1, g)
            with pe.Fori(0, SLICES) as i:
                mlp_slice_pe(pe, 0, U_MLP0, N_MLP0, i, h_hi, h_lo)
            gates_pe(pe)
            in_pe(pe)
            pe.wait_ge(vm_done, 1)
            pe.wait_ge(sel_in, 16)
            pe.wait_ge(gate_act, 4)
            pe.wait_ge(out_free, N_OUT)
            for c in range(TILES):
                chunk_pe(pe, c)
            s_pe(pe)
            out_pe(pe)
            for g in range(3):
                norm_pe(pe, 3, g)
            with pe.Fori(0, SLICES) as i:
                mlp_slice_pe(pe, 1, U_MLP1, N_MLP1, i, h_hi2, h_lo2)
            y_pe(pe)


_INS = ["x_prompt", "x_sample", "cache_k", "cache_v", "state_C", "state_n", "state_m", "meta_tokens",
        "rel_table", "norm_mix", "norm_mlp", "attn_w_qkv", "attn_q_norm", "attn_k_norm", "attn_sinks",
        "attn_w_o", "mlstm_w_in", "mlstm_w_gate", "mlstm_b_gate", "mlstm_out_norm", "mlstm_w_out",
        "mlp_w_up", "mlp_w_down"]
_OUTS = [(1, SEQ, D), (NB, NS, D),
         (1, 1, WIN, KH, HD), (1, 1, WIN, KH, HD), (1, NB, WIN, KH, HD), (1, NB, WIN, KH, HD),
         (1, 1, MH, DK, DV), (1, 1, MH, DK), (1, 1, MH),
         (1, NB, MH, DK, DV), (1, NB, MH, DK), (1, NB, MH)]
_SCRATCH = {"x0": [P, KC, TP], "x1": [P, KC, TP], "og": [P, KC, TP], "line": [QH, BLK, LINE]}


def kernel(**inputs):
    import concourse.bacc as _bacc
    from concourse.bass_utils import run_bass_kernel_spmd as _run

    nc = _bacc.Bacc("TRN2", target_bir_lowering=False, num_devices=1)
    arrays, args = {}, {}
    for name in _INS:
        arr = np.ascontiguousarray(inputs[name])
        arrays[f"in_{name}"] = arr
        args[name] = nc.dram_tensor(f"in_{name}", arr.shape, F32, kind="ExternalInput").ap()
    consts = {"const": np.concatenate([CONST[k] for k in CONST], axis=1), "select": selector_constants(),
              "buckets": bucket_constant(), "keep": scan_constant()}
    for name, arr in consts.items():
        arr = np.ascontiguousarray(arr)
        arrays[f"in_{name}"] = arr
        args[name] = nc.dram_tensor(f"in_{name}", arr.shape, F32, kind="ExternalInput").ap()
    outs = [nc.dram_tensor(f"out_{i}", shape, F32, kind="ExternalOutput").ap() for i, shape in enumerate(_OUTS)]
    scratch = {k: nc.dram_tensor(f"scratch_{k}", s, F32, kind="Internal").ap() for k, s in _SCRATCH.items()}
    build(nc, args, outs, scratch)
    r = _run(nc, [arrays], core_ids=[0])
    return tuple(r.results[0][f"out_{i}"] for i in range(len(_OUTS)))
```

```python
from contextlib import ExitStack

import numpy as np

import concourse.bass as bass
from concourse import mybir

F32 = mybir.dt.float32
F32R = mybir.dt.float32r
ACT = mybir.ActivationFunctionType
ALU = mybir.AluOpType
AX = mybir.AxisListType.X

P = 128
D = 1024
KC = D // P
SEQ, META, NB, NS = 1024, 16, 8, 4
SAMPLE = NB * NS
BLK = 128
NBLK = SEQ // BLK
COL_S = SEQ
COL_M = SEQ + SAMPLE
T = SEQ + SAMPLE + META
TG = 358
TP = 3 * TG
TILES = NBLK + 1
LAST = SAMPLE + META
EPS = 1e-6
QH, KH, HD, WIN = 16, 4, 64, 128
MH, DK, DV = 4, 128, 256
VH = DV + 1
FF = 4096
SLICES = 8
NEG = -1e30
CAP = 15.0
BUCKETS, MAX_DISTANCE = 32, 128
LINE = 384

U_QKV, U_WO, U_MLP0 = 0, 12, 20
U_IN = U_MLP0 + 8 * SLICES
U_OUT = U_IN + 24
U_MLP1 = U_OUT + 8
U_END = U_MLP1 + 8 * SLICES
N_QKV, N_WO, N_MLP0 = 0, 12, 20
N_IN = N_MLP0 + 12 * SLICES
N_OUT = N_IN + 25
N_MLP1 = N_OUT + 8
AHEAD = 2


def outs_through(u):
    if u < U_MLP0:
        return u + 1
    if u < U_IN:
        i, j = divmod(u - U_MLP0, 8)
        return N_MLP0 + 12 * i + (j + 1 if j < 4 else 2 * j - 2)
    if u < U_OUT:
        return N_IN + 1 + (u - U_IN) + 1
    if u < U_MLP1:
        return N_OUT + (u - U_OUT) + 1
    i, j = divmod(u - U_MLP1, 8)
    return N_MLP1 + 12 * i + (j + 1 if j < 4 else 2 * j - 2)


def is_down(u):
    for u0 in (U_MLP0, U_MLP1):
        if u0 <= u < u0 + 8 * SLICES:
            return (u - u0) % 8 >= 4
    return False


def shape_constants():
    c = {}
    c["ident"] = np.eye(P, dtype=np.float32)
    c["ones"] = np.ones((P, P), np.float32)
    two = np.zeros((P, P), np.float32)
    two[:HD, :HD] = 1.0
    two[HD:, HD:] = 1.0
    c["head_ones"] = two
    j, t = np.arange(P)[:, None], np.arange(P)[None, :]
    c["causal"] = np.where(j <= t, 0.0, NEG).astype(np.float32)
    js, ts = j[:SAMPLE], t[:, :SAMPLE]
    own = (js // NS == ts // NS) & (js <= ts)
    c["own_causal"] = np.zeros((P, SAMPLE), np.float32)
    c["own_causal"][:SAMPLE] = np.where(own, 0.0, NEG)
    c["pair"] = np.zeros((P, MH), np.float32)
    for h in range(MH):
        c["pair"][h, h] = c["pair"][32 + h, h] = 1.0
    return c


def bucket_constant():
    out = np.zeros((BUCKETS + 1, LINE), np.float32)
    exact = BUCKETS // 2
    for e in range(LINE):
        dist = 2 * BLK - 1 - e
        if 0 <= dist <= WIN:
            b = dist if dist < exact else exact + int(
                np.log(dist / exact) / np.log(MAX_DISTANCE / exact) * (BUCKETS - exact) + 1e-6)
            out[min(b, BUCKETS - 1), e] = 1.0
        else:
            out[BUCKETS, e] = NEG
    return out


def scan_constant():
    keep = np.ones((MH, TP), np.float32)
    keep[:, 0:SEQ:BLK] = 0.0
    keep[:, COL_S:COL_M:NS] = 0.0
    keep[:, COL_M] = 0.0
    return keep


CONST = shape_constants()
CONST_AT, _n = {}, 0
for _k, _v in CONST.items():
    CONST_AT[_k] = (_n, _n + _v.shape[1])
    _n += _v.shape[1]
CONST_COLS = _n


def build(nc, a, out, scratch):
    with ExitStack() as ctx:
        R0 = 16512
        R1 = R0 + 37024
        R2 = R1 + 34368
        R3 = R2 + 34368
        RAW = R3 + 34368
        WHI = RAW + 16384
        WLO = WHI + 16384
        R4 = WLO + 16384
        BUF = 4320
        RC = R4 + 4 * BUF

        def at(name, offset, shape, dt=F32):
            return nc.alloc_sbuf_tensor_at(name, shape, dt, offset=offset)

        x = at("x", R0, [P, KC, TP])
        x_tok = at("x_tok", R1, [P, TILES, D])
        h_hi = at("h_hi", R1, [P, KC, TP], F32R)
        h_lo = at("h_lo", R2, [P, KC, TP], F32R)
        act_hi = at("act_hi", R3, [P, 4, TP], F32R)
        act_lo = at("act_lo", R3 + 4 * TP * 4, [P, 4, TP], F32R)
        raw = at("raw", RAW, [P, 2, 2048])
        w_hi = at("w_hi", WHI, [P, 4, 1024], F32R)
        w_lo = at("w_lo", WLO, [P, 4, 1024], F32R)
        sq = [at(f"sq{i}", R4 + i * BUF, [P, TP]) for i in range(2)]
        relu = [at(f"relu{i}", R4 + i * BUF, [P, TP]) for i in range(2)]
        rstd = at("rstd", R4 + 2 * BUF, [P, 3, TG])
        acc = at("acc", R4 + 3 * BUF, [P, TP])
        relu_sq = at("relu_sq", R4 + 3 * BUF, [P, TP])
        head_rstd = at("head_rstd", R4 + 3 * BUF, [P, 3, TG])
        q = at("q", R3, [P, KC, TP])
        kn = at("kn", R0, [P, 2, TP])
        v_tok = at("v_tok", R0 + 8608, [P, TILES, KH * HD])
        bias = at("bias", R0 + 8608 + 9216, [P, QH, 2 * BLK])
        v_meta = at("v_meta", R0 + 8608 + 9216 + 16384, [META, KH * HD])
        vT = [at(f"vT{i}", R4 + i * BUF, [P, TP]) for i in range(2)]
        cst = at("cst", RC, [P, CONST_COLS])
        at_c = RC + (CONST_COLS * 4 + 31) // 32 * 32
        gains = at("gains", at_c, [P, 5, KC])
        qk_gain = at("qk_gain", at_c + 320, [P, 2])
        gain_rows = at("gain_rows", at_c + 352, [5 * KC, P])
        sinks = at("sinks", at_c + 160, [P, QH])
        nsinks = at("nsinks", at_c + 224, [P, QH])
        eps = at("eps", at_c + 288, [P, 1])
        tokout = [at(f"tokout{i}", at_c + 352 + i * 1024, [P, 256]) for i in range(2)]
        gain_of = (0, 2, 1, 3)
        ident = cst[:, slice(*CONST_AT["ident"])]
        ones = cst[:, slice(*CONST_AT["ones"])]
        head_ones = cst[:, slice(*CONST_AT["head_ones"])]

        ps = ctx.enter_context(nc.psum_tensor("ps", [P, 8, 512], F32))

        def grp(ap):
            return ap.rearrange("p (g n) -> p g n", g=3)

        def sem(name):
            return ctx.enter_context(nc.semaphore(name))

        x_in = [sem(f"x_in{c}") for c in range(TILES)]
        ident_in, gains_in, const_in = sem("ident_in"), sem("gains_in"), sem("const_in")
        gains_t, gains_ready = sem("gains_t"), sem("gains_ready")
        xt_ready = sem("xt_ready")
        x_by_act, x_by_dve = sem("x_by_act"), sem("x_by_dve")
        raw_in = [sem("raw_in0"), sem("raw_in1")]
        w_hi_ready, w_lo_ready = sem("w_hi_ready"), sem("w_lo_ready")
        out_ready = sem("out_ready")
        out_free = sem("out_free")
        norm_sq, norm_acc, norm_summed = sem("norm_sq"), sem("norm_acc"), sem("norm_summed")
        norm_ln, norm_rstd = sem("norm_ln"), sem("norm_rstd")
        norm_hi, norm_lo = sem("norm_hi"), sem("norm_lo")
        x_saved, x1_saved, x_back = sem("x_saved"), sem("x1_saved"), sem("x_back")
        head_sq = sem("head_sq")
        qk_sum, qk_ln, qk_rstd, qk_normed = sem("qk_sum"), sem("qk_ln"), sem("qk_rstd"), sem("qk_normed")
        vt_ready, v_taken = sem("vt_ready"), sem("v_taken")
        up_done, act_split, sq_done = sem("up_done"), sem("act_split"), sem("sq_done")
        line_out = sem("line_out")
        cache_t, cache_c, stored = sem("cache_t"), sem("cache_c"), sem("stored")
        kv_out = sem("kv_out")

        raw_k8 = raw[:, :, :].rearrange("p s (k n) -> p s k n", k=8)
        raw_k4 = raw[:, :, :].rearrange("p s (k n) -> p s k n", k=4)
        raw_per = [64] * 4 + [16] * 2 + [64] * 4 + [16] * 200

        def raw_target(r):
            return sum(raw_per[r % 2:r + 1:2])

        def raw_unit(j, slot, down):
            if down:
                return raw_k4[:, slot, :, 256 * j:256 * j + 256]
            return raw_k8[:, slot, :, 128 * j:128 * j + 128]

        def unit_view(w, slot, down):
            return w[:, slot, :].rearrange("p (k n) -> p k n", k=4 if down else 8)

        def split_hi(act, slot, rslot, j, down, raw_wait, outs_wait):
            act.wait_ge(raw_in[rslot], raw_wait)
            if outs_wait is not None:
                act.wait_ge(out_ready, outs_wait)
            nc.scalar.activation(unit_view(w_hi, slot, down), raw_unit(j, rslot, down),
                                 ACT.Copy).then_inc(w_hi_ready, 1)

        def split_lo(dve, slot, rslot, j, down, hi_wait):
            dve.wait_ge(w_hi_ready, hi_wait)
            nc.vector.tensor_tensor(unit_view(w_lo, slot, down), raw_unit(j, rslot, down),
                                    unit_view(w_hi, slot, down).bitcast(F32), ALU.subtract
                                    ).then_inc(w_lo_ready, 1)

        def split_hi_static(act, u):
            if u < U_END:
                split_hi(act, u % 4, (u // 2) % 2, u % 2, is_down(u), raw_target(u // 2),
                         outs_through(u - 4) if u >= 4 else None)

        def split_lo_static(dve, u):
            if u < U_END:
                split_lo(dve, u % 4, (u // 2) % 2, u % 2, is_down(u), u + 1)

        def out_banks(n):
            return 3 * (n % 2)

        def chunk_mms(slot, k, kc, cols, bank, hi, lo, k_of, start, stop, groups=None):
            wh = w_hi[:, slot, :].rearrange("p (k n) -> p k n", k=kc)[:, k, cols]
            wl = w_lo[:, slot, :].rearrange("p (k n) -> p k n", k=kc)[:, k, cols]
            for g in range(3):
                o = ps[:, bank + g, 0:TG]
                c = slice(g * TG, g * TG + TG)
                nc.tensor.matmul(o, wh, hi[:, k_of, c], start=start, stop=False)
                nc.tensor.matmul(o, wh, lo[:, k_of, c], start=False, stop=False)
            for g in range(3):
                last = nc.tensor.matmul(ps[:, bank + g, 0:TG], wl, hi[:, k_of, g * TG:g * TG + TG],
                                        start=False, stop=stop)
            return last

        def w_block(w, slot, k, kc, cols):
            return w[:, slot, :].rearrange("p (k n) -> p k n", k=kc)[:, k, cols]

        def pass_hi(slot, k, kc, cols, bank, hi, start):
            for i, w in enumerate((w_hi, w_lo)):
                for g in range(3):
                    nc.tensor.matmul(ps[:, bank + g, 0:TG], w_block(w, slot, k, kc, cols),
                                     hi[:, k, g * TG:g * TG + TG], start=start and i == 0, stop=False)

        def pass_lo(slot, k, kc, cols, bank, lo, stop):
            for g in range(3):
                last = nc.tensor.matmul(ps[:, bank + g, 0:TG], w_block(w_hi, slot, k, kc, cols),
                                        lo[:, k, g * TG:g * TG + TG], start=False, stop=stop)
            return last

        def pe_unit(pe, u, n, hi, lo, sides=None, first_norm=None, side_at=(2, 4, 6)):
            pe.wait_ge(w_lo_ready, u + 1)
            if n >= 2:
                pe.wait_ge(out_free, n - 1)
            for k in range(KC):
                if first_norm is not None:
                    pe.wait_ge(norm_lo, KC * first_norm + k + 1)
                if sides and k in side_at:
                    sides(side_at.index(k))
                last = chunk_mms(u % 4, k, 8, slice(0, P), out_banks(n), hi, lo, k, k == 0, k == KC - 1)
            last.then_inc(out_ready, 1)

        def norm_act(act, m, f, x, h_hi):
            nc.scalar.activation(h_hi[:, f, :], x[:, f, :], ACT.Copy,
                                 scale=gains[:, gain_of[m], f:f + 1]).then_inc(norm_hi, 1)
            if f >= 2:
                act.wait_ge(norm_acc, (KC - 1) * m + f - 1)
            nc.scalar.activation(sq[f % 2][:, :], x[:, f, :], ACT.Square).then_inc(norm_sq, 1)

        def norm_lo_dve(dve, m, f, x, h_hi, h_lo):
            dve.wait_ge(norm_hi, KC * m + f + 1)
            nc.vector.scalar_tensor_tensor(out=h_lo[:, f, :], in0=x[:, f, :], scalar=gains[:, gain_of[m], f:f + 1],
                                           in1=h_hi[:, f, :].bitcast(F32), op0=ALU.mult, op1=ALU.subtract
                                           ).then_inc(norm_lo, 1)

        def norm_acc_dve(dve, m, f):
            dve.wait_ge(norm_sq, KC * m + f + 1)
            if f >= 2:
                dve.wait_ge(norm_acc, (KC - 1) * m + f - 1)
            first = sq[0] if f == 1 else acc
            nc.vector.tensor_tensor(acc[:, :], first[:, :], sq[f % 2][:, :], ALU.add).then_inc(norm_acc, 1)

        def norm_pe(pe, m, g):
            pe.wait_ge(norm_acc, (KC - 1) * (m + 1))
            if g == 2:
                pe.wait_ge(norm_ln, 3 * m + 1)
            nc.tensor.matmul(ps[:, 6 + g % 2, 0:TG], ones, acc[:, g * TG:g * TG + TG], start=True, stop=True
                             ).then_inc(norm_summed, 1)

        def norm_rstd_act(act, m):
            for g in range(3):
                act.wait_ge(norm_summed, 3 * m + g + 1)
                nc.scalar.activation(rstd[:, g, :], ps[:, 6 + g % 2, 0:TG], ACT.Ln, scale=1.0 / D,
                                     bias=eps[:, 0:1]).then_inc(norm_ln, 1)
            act.wait_ge(norm_ln, 3 * m + 3)
            nc.scalar.activation(rstd[:, :, :], rstd[:, :, :], ACT.Exp, scale=-0.5).then_inc(norm_rstd, 1)

        def times_rstd(dst, n, scale=1.0, rows=slice(0, P)):
            nc.vector.scalar_tensor_tensor(out=dst, in0=ps[rows, out_banks(n):out_banks(n) + 3, 0:TG], scalar=scale,
                                           in1=rstd[rows, :, :], op0=ALU.mult, op1=ALU.mult
                                           ).then_inc(out_free, 1)

        def x_rows(c):
            return BLK if c < NBLK else LAST

        small = []
        for half in range(2):
            small += [(qk_gain[HD * half:HD * half + HD, 0:1], a["attn_q_norm"].rearrange("a d -> d a")),
                      (qk_gain[HD * half:HD * half + HD, 1:2], a["attn_k_norm"].rearrange("a d -> d a"))]
        for s in range(4):
            gp, ip = divmod(s, 2)
            small += [(sinks[:, 4 * s:4 * s + 4].rearrange("p (a b) -> p a b", a=2),
                       bass.AP(a["attn_sinks"].tensor, 8 * gp + 2 * ip, [[0, P], [4, 2], [1, 2]]))]

        def load_x(sp):
            for c in range(TILES):
                if c < NBLK:
                    sp.dma_start(x_tok[:, c, :], a["x_prompt"][0, c * P:c * P + P, :]).then_inc(x_in[c], 16)
                else:
                    sp.dma_start(x_tok[0:SAMPLE, c, :], a["x_sample"].rearrange("b s d -> (b s) d")
                                 ).then_inc(x_in[c], 16)
                    sp.dma_start(x_tok[SAMPLE:LAST, c, :], a["meta_tokens"]).then_inc(x_in[c], 16)

        def x_tile_wait(eng, c):
            eng.wait_ge(x_in[c], 16 if c < NBLK else 32)

        def load_pe(pe):
            pe.wait_ge(ident_in, 16)
            for c in range(TILES):
                x_tile_wait(pe, c)
                n = x_rows(c)
                for half in range(2):
                    i = 2 * c + half
                    if i >= 8:
                        pe.wait_ge((x_by_act, x_by_dve)[half], (i - 8) // 2 + 1)
                    for f in range(4):
                        last = nc.tensor.transpose(ps[:, i % 8, f * P:f * P + n],
                                                   x_tok[0:n, c, (4 * half + f) * P:(4 * half + f + 1) * P],
                                                   ident[0:n, 0:n])
                    last.then_inc(xt_ready, 1)

        def take_x(eng, c, half):
            n = x_rows(c)
            eng.wait_ge(xt_ready, 2 * c + half + 1)
            src = ps[:, (2 * c + half) % 8, :].rearrange("p (f n) -> p f n", f=4)[:, :, 0:n]
            return x[:, 4 * half:4 * half + 4, c * P:c * P + n], src

        def load_qkv(sp, r):
            w = a["attn_w_qkv"][0].rearrange("(k p) n -> p k n", p=P)
            if r < 4:
                gp, i = r // 2, 2 * (r % 2)
                dst = raw_k8[:, r % 2, :, :].rearrange("p k (c g d) -> p k c g d", c=2, g=2)
                for g in range(2):
                    for c in range(2):
                        c0 = gp * 512 + g * 256 + (i + c) * HD
                        sp.dma_start(dst[:, :, c, g, :], w[:, :, c0:c0 + HD]).then_inc(raw_in[r % 2], 16)
            else:
                sp.dma_start(raw_k8[:, r % 2, :, :], w[:, :, 256 * r:256 * r + 256]).then_inc(raw_in[r % 2], 16)

        def load_wo(sp, r):
            w = a["attn_w_o"][0].rearrange("(gp g i d) n -> gp g d i n", gp=2, g=2, i=4)
            c0 = 256 * (r - U_WO // 2)
            for gp in range(2):
                for g in range(2):
                    sp.dma_start(raw_k8[HD * g:HD * g + HD, r % 2, 4 * gp:4 * gp + 4, :],
                                 w[gp, g][:, :, c0:c0 + 256]).then_inc(raw_in[r % 2], 16)

        def load_cols(sp, w, r, c0):
            sp.dma_start(raw_k8[:, r % 2, :, :],
                         w.rearrange("(k p) n -> p k n", p=P)[:, :, c0:c0 + 256]).then_inc(raw_in[r % 2], 16)

        def qk_dst(c):
            return q[:, c, :] if c < 8 else kn[:, c - 8, :]

        def side_bank(s):
            return 6 + s % 2

        def qkv_side_pe(pe, c, g):
            s = 3 * c + g
            if s >= 2:
                t = s - 2
                pe.wait_ge(qk_ln, t + 1) if t < 30 else pe.wait_ge(v_taken, t - 29)
            elif s == 0:
                pe.wait_ge(norm_ln, 3)
            if c < 10:
                pe.wait_ge(head_sq, c + 1)
                nc.tensor.matmul(ps[:, side_bank(s), 0:TG], head_ones, sq[c % 2][:, g * TG:g * TG + TG],
                                 start=True, stop=True).then_inc(qk_sum, 1)
            else:
                pe.wait_ge(out_free, c + 1)
                src = vT[c - 10]
                for t in range(4 * g, min(4 * g + 4, TILES)):
                    n = x_rows(t)
                    last = nc.tensor.transpose(ps[0:n, side_bank(s), (t % 4) * P:(t % 4) * P + P],
                                               src[:, t * P:t * P + n], ident)
                last.then_inc(vt_ready, 1)

        def qkv_pe(pe):
            for c in range(12):
                if c == 0:
                    pe_unit(pe, c, c, h_hi, h_lo, first_norm=0)
                    for g in range(3):
                        norm_pe(pe, 0, g)
                else:
                    pe_unit(pe, c, c, h_hi, h_lo, lambda g, c=c: qkv_side_pe(pe, c - 1, g),
                            side_at=(2, 4, 6) if c > 1 else (5, 6, 7))
            for g in range(3):
                qkv_side_pe(pe, 11, g)

        def qkv_side_act(act, c):
            for g in range(3):
                s = 3 * c + g
                act.wait_ge(qk_sum, s + 1)
                if c:
                    act.wait_ge(qk_normed, s - 2)
                nc.scalar.activation(head_rstd[:, g, :], ps[:, side_bank(s), 0:TG], ACT.Ln,
                                     scale=1.0 / HD, bias=eps[:, 0:1]).then_inc(qk_ln, 1)
                act.wait_ge(qk_ln, s + 1)
                nc.scalar.activation(head_rstd[:, g, :], head_rstd[:, g, :], ACT.Exp, scale=-0.5
                                     ).then_inc(qk_rstd, 1)

        def qkv_act(act):
            for c in range(12):
                split_hi_static(act, c + AHEAD)
                if c == 0:
                    norm_rstd_act(act, 0)
                elif c <= 10:
                    qkv_side_act(act, c - 1)
                if c < 10:
                    act.wait_ge(out_free, c + 1)
                    if c >= 2:
                        act.wait_ge(qk_sum, 3 * (c - 1))
                    nc.scalar.activation(sq[c % 2][:, :], qk_dst(c), ACT.Square).then_inc(head_sq, 1)

        def qkv_side_dve(dve, c):
            for g in range(3):
                s = 3 * c + g
                if c < 10:
                    dve.wait_ge(qk_rstd, s + 1)
                    d = qk_dst(c)[:, g * TG:g * TG + TG]
                    nc.vector.scalar_tensor_tensor(out=d, in0=d, scalar=qk_gain[:, c // 8:c // 8 + 1],
                                                   in1=head_rstd[:, g, :], op0=ALU.mult, op1=ALU.mult
                                                   ).then_inc(qk_normed, 1)
                else:
                    dve.wait_ge(vt_ready, s - 29)
                    n, tiles = (P, 4) if g < 2 else (LAST, 1)
                    nc.vector.tensor_copy(
                        v_tok[0:n, 4 * g:4 * g + tiles, (c - 10) * P:(c - 9) * P],
                        ps[0:n, side_bank(s), :].rearrange("p (t n) -> p t n", t=4)[:, 0:tiles, :]
                    ).then_inc(v_taken, 1)

        def qkv_dve(dve):
            for c in range(12):
                split_lo_static(dve, c + AHEAD)
                if c:
                    qkv_side_dve(dve, c - 1)
                dve.wait_ge(out_ready, c + 1)
                if c == 0:
                    dve.wait_ge(norm_rstd, 1)
                if c == 8:
                    dve.wait_ge(x_saved, 16)
                if c >= 10:
                    dve.wait_ge(qk_sum, 27 + 3 * (c - 10))
                times_rstd(grp(qk_dst(c) if c < 10 else vT[c - 10][:, :]), c)
            qkv_side_dve(dve, 11)

        cache_src = [(NBLK - 1, BLK), (NBLK, SAMPLE)]

        def caches_pe(pe):
            for j, (t, n) in enumerate(cache_src):
                for gp in range(2):
                    last = nc.tensor.transpose(ps[0:n, 6 + j, gp * P:gp * P + P], kn[:, gp, t * P:t * P + n], ident)
                last.then_inc(cache_t, 1)

        def caches_dve(dve):
            for j, (t, n) in enumerate(cache_src):
                dve.wait_ge(cache_t, j + 1)
                nc.vector.tensor_copy(tokout[j][0:n, :], ps[0:n, 6 + j, 0:256]).then_inc(cache_c, 1)

        def caches_v(sp):
            for i in range(2):
                src = a["cache_k" if i == 0 else "cache_v"][0]
                sp.dma_start(out[4 + i][0][:, 0:WIN - NS, :, :], src[:, NS:WIN, :, :]).then_inc(kv_out, 16)
            sp.wait_ge(v_taken, 6)
            sp.dma_start(out[3][0, 0].rearrange("s h d -> s (h d)"), v_tok[:, NBLK - 1, :]).then_inc(kv_out, 16)
            for b in range(NB):
                sp.dma_start(out[5][0, b, WIN - NS:WIN].rearrange("s h d -> s (h d)"),
                               v_tok[NS * b:NS * b + NS, NBLK, :]).then_inc(kv_out, 16)

        def caches_k(sp):
            sp.wait_ge(cache_c, 2)
            sp.dma_start(out[2][0, 0].rearrange("s h d -> s (h d)"), tokout[0][:, :]).then_inc(kv_out, 16)
            for b in range(NB):
                sp.dma_start(out[4][0, b, WIN - NS:WIN].rearrange("s h d -> s (h d)"),
                               tokout[1][NS * b:NS * b + NS, :]).then_inc(kv_out, 16)

        rel_ext = at("rel_ext", R4 + 2 * BUF, [BUCKETS + 1, QH])
        bucket = at("bucket", R4 + 2 * BUF + 64, [BUCKETS + 1, LINE])
        line = at("line", R0 + 35232, [QH, LINE])
        s_bias = at("s_bias", R1, [P, WIN + NS])
        line_in, line_mm, line_c = sem("line_in"), sem("line_mm"), sem("line_c")
        bias_in = sem("bias_in")
        rel_one = sem("rel_one")

        def bias_pool(pool):
            pool.dma_start(bucket[:, :], a["buckets"]).then_inc(line_in, 16)
            pool.dma_start(rel_ext[0:BUCKETS, :], a["rel_table"]).then_inc(line_in, 16)

        def line_src(base, dims):
            return bass.AP(scratch["line"].tensor, base, dims)

        def line_write(sp):
            sp.wait_ge(line_c, 1)
            sp.dma_start(scratch["line"][:, :, :], line[:, :].unsqueeze(1).to_broadcast([QH, BLK, LINE])
                         ).then_inc(line_out, 16)

        def bias_read(sp):
            sp.wait_ge(line_out, 16)
            sp.wait_ge(x_saved, 16)
            sp.wait_ge(norm_lo, KC)
            sp.wait_ge(norm_sq, KC)
            for s in range(4):
                gp, ip = divmod(s, 2)
                for par in range(2):
                    sp.dma_start(bias[:, 4 * s + 2 * par:4 * s + 2 * par + 2, :],
                                   line_src((8 * gp + 4 * par + 2 * ip) * BLK * LINE + BLK - 1,
                                            [[LINE - 1, P], [BLK * LINE, 2], [1, 2 * BLK]])
                                   ).then_inc(bias_in, 16)

        NG = 4 * TILES
        P_BUFS = 4
        LAG = 3
        prob = [at(f"prob{i}", R4 + i * 4096 if i < 3 else R1 + 29216, [P, 4, 2 * BLK]) for i in range(P_BUFS)]
        probT = at("probT", R4 + 3 * 4096, [P, 4, 2, BLK])
        at_s = at_c + 352 + 2048
        stat = at("stat", at_s, [P, P_BUFS, 5, 4])
        esink = at("esink", at_s + 320, [P, P_BUFS, 4])
        o_hi = at("o_hi", R3, [P, KC, TP], F32R)
        o_lo = at("o_lo", R2, [P, KC, TP], F32R)
        s_done, s_taken, max_done = sem("s_done"), sem("s_taken"), sem("max_done")
        negm_done, logit_done, exp_done = sem("negm_done"), sem("logit_done"), sem("exp_done")
        den_done, rden_done, prob_ready = sem("den_done"), sem("rden_done"), sem("prob_ready")
        t_done, pT_ready, pv_done = sem("t_done"), sem("pT_ready"), sem("pv_done")
        o_hi_done, o_taken, vmeta_done = sem("o_hi_done"), sem("o_taken"), sem("vmeta_done")

        def block_of(n):
            b, step = divmod(n, 4)
            if b == 0:
                return (COL_M, META), (0, None, 0), BLK, BLK + META, step
            col = BLK * (b - 1)
            if b == 1:
                return (col, BLK), (COL_M, None, META), BLK - META, 2 * BLK, step
            return (col, BLK), (col - BLK, b - 2, BLK), 0, 2 * BLK, step

        def att_scores_pe(pe, n):
            (qc, nq), (pc, _, npk), k0, k1, step = block_of(n)
            gp, ip = divmod(step, 2)
            if n >= 2:
                pe.wait_ge(s_taken, n - 1)
            for par in range(2):
                rows = slice(HD * par, HD * par + HD)
                bank = 2 * (n % 2) + par
                for i in range(2):
                    lhsT = q[rows, 4 * gp + 2 * ip + i, qc:qc + nq]
                    o = ps[0:nq, bank, 2 * BLK * i:2 * BLK * i + 2 * BLK]
                    if npk == BLK:
                        last = nc.tensor.matmul(o, lhsT, kn[rows, gp, pc:pc + 2 * BLK], start=True, stop=True)
                    else:
                        if npk:
                            nc.tensor.matmul(o[:, k0:BLK], lhsT, kn[rows, gp, pc:pc + npk],
                                             start=True, stop=True)
                        last = nc.tensor.matmul(o[:, BLK:k1], lhsT, kn[rows, gp, qc:qc + nq],
                                                start=True, stop=True)
            last.then_inc(s_done, 1)

        def att_transpose_pe(pe, n):
            (qc, nq), (pc, _, npk), k0, k1, step = block_of(n)
            pe.wait_ge(prob_ready, n + 1)
            if n >= 1:
                pe.wait_ge(pT_ready, n)
            for k in range(4):
                bank = 4 + k // 2
                for part, (c0, nk) in enumerate(((k0, npk), (BLK, nq))):
                    if nk:
                        o = ps[0:nk, bank, (k % 2) * 2 * BLK + part * BLK:][:, 0:nq]
                        last = nc.tensor.transpose(o, prob[n % P_BUFS][0:nq, k, c0:c0 + nk],
                                                   ident[0:nq, 0:nq])
            last.then_inc(t_done, 1)

        def att_values_pe(pe, n):
            (qc, nq), (pc, pt, npk), k0, k1, step = block_of(n)
            b = n // 4
            gp, ip = divmod(step, 2)
            pe.wait_ge(pT_ready, n + 1)
            if n >= 2:
                pe.wait_ge(o_taken, n - 1)
            for par in range(2):
                cols = slice((2 * gp + par) * HD, (2 * gp + par) * HD + HD)
                for i in range(2):
                    k = 2 * par + i
                    o = ps[HD * par:HD * par + HD, 6 + n % 2, BLK * i:BLK * i + nq]
                    if npk:
                        v = v_tok[:, pt, cols] if pt is not None else v_meta[:, cols]
                        nc.tensor.matmul(o, v, probT[0:npk, k, 0, 0:nq], start=True, stop=False)
                    v = v_tok[:, b - 1, cols] if b else v_meta[:, cols]
                    last = nc.tensor.matmul(o, v, probT[0:nq, k, 1, 0:nq], start=npk == 0, stop=True)
            last.then_inc(pv_done, 1)

        def att_pe(pe):
            pe.wait_ge(vmeta_done, 1)
            pe.wait_ge(v_taken, 6)
            for n in range(NG + LAG):
                if n >= LAG:
                    att_transpose_pe(pe, n - LAG)
                if n < NG:
                    att_scores_pe(pe, n)
                if n >= LAG:
                    att_values_pe(pe, n - LAG)

        def att_softmax_dve(dve, n):
            (qc, nq), (pc, _, npk), k0, k1, step = block_of(n)
            b3 = n % P_BUFS
            st = stat[0:nq, b3, :, :]
            dve.wait_ge(s_done, n + 1)
            if n >= P_BUFS:
                dve.wait_ge(t_done, n - P_BUFS + 1)
            src = ps[0:nq, 2 * (n % 2):2 * (n % 2) + 2, :].rearrange("p b (i s) -> p (b i) s", i=2)
            pr = prob[b3][0:nq, :, k0:k1]
            nc.vector.scalar_tensor_tensor(out=pr, in0=src[:, :, k0:k1], scalar=HD ** -0.5,
                                           in1=bias[0:nq, 4 * step:4 * step + 4, k0:k1],
                                           op0=ALU.mult, op1=ALU.add).then_inc(s_taken, 1)
            dve.wait_ge(s_taken, n + 1)
            nc.vector.tensor_reduce(st[:, 0, :], pr, AX, ALU.max).then_inc(max_done, 1)
            dve.wait_ge(max_done, n + 1)
            nc.vector.scalar_tensor_tensor(out=st[:, 1, :], in0=st[:, 0, :], scalar=-1.0,
                                           in1=nsinks[0:nq, 4 * step:4 * step + 4],
                                           op0=ALU.mult, op1=ALU.min).then_inc(negm_done, 1)
            dve.wait_ge(negm_done, n + 1)
            nc.vector.tensor_tensor(st[:, 2, :], sinks[0:nq, 4 * step:4 * step + 4], st[:, 1, :], ALU.add
                                    ).then_inc(logit_done, 1)

        def att_exp_act(act, n):
            (qc, nq), (pc, _, npk), k0, k1, step = block_of(n)
            b3 = n % P_BUFS
            st = stat[0:nq, b3, :, :]
            act.wait_ge(logit_done, n + 1)
            for k in range(4):
                pr = prob[b3][0:nq, k, k0:k1]
                nc.scalar.activation(pr, pr, ACT.Exp, bias=st[:, 1, k:k + 1], accum_out=st[:, 3, k:k + 1])
            nc.scalar.activation(esink[0:nq, b3, :], st[:, 2, :], ACT.Exp).then_inc(exp_done, 1)

        def att_den_dve(dve, n):
            nq = block_of(n)[0][1]
            b3 = n % P_BUFS
            st = stat[0:nq, b3, :, :]
            dve.wait_ge(exp_done, n + 1)
            nc.vector.tensor_tensor(st[:, 3, :], st[:, 3, :], esink[0:nq, b3, :], ALU.add).then_inc(den_done, 1)
            dve.wait_ge(den_done, n + 1)
            nc.vector.reciprocal(st[:, 4, :], st[:, 3, :]).then_inc(rden_done, 1)

        def att_scale_pool(pool, n):
            (qc, nq), (pc, _, npk), k0, k1, step = block_of(n)
            b3 = n % P_BUFS
            pool.wait_ge(rden_done, n + 1)
            pr = prob[b3][0:nq, :, k0:k1]
            nc.gpsimd.tensor_tensor(pr, pr, stat[0:nq, b3, 4, :].unsqueeze(2).to_broadcast([nq, 4, k1 - k0]),
                                    ALU.mult).then_inc(prob_ready, 1)

        def att_pT_act(act, n):
            (qc, nq), (pc, _, npk), k0, k1, step = block_of(n)
            act.wait_ge(t_done, n + 1)
            if n >= 1:
                act.wait_ge(pv_done, n)
            src = ps[:, 4:6, :].rearrange("p b (i c s) -> p (b i) c s", i=2, c=2)
            if npk == BLK:
                nc.scalar.activation(probT[:, :, :, :], src, ACT.Copy).then_inc(pT_ready, 1)
            else:
                if npk:
                    nc.scalar.activation(probT[0:npk, :, 0, 0:nq], src[0:npk, :, 0, 0:nq], ACT.Copy)
                nc.scalar.activation(probT[0:nq, :, 1, 0:nq], src[0:nq, :, 1, 0:nq], ACT.Copy
                                     ).then_inc(pT_ready, 1)

        def o_views(n):
            (qc, nq), _, _, _, step = block_of(n)
            gp, ip = divmod(step, 2)
            c = 4 * gp + 2 * ip
            src = ps[:, 6 + n % 2, 0:2 * BLK].rearrange("p (i s) -> p i s", i=2)[:, :, 0:nq]
            return src, o_hi[:, c:c + 2, qc:qc + nq], o_lo[:, c:c + 2, qc:qc + nq]

        def att_o_act(act, n):
            src, hi, lo = o_views(n)
            act.wait_ge(pv_done, n + 1)
            nc.scalar.activation(hi, src, ACT.Copy).then_inc(o_hi_done, 1)

        def att_o_dve(dve, n):
            src, hi, lo = o_views(n)
            dve.wait_ge(o_hi_done, n + 1)
            nc.vector.tensor_tensor(lo, src, hi.bitcast(F32), ALU.subtract).then_inc(o_taken, 1)

        def att_act(act):
            for n in range(NG + LAG):
                if n >= LAG:
                    att_pT_act(act, n - LAG)
                if 1 <= n <= NG:
                    att_exp_act(act, n - 1)
                if n >= LAG:
                    att_o_act(act, n - LAG)

        def att_dve(dve):
            dve.wait_ge(v_taken, 6)
            nc.vector.tensor_copy(v_meta[:, :], v_tok[SAMPLE:LAST, NBLK, :]).then_inc(vmeta_done, 1)
            dve.wait_ge(bias_in, 16 * 8)
            for n in range(NG + LAG + 1):
                if n == NG // 2:
                    sample_dve(dve)
                if n < NG:
                    att_softmax_dve(dve, n)
                if 1 <= n <= NG:
                    att_den_dve(dve, n - 1)
                if n > LAG:
                    att_o_dve(dve, n - LAG - 1)

        SK = WIN + SAMPLE
        k_raw = at("k_raw", R1 + 544, [P, NB, KH * HD])
        kcT = at("kcT", R1 + 544 + 8192, [P, 2, NB, WIN])
        v_c = at("v_c", R1 + 544 + 16384, [P, NB, KH * HD])
        q_big = at("q_big", R1 + 544 + 24576, [P, 2, NB, 2 * P // NS])
        sb_new = at("sb_new", R4, [P, 4, SK])
        s_prob = at("s_prob", R4 + 2560, [P, 4, SK])
        pcT = at("pcT", R4 + 5120, [P, 4, P])
        pnT = at("pnT", R4 + 5120 + 2048, [SAMPLE, 4, P])
        s_sink = at("s_sink", at_s + 320 + 64 + 64, [P, 1])
        small += [(s_sink[64 * half:64 * half + 64, 0:1],
                   bass.AP(a["attn_sinks"].tensor, 0, [[1, QH], [0, NS], [1, 1]])) for half in range(2)]
        s_stat = at("s_stat", R4 + 5120 + 4096 + 32, [P, 6, 4])
        kc_in, sq_steps, sa_steps, sp_steps = sem("kc_in"), sem("sample_dve"), sem("sample_act"), sem("sample_pe")

        def sample_loads(sp):
            sp.wait_ge(out_ready, 12)
            sp.dma_start(k_raw[:, :, :], a["cache_k"][0].rearrange("b s h d -> s b (h d)")).then_inc(kc_in, 16)
            sp.dma_start(v_c[:, :, :], a["cache_v"][0].rearrange("b s h d -> s b (h d)")).then_inc(kc_in, 16)
            sp.wait_ge(line_out, 16)
            for half in range(2):
                sp.dma_start(s_bias[64 * half:64 * half + 64, :],
                               line_src(BLK - 1, [[BLK * LINE, QH], [LINE - 1, NS], [1, WIN + NS]])
                               ).then_inc(kc_in, 16)

        def sample_dve(dve):
            step = [0]

            def inc(ins):
                step[0] += 1
                ins.then_inc(sq_steps, 1)
                return step[0]

            def after(k):
                dve.wait_ge(sq_steps, k)

            dve.wait_ge(out_ready, 12)
            z = inc(nc.vector.memset(q_big[:, :, :, :], 0.0))
            after(z)
            for gp in range(2):
                for par in range(2):
                    g = 2 * gp + par
                    rows = slice(HD * par, HD * par + HD)
                    dst = q_big[rows, gp, :, 16 * g:16 * g + 16].rearrange("p b (c i) -> p b c i", i=NS)
                    src = q[rows, 4 * gp:4 * gp + 4, COL_S:COL_M].rearrange("p c (b i) -> p b c i", i=NS)
                    inc(nc.vector.tensor_copy(dst, src))
            assert step[0] == 5

        def sample_dve2(dve):
            step = [5]

            def inc(ins):
                step[0] += 1
                ins.then_inc(sq_steps, 1)
                return step[0]

            def after(k):
                dve.wait_ge(sq_steps, k)

            caches_dve(dve)
            for j in range(4):
                dve.wait_ge(sp_steps, j + 1)
                dst = kcT[:, j // 2, 4 * (j % 2):4 * (j % 2) + 4, :]
                inc(nc.vector.tensor_copy(dst, ps[:, j, :].rearrange("p (b s) -> p b s", b=4)))
            dve.wait_ge(kc_in, 64)
            dve.wait_ge(t_done, NG)
            m = inc(nc.vector.memset(sb_new[:, :, WIN:SK], NEG))
            inc(nc.vector.tensor_copy(sb_new[:, :, 0:WIN],
                                      s_bias[:, 0:WIN].unsqueeze(1).to_broadcast([P, 4, WIN])))
            after(m)
            for b in range(NB):
                rows = slice(64 * (b % 2), 64 * (b % 2) + 64)
                inc(nc.vector.tensor_copy(sb_new[rows, b // 2, WIN + NS * b:WIN + NS * b + NS],
                                          s_bias[rows, WIN:WIN + NS]))
            after(step[0])
            dve.wait_ge(sp_steps, 5)
            sc = ps[:, 4:6, :].rearrange("p b (i s) -> p (b i) s", i=2)[:, :, 0:SK]
            k = inc(nc.vector.scalar_tensor_tensor(out=s_prob[:, :, :], in0=sc, scalar=HD ** -0.5,
                                                   in1=sb_new[:, :, :], op0=ALU.mult, op1=ALU.add))
            after(k)
            k = inc(nc.vector.tensor_reduce(s_stat[:, 0, :], s_prob[:, :, :], AX, ALU.max))
            after(k)
            sink4 = s_sink[:, 0:1].to_broadcast([P, 4])
            k = inc(nc.vector.tensor_tensor(s_stat[:, 0, :], s_stat[:, 0, :], sink4, ALU.max))
            after(k)
            k = inc(nc.vector.tensor_scalar(s_stat[:, 1, :], s_stat[:, 0, :], -1.0, None, ALU.mult))
            after(k)
            k = inc(nc.vector.tensor_tensor(s_stat[:, 2, :], s_stat[:, 1, :], sink4, ALU.add))
            assert k == 24, k
            dve.wait_ge(sa_steps, 1)
            k = inc(nc.vector.tensor_tensor(s_stat[:, 3, :], s_stat[:, 3, :], s_stat[:, 4, :], ALU.add))
            after(k)
            k = inc(nc.vector.reciprocal(s_stat[:, 5, :], s_stat[:, 3, :]))
            after(k)
            k = inc(nc.vector.tensor_tensor(s_prob[:, :, :], s_prob[:, :, :],
                                            s_stat[:, 5, :].unsqueeze(2).to_broadcast([P, 4, SK]), ALU.mult))
            assert k == 27, k
            dve.wait_ge(sp_steps, 6)
            k = inc(nc.vector.tensor_copy(pnT[:, :, :], ps[0:SAMPLE, 7, :].rearrange("p (t r) -> p t r", t=4)))
            assert k == 28
            dve.wait_ge(sa_steps, 3)
            for gp in range(2):
                src, hi, lo = sample_o(gp)
                inc(nc.vector.tensor_tensor(lo, src, hi.bitcast(F32), ALU.subtract))
            assert step[0] == 30

        def sample_o(gp):
            src = ps[:, 0, P * gp:P * gp + P].rearrange("p (b c i) -> p b c i", b=NB, i=NS)
            hi, lo = (o[:, 4 * gp:4 * gp + 4, COL_S:COL_M].rearrange("p c (b i) -> p b c i", i=NS)
                      for o in (o_hi, o_lo))
            return src, hi, lo

        def sample_act(act):
            act.wait_ge(sq_steps, 24)
            for t in range(4):
                nc.scalar.activation(s_prob[:, t, :], s_prob[:, t, :], ACT.Exp, bias=s_stat[:, 1, t:t + 1],
                                     accum_out=s_stat[:, 3, t:t + 1])
            nc.scalar.activation(s_stat[:, 4, :], s_stat[:, 2, :], ACT.Exp).then_inc(sa_steps, 1)
            act.wait_ge(sp_steps, 6)
            nc.scalar.activation(pcT[:, :, :], ps[:, 6, :].rearrange("p (t r) -> p t r", t=4), ACT.Copy
                                 ).then_inc(sa_steps, 1)
            act.wait_ge(sp_steps, 7)
            for gp in range(2):
                src, hi, lo = sample_o(gp)
                last = nc.scalar.activation(hi, src, ACT.Copy)
            last.then_inc(sa_steps, 1)

        def sample_pe(pe):
            pe.wait_ge(o_taken, NG)
            caches_pe(pe)
            pe.wait_ge(kc_in, 64)
            for j in range(4):
                for i in range(4):
                    b = 4 * (j % 2) + i
                    last = nc.tensor.transpose(ps[:, j, P * i:P * i + P],
                                               k_raw[:, b, P * (j // 2):P * (j // 2) + P], ident)
                last.then_inc(sp_steps, 1)
            pe.wait_ge(sq_steps, 9)
            for b in range(NB):
                o = ps[64 * (b % 2):64 * (b % 2) + 64, 4 + b // 4, 256 * (b // 2 % 2):256 * (b // 2 % 2) + SK]
                for c, ncol, keys in ((0, WIN, lambda gp: kcT[:, gp, b, :]),
                                      (WIN, SAMPLE, lambda gp: kn[:, gp, COL_S:COL_M])):
                    for gp in range(2):
                        last = nc.tensor.matmul(o[:, c:c + ncol], q_big[:, gp, b, :], keys(gp),
                                                start=gp == 0, stop=gp == 1)
            last.then_inc(sp_steps, 1)
            pe.wait_ge(sq_steps, 27)
            pe.wait_ge(cache_c, 2)
            for t in range(4):
                nc.tensor.transpose(ps[:, 6, P * t:P * t + P], s_prob[:, t, 0:WIN], ident)
                last = nc.tensor.transpose(ps[0:SAMPLE, 7, P * t:P * t + P], s_prob[:, t, WIN:SK], ident)
            last.then_inc(sp_steps, 1)
            pe.wait_ge(sq_steps, 28)
            pe.wait_ge(sa_steps, 2)
            for g in range(KH):
                gp, par = divmod(g, 2)
                for b in range(NB):
                    r = 64 * (b % 2) + 16 * g
                    o = ps[HD * par:HD * par + HD, 0, P * gp + 16 * b:P * gp + 16 * b + 16]
                    cols = slice(HD * g, HD * g + HD)
                    nc.tensor.matmul(o, v_c[:, b, cols], pcT[:, b // 2, r:r + 16], start=True, stop=False)
                    last = nc.tensor.matmul(o, v_tok[0:SAMPLE, NBLK, cols], pnT[:, b // 2, r:r + 16],
                                            start=False, stop=True)
            last.then_inc(sp_steps, 1)

        def add_x_dve(dve, n, f, x):
            dve.wait_ge(out_ready, n + 1)
            nc.vector.tensor_tensor(grp(x[:, f, :]), grp(x[:, f, :]), ps[:, out_banks(n):out_banks(n) + 3, 0:TG],
                                    ALU.add).then_inc(out_free, 1)

        def reload_x(sp):
            sp.wait_ge(sp_steps, 7)
            sp.wait_ge(kv_out, 16 * 20)
            for f in range(KC):
                sp.dma_start(x[:, f, :], scratch["x0"][:, f, :]).then_inc(x_back, 16)

        def wo_pe(pe):
            pe.wait_ge(sq_steps, 30)
            for c in range(KC):
                pe_unit(pe, U_WO + c, N_WO + c, o_hi, o_lo)

        def project_act(act, u0, n0, m, x, h_hi):
            for c in range(KC):
                split_hi_static(act, u0 + c + AHEAD)
                act.wait_ge(out_free, n0 + c + 1)
                norm_act(act, m, c, x, h_hi)

        def project_dve(dve, u0, n0, m, x, h_hi, h_lo, back):
            for c in range(KC):
                split_lo_static(dve, u0 + c + AHEAD)
                if c >= 2:
                    norm_acc_dve(dve, m, c - 1)
                if c == 0:
                    dve.wait_ge(back, 16 * KC)
                add_x_dve(dve, n0 + c, c, x)
            norm_acc_dve(dve, m, KC - 1)
            dve.wait_ge(out_ready, n0 + KC)
            for c in range(KC):
                norm_lo_dve(dve, m, c, x, h_hi, h_lo)

        def mlp_slice_sp(sp, layer, u0, i):
            r0 = u0 // 2
            up = a["mlp_w_up"][layer].rearrange("(k p) n -> p k n", p=P)
            down = a["mlp_w_down"][layer].rearrange("(s p) n -> p s n", p=P)
            for j in range(4):
                slot = (r0 + j) % 2
                sp.wait_ge(w_lo_ready, i * 8 + (2 * (r0 + j) - 2))
                if j < 2:
                    src = up[:, :, bass.ds(i * 512 + 256 * j, 256)]
                    sp.dma_start(raw_k8[:, slot, :, :], src).then_inc(raw_in[slot], 16)
                else:
                    src = down[:, bass.ds(i * 4, 4), 512 * (j - 2):512 * (j - 2) + 512]
                    sp.dma_start(raw_k4[:, slot, :, :], src).then_inc(raw_in[slot], 16)

        def local_outs(j):
            return j + 1 if j < 4 else 2 * j - 2

        def mlp_raw_wait(u0, i, j):
            r = u0 // 2 + j // 2
            base = raw_target(u0 // 2 + (j // 2) % 2 - 2)
            return r % 2, i * 32 + (base + 16 * (j // 4 + 1))

        def mlp_split_hi(act, u0, n0, i, j):
            jj = j + AHEAD
            rslot, rwait = mlp_raw_wait(u0, i, jj)
            done = (n0 - 1, n0)[j] if j < 2 else n0 + local_outs(j - 2)
            split_hi(act, (u0 + jj) % 4, rslot, jj % 2, 4 <= jj < 8, rwait, i * 12 + done)

        def mlp_split_lo(dve, u0, i, j):
            jj = j + AHEAD
            split_lo(dve, (u0 + jj) % 4, (u0 // 2 + jj // 2) % 2, jj % 2, 4 <= jj < 8, i * 8 + (u0 + jj + 1))

        def mlp_slice_act(act, layer, u0, n0, i, prefetch=8, norm=None):
            ups = 4 * SLICES * layer
            for j in range(8):
                if j < prefetch:
                    mlp_split_hi(act, u0, n0, i, j)
                if j < 4:
                    act.wait_ge(out_free, i * 12 + (n0 + j + 1))
                    nc.scalar.activation(act_hi[:, j, :], relu[j % 2][:, :], ACT.Square).then_inc(up_done, 1)
                elif norm:
                    for o in (2 * j - 8, 2 * j - 7):
                        act.wait_ge(out_free, i * 12 + (n0 + 5 + o))
                        if o == 0:
                            act.wait_ge(act_split, i * 4 + (ups + 4))
                        norm_act(act, norm[0], o, norm[1], norm[2])

        def mlp_slice_dve(dve, layer, u0, n0, i, x, prefetch=8, norm=None):
            ups = 4 * SLICES * layer
            for j in range(8):
                if j < prefetch:
                    mlp_split_lo(dve, u0, i, j)
                if j < 4:
                    n = n0 + j
                    dve.wait_ge(out_ready, i * 12 + (n + 1))
                    nc.vector.scalar_tensor_tensor(out=grp(relu[j % 2][:, :]),
                                                   in0=ps[:, out_banks(n):out_banks(n) + 3, 0:TG], scalar=0.0,
                                                   in1=rstd[:, :, :], op0=ALU.max, op1=ALU.mult
                                                   ).then_inc(out_free, 1)
                    dve.wait_ge(out_free, i * 12 + (n + 1))
                    if j:
                        dve.wait_ge(act_split, i * 4 + (ups + j))
                    nc.vector.tensor_tensor(relu_sq[:, :], relu[j % 2][:, :], relu[j % 2][:, :], ALU.mult
                                            ).then_inc(sq_done, 1)
                    dve.wait_ge(sq_done, i * 4 + (ups + j + 1))
                    dve.wait_ge(up_done, i * 4 + (ups + j + 1))
                    nc.vector.tensor_tensor(act_lo[:, j, :], relu_sq[:, :], act_hi[:, j, :].bitcast(F32),
                                            ALU.subtract).then_inc(act_split, 1)
                else:
                    for o in (2 * j - 8, 2 * j - 7):
                        n = n0 + 4 + o
                        dve.wait_ge(out_ready, i * 12 + (n + 1))
                        dve.wait_ge(out_free, i * 12 + (n0 + o - 7))
                        nc.vector.tensor_tensor(grp(x[:, o, :]), grp(x[:, o, :]),
                                                ps[:, out_banks(n):out_banks(n) + 3, 0:TG], ALU.add
                                                ).then_inc(out_free, 1)
                        if norm and o:
                            if o >= 2:
                                norm_acc_dve(dve, norm[0], o - 1)
                            norm_lo_dve(dve, norm[0], o - 1, *norm[1:])
            if norm:
                norm_acc_dve(dve, norm[0], KC - 1)
                norm_lo_dve(dve, norm[0], KC - 1, *norm[1:])

        def mlp_slice_pe(pe, layer, u0, n0, i, h_hi, h_lo):
            ups = 4 * SLICES * layer
            for j in range(8):
                pe.wait_ge(w_lo_ready, i * 8 + (u0 + j + 1))
                slot = (u0 + j) % 4
                deep, hi, lo = (8, h_hi, h_lo) if j < 4 else (4, act_hi, act_lo)
                for c in range(1 if j < 4 else 2):
                    o = j if j < 4 else 4 + 2 * (j - 4) + c
                    pe.wait_ge(out_free, i * 12 + (n0 + o - 1))
                    for k in range(deep):
                        if o == 0:
                            pe.wait_ge(norm_hi, KC * (2 * layer + 1) + k + 1)
                        if o == 4:
                            pe.wait_ge(act_split, i * 4 + (ups + k + 1))
                        pass_hi(slot, k, deep, slice(P * c, P * c + P), out_banks(n0 + o), hi, k == 0)
                    for k in range(deep):
                        if o == 0:
                            pe.wait_ge(norm_lo, KC * (2 * layer + 1) + k + 1)
                        last = pass_lo(slot, k, deep, slice(P * c, P * c + P), out_banks(n0 + o), lo, k == deep - 1)
                    last.then_inc(out_ready, 1)

        ROWB = 4320
        at_g = at_s + 320 + 64
        t_i, t_f, b_row, jump, m_rel, m_abs, m_prev, keep = (
            at(nm, R0 + i * ROWB, [MH, TP]) for i, nm in enumerate(
                ["t_i", "t_f", "b_row", "jump", "m_rel", "m_abs", "m_prev", "keep"]))
        u_s = at("u_s", R0 + 8 * ROWB, [MH, SAMPLE])
        m0 = at("m0", R0 + 8 * ROWB + 128, [MH, NB])
        wg_raw = at("wg_raw", at_g + 96, [P, KC, 2 * MH])
        wg_hi = at("wg_hi", R0 + 34368, [P, KC, 64 + MH], F32R)
        wg_lo = at("wg_lo", at_c + 352, [P, KC, 64 + MH], F32R)
        rows_u = at("rows_u", R4, [P, TP])
        rows_m = at("rows_m", R4 + BUF, [P, TP])
        stage = at("stage", R4 + 3 * BUF, [P, TP])
        v_m = at("v_m", R4 + 2 * BUF, [META, MH, VH])
        qk = at("qk", R3, [P, KC, TP])
        v = at("v", R0, [P, TILES, MH, VH])
        c0 = at("c0", R0, [P, NB, MH, VH])
        og = at("og", R1, [P, KC, TP])
        y_hi = at("y_hi", R3, [P, KC, TP], F32R)
        y_lo = at("y_lo", R1, [P, KC, TP], F32R)
        x2 = at("x2", R2, [P, KC, TP])
        h_hi2 = at("h_hi2", R0, [P, KC, TP], F32R)
        h_lo2 = at("h_lo2", R1, [P, KC, TP], F32R)
        names = ["rr", "decay", "sw", "kts", "qs", "e_sb", "dd", "zr"]
        rr, decay, sw, kts, qs, e_sb, dd, zr = (at(nm, R2 + 2048 * i, [P, MH, P]) for i, nm in enumerate(names))
        nsq = at("nsq", R2 + 16384, [P, MH, 2, P])
        numr = at("numr", R2 + 16384 + 4096, [P, MH, 2, P])
        cst_ = at("c_state", R2 + 16384 + 8192, [P, MH, VH])
        a_sb = at("a_sb", R2 + 16384 + 8192 + 4128, [P, MH])
        a_s = at("a_s", R2 + 16384 + 8192 + 4128 + 32, [P, MH, SAMPLE])
        bgate = at("bgate", at_g, [MH, 2])
        bg15 = at("bg15", at_g + 32, [MH, 2])
        pair = cst[:, slice(*CONST_AT["pair"])]

        def row_of(k):
            return ident[:, k:k + 1].to_broadcast([P, P])

        causal = cst[:, slice(*CONST_AT["causal"])]
        own_causal = cst[:, slice(*CONST_AT["own_causal"])]
        small += [(bgate[:, :], a["mlstm_b_gate"][0].rearrange("(g h) -> h g", g=2)),
                  (wg_raw[:, :, :], a["mlstm_w_gate"][0].rearrange("(k p) n -> p k n", p=P))]
        wg_cols = [(slice(0, MH), slice(0, MH)), (slice(64, 64 + MH), slice(MH, 2 * MH))]

        wg_zero, wg_split_hi, wg_split = sem("wg_zero"), sem("wg_split_hi"), sem("wg_split")
        keep_in, gate_dve, gate_act = sem("keep_in"), sem("gate_dve"), sem("gate_act")
        vt2_ready, v2_taken, og_done, og_out, n_in = (sem(s) for s in
            ("vt2_ready", "v2_taken", "og_done", "og_out", "n_in"))
        og_in = [sem(f"og_in{i}") for i in range(3)]
        o_sig = sem("o_sig")
        v_ones, vm_done = sem("v_ones"), sem("vm_done")
        (rr_ready, kT_ready, st_ready, d_ready, decay_ready, sw_ready, kts_ready, bc_ready, qs_ready, e_ready,
         num_ready, dd_step, nsq_ready, ss_ready, z_ready, ln_z, r_ready, numr_ready, y_ready, yhi_ready, ylo_ready,
         cup_ready, c_new) = (sem(s) for s in (
             "rr_ready", "kT_ready", "st_ready", "d_ready", "decay_ready", "sw_ready", "kts_ready", "bc_ready",
             "qs_ready", "e_ready", "num_ready", "dd_step", "nsq_ready", "ss_ready", "z_ready", "ln_z", "r_ready",
             "numr_ready", "y_ready", "yhi_ready", "ylo_ready", "cup_ready", "c_new"))
        abs_ready = sem("abs_ready")
        c0_in, sm_pe, sm_dve, sm_act, c0_out = (sem(s) for s in ("c0_in", "sm_pe", "sm_dve", "sm_act", "c0_out"))
        x2_back = sem("x2_back")

        def gates_pool(pool):
            pool.wait_ge(out_free, N_IN)
            pool.dma_start(scratch["x1"], x[:, :, :]).then_inc(x1_saved, 16)
            pool.wait_ge(x1_saved, 16)
            pool.wait_ge(norm_lo, 3 * KC)
            pool.wait_ge(norm_sq, 3 * KC)
            pool.wait_ge(out_ready, N_IN + 1)
            pool.dma_start(keep[:, :], a["keep"]).then_inc(keep_in, 16)
            pool.dma_start(m0[:, :], a["state_m"][0].rearrange("b h -> h b"),
                           allow_slow_non_contiguous=True).then_inc(keep_in, 16)

        def gates_pe(pe):
            n = N_IN
            pe.wait_ge(wg_split, 1)
            pe.wait_ge(out_free, n - 1)
            for k in range(KC):
                pe.wait_ge(norm_lo, 2 * KC + k + 1)
                if k in (4, 5, 6):
                    norm_pe(pe, 2, k - 4)
                for g in range(3):
                    o = ps[0:64 + MH, out_banks(n) + g, 0:TG]
                    c = slice(g * TG, g * TG + TG)
                    nc.tensor.matmul(o, wg_hi[:, k, :], h_hi[:, k, c], start=k == 0, stop=False)
                    nc.tensor.matmul(o, wg_hi[:, k, :], h_lo[:, k, c], start=False, stop=False)
                    last = nc.tensor.matmul(o, wg_lo[:, k, :], h_hi[:, k, c], start=False, stop=k == KC - 1)
            last.then_inc(out_ready, 1)

        def gates_act1(act):
            act.wait_ge(gate_dve, 1)
            act.wait_ge(out_free, N_IN + 1)
            for i, t in enumerate((t_i, t_f)):
                last = nc.scalar.activation(t[:, :], t[:, :], ACT.Tanh, scale=1.0 / CAP, bias=bg15[:, i:i + 1])
            last.then_inc(gate_act, 1)
            act.preload_act_table_set("natural_log_exp_and_others")
            act.wait_ge(gate_act, 1)
            nc.scalar.activation(t_f[:, :], t_f[:, :], ACT.Exp, scale=-CAP).then_inc(gate_act, 1)
            act.wait_ge(gate_act, 2)
            nc.scalar.activation(t_f[:, :], t_f[:, :], ACT.Ln, bias=1.0).then_inc(gate_act, 1)

        def gates_dve(dve):
            dve.wait_ge(out_ready, N_IN + 1)
            dve.wait_ge(norm_rstd, 3)
            dve.wait_ge(x1_saved, 16)
            dve.wait_ge(norm_sq, 3 * KC)
            nc.vector.tensor_tensor(grp(t_i[:, :]), ps[0:MH, out_banks(N_IN):out_banks(N_IN) + 3, 0:TG],
                                    rstd[0:MH, :, :], ALU.mult).then_inc(gate_dve, 1)
            nc.vector.tensor_tensor(grp(t_f[:, :]), ps[64:64 + MH, out_banks(N_IN):out_banks(N_IN) + 3, 0:TG],
                                    rstd[64:64 + MH, :, :], ALU.mult).then_inc(out_free, 1)

        def gates_dve2(dve):
            step = [1]

            def do(ins):
                step[0] += 1
                ins.then_inc(gate_dve, 1)
                dve.wait_ge(gate_dve, step[0])

            dve.wait_ge(norm_summed, 9)
            do(nc.vector.memset(rows_u[:, :], 0.0))
            do(nc.vector.memset(rows_m[:, :], 0.0))
            do(nc.vector.memset(rows_u[32:32 + MH, :], 1.0))
            do(nc.vector.memset(rows_m[0:MH, :], 1.0))
            dve.wait_ge(x1_saved, 16)
            do(nc.vector.memset(jump[:, :], 0.0))
            do(nc.vector.memset(m_prev[:, COL_M:T], 0.0))
            dve.wait_ge(keep_in, 32)
            dve.wait_ge(gate_act, 3)
            do(nc.vector.tensor_tensor_scan(b_row[:, 0:T], keep[:, 0:T], t_f[:, 0:T], 0.0, ALU.mult, ALU.subtract))
            u = rows_u[0:MH, 0:T]
            do(nc.vector.scalar_tensor_tensor(out=u, in0=t_i[:, 0:T], scalar=CAP, in1=b_row[:, 0:T],
                                              op0=ALU.mult, op1=ALU.subtract))
            do(nc.vector.tensor_copy(jump[:, BLK:SEQ:BLK], b_row[:, BLK - 1:SEQ - 1:BLK]))
            do(nc.vector.tensor_copy(jump[:, 0:1], b_row[:, T - 1:T]))
            do(nc.vector.memset(jump[:, COL_S:COL_M:NS], NEG))
            do(nc.vector.tensor_copy(u_s[:, :], rows_u[0:MH, COL_S:COL_M]))
            do(nc.vector.tensor_tensor(u_s[:, 0:SAMPLE:NS], u_s[:, 0:SAMPLE:NS], m0[:, :], ALU.max))
            do(nc.vector.tensor_tensor_scan(m_rel[:, COL_M:T], jump[:, COL_M:T], rows_u[0:MH, COL_M:T], 0.0,
                                            ALU.add, ALU.max))
            do(nc.vector.tensor_tensor_scan(m_rel[:, 0:SEQ], jump[:, 0:SEQ], rows_u[0:MH, 0:SEQ],
                                            m_rel[:, T - 1:T], ALU.add, ALU.max))
            do(nc.vector.tensor_tensor_scan(m_rel[:, COL_S:COL_M], jump[:, COL_S:COL_M], u_s[:, :], 0.0,
                                            ALU.add, ALU.max))
            do(nc.vector.tensor_tensor(m_abs[:, 0:T], m_rel[:, 0:T], b_row[:, 0:T], ALU.add))
            do(nc.vector.tensor_copy(m_prev[:, 0:BLK], m_abs[:, T - 1:T].to_broadcast([MH, BLK])))
            do(nc.vector.tensor_copy(m_prev[:, BLK:SEQ].rearrange("p (c n) -> p c n", n=BLK),
                                     m_abs[:, BLK - 1:SEQ - 1:BLK].unsqueeze(2).to_broadcast([MH, NBLK - 1, BLK])))
            do(nc.vector.tensor_copy(m_prev[:, COL_S:COL_M].rearrange("p (b n) -> p b n", n=NS),
                                     m0[:, :].unsqueeze(2).to_broadcast([MH, NB, NS])))
            do(nc.vector.tensor_tensor(m_prev[:, 0:T], m_prev[:, 0:T], m_rel[:, 0:T], ALU.subtract))
            do(nc.vector.tensor_scalar(rows_m[32:32 + MH, 0:T], m_rel[:, 0:T], -1.0, None, ALU.mult))
            return step[0]
        GATE_STEPS = 23

        def gates_act2(act):
            act.wait_ge(gate_dve, GATE_STEPS)
            nc.scalar.activation(rows_m[64:64 + MH, 0:T], m_prev[:, 0:T], ACT.Exp)
            nc.scalar.activation(rows_m[96:96 + MH, 0:T], m_abs[:, 0:T], ACT.Exp, scale=-1.0).then_inc(gate_act, 1)

        def gates_out(pool):
            pool.wait_ge(gate_dve, GATE_STEPS)
            pool.dma_start(out[8][0].rearrange("b h -> h b"), m_abs[:, SEQ - 1:SEQ],
                           allow_slow_non_contiguous=True).then_inc(stored, 16)
            pool.dma_start(out[11][0].rearrange("b h -> h b"), m_abs[:, COL_S + NS - 1:COL_M:NS],
                           allow_slow_non_contiguous=True).then_inc(stored, 16)

        def in_side_pe(pe, vc, g):
            s = 3 * vc + g
            if s >= 2:
                pe.wait_ge(v2_taken, s - 1)
            pe.wait_ge(out_free, N_IN + 1 + 8 + vc + 1)
            for t in range(4 * g, min(4 * g + 4, TILES)):
                n = x_rows(t)
                last = nc.tensor.transpose(ps[0:n, side_bank(s), (t % 4) * P:(t % 4) * P + P],
                                           stage[:, t * P:t * P + n], ident)
            last.then_inc(vt2_ready, 1)

        def in_pe(pe):
            for c in range(24):
                sides = (lambda g, c=c: in_side_pe(pe, c - 9, g)) if 9 <= c < 17 else None
                pe_unit(pe, U_IN + c, N_IN + 1 + c, h_hi, h_lo, sides)

        def in_side_dve(dve, vc):
            if vc == 0:
                dve.wait_ge(gate_act, 4)
                dve.wait_ge(stored, 16 * 2)
                nc.vector.memset(v[SAMPLE:64, NBLK, :, :], 0.0).then_inc(v_ones, 1)
                dve.wait_ge(v_ones, 1)
                nc.vector.memset(v[:, :, :, DV:VH], 1.0)
            for g in range(3):
                dve.wait_ge(vt2_ready, 3 * vc + g + 1)
                n, tiles = (P, 4) if g < 2 else (LAST, 1)
                nc.vector.tensor_copy(
                    v[0:n, 4 * g:4 * g + tiles, vc // 2, P * (vc % 2):P * (vc % 2) + P],
                    ps[0:n, side_bank(3 * vc + g), :].rearrange("p (t n) -> p t n", t=4)[:, 0:tiles, :]
                ).then_inc(v2_taken, 1)

        def in_act(act):
            for c in range(24):
                split_hi_static(act, U_IN + c + AHEAD)
                if c == 0:
                    gates_act1(act)
                if c == 1:
                    gates_act2(act)
                if c >= 16:
                    act.wait_ge(out_free, N_IN + c + 2)
                    nc.scalar.activation(stage[:, :], stage[:, :], ACT.Sigmoid).then_inc(o_sig, 1)

        def in_dve(dve):
            for c in range(24):
                n = N_IN + 1 + c
                split_lo_static(dve, U_IN + c + AHEAD)
                if 9 <= c < 17:
                    in_side_dve(dve, c - 9)
                dve.wait_ge(out_ready, n + 1)
                if c > 16:
                    dve.wait_ge(og_out, 16 * (c - 16))
                if c < 8:
                    times_rstd(grp(qk[:, c, :]), n, 1.0 if c < MH else DK ** -0.5)
                else:
                    times_rstd(grp(stage[:, :]), n)
                if c == 0:
                    got = gates_dve2(dve)
                    assert got == GATE_STEPS, got
                if c >= 16:
                    oc = c - 16
                    dve.wait_ge(o_sig, oc + 1)
                    nc.vector.tensor_scalar(stage[:, :], stage[:, :], gains[:, 4, oc:oc + 1], None, ALU.mult
                                            ).then_inc(og_done, 1)

        def og_pool(pool):
            for oc in range(KC):
                pool.wait_ge(og_done, oc + 1)
                if oc:
                    pool.wait_ge(og_out, 16 * oc)
                pool.dma_start(scratch["og"][:, oc, :], stage[:, :]).then_inc(og_out, 16)

        OG_PARTS = (slice(COL_S, T), slice(0, SEQ // 2), slice(SEQ // 2, SEQ))

        def og_load(sp):
            sp.wait_ge(og_out, 16 * KC)
            sp.wait_ge(out_ready, N_OUT)
            for i, cols in enumerate(OG_PARTS):
                sp.dma_start(og[:, :, cols], scratch["og"][:, :, cols]).then_inc(og_in[i], 16)
            sp.dma_start(n_rows[0:NB * MH, :], a["state_n"][0].rearrange("b h k -> (b h) k")).then_inc(n_in, 16)

        def chunk_of(c):
            return (COL_M, META) if c == 0 else (BLK * (c - 1), BLK)

        def hview(bank, n, rows=P):
            return ps[0:rows, bank, 0:MH * n].rearrange("p (h n) -> p h n", h=MH)

        CB = (0, 1, 3, 4)

        def keys_pe(pe, c):
            col, n = chunk_of(c)
            cs = slice(col, col + n)
            if c:
                pe.wait_ge(c_new, 4 * c - 2)
            for h in range(MH):
                last = nc.tensor.transpose(ps[0:n, 0, P * h:P * h + P], qk[:, MH + h, cs], ident)
            last.then_inc(kT_ready, 1)
            for h in range(MH):
                last = nc.tensor.matmul(ps[0:n, 1, n * h:n * h + n], qk[:, MH + h, cs], qk[:, h, cs],
                                        start=True, stop=True)
            last.then_inc(st_ready, 1)

        def exponents_pe(pe, c):
            col, n = chunk_of(c)
            cs = slice(col, col + n)
            if c:
                pe.wait_ge(decay_ready, c)
            pe.wait_ge(rr_ready, c + 1)
            nc.tensor.matmul(ps[0:n, 2, 0:MH * n], ident[0:n, 0:n],
                             causal[0:n, 0:n].unsqueeze(1).to_broadcast([n, MH, n]), start=True, stop=False)
            for h in range(MH):
                last = nc.tensor.matmul(ps[0:n, 2, n * h:n * h + n], rows_u[0:64, cs], rr[0:64, h, 0:n],
                                        start=False, stop=h == MH - 1)
            last.then_inc(d_ready, 1)

        def rows_pe(pe, c):
            col, n = chunk_of(c)
            cs = slice(col, col + n)
            if c:
                pe.wait_ge(c_new, 4 * c)
            for w in range(2):
                for h in range(MH):
                    last = nc.tensor.matmul(ps[:, 3 + w, n * h:n * h + n], row_of(64 + 32 * w + h),
                                            rows_m[:, cs], start=True, stop=True)
            last.then_inc(bc_ready, 1)

        def outputs_pe(pe, c):
            col, n = chunk_of(c)
            vals = (lambda h, k0, k1: v_m[:, h, k0:k1]) if c == 0 else (lambda h, k0, k1: v[:, c - 1, h, k0:k1])
            pe.wait_ge(sw_ready, c + 1)
            if c:
                pe.wait_ge(numr_ready, c)
                pe.wait_ge(z_ready, c)
                pe.wait_ge(qs_ready, c + 1)
            for h in range(MH):
                for half in range(2):
                    o = ps[:, 5 + h // 2, (2 * (h % 2) + half) * n:][:, 0:n]
                    nc.tensor.matmul(o, vals(h, P * half, P * half + P), sw[0:n, h, 0:n],
                                     start=True, stop=c == 0)
                    if c:
                        nc.tensor.matmul(o, cst_[:, h, P * half:P * half + P], qs[:, h, 0:n],
                                         start=False, stop=True)
            if n == BLK:
                nc.tensor.matmul(ps[:, 7, :], ones[0:n, :], sw[0:n, :, :].rearrange("p h n -> p (h n)"),
                                 start=True, stop=False)
                for h in range(MH):
                    last = nc.tensor.matmul(ps[:, 7, n * h:n * h + n], cst_[:, h, DV:VH].to_broadcast([P, P]),
                                            qs[:, h, :], start=False, stop=h == MH - 1)
            else:
                last = nc.tensor.matmul(ps[:, 7, 0:MH * n], ones[0:n, :], sw[0:n, :, 0:n], start=True, stop=True)
            last.then_inc(num_ready, 1)

        def states_pe(pe, c):
            col, n = chunk_of(c)
            vals = (lambda h: v_m[:, h, :]) if c == 0 else (lambda h: v[:, c - 1, h, :])
            pe.wait_ge(kts_ready, c + 1)
            pe.wait_ge(qs_ready, c + 1)
            pe.wait_ge(e_ready, c + 1)
            for h in range(MH):
                nc.tensor.matmul(ps[:, CB[h], 0:VH], kts[0:n, h, :], vals(h), start=True, stop=True
                                 ).then_inc(cup_ready, 1)

        def squares_pe(pe, c):
            col, n = chunk_of(c)
            pe.wait_ge(abs_ready, c + 1)
            pe.wait_ge(nsq_ready, c + 1)
            for half in range(2):
                last = nc.tensor.matmul(ps[:, 7, 0:MH * n], ones, nsq[:, :, half, 0:n], start=half == 0,
                                        stop=half == 1)
            last.then_inc(ss_ready, 1)

        def chunks_pe(pe):
            exponents_pe(pe, 0)
            keys_pe(pe, 0)
            rows_pe(pe, 0)
            for c in range(TILES):
                outputs_pe(pe, c)
                states_pe(pe, c)
                squares_pe(pe, c)
                if c < NBLK:
                    exponents_pe(pe, c + 1)
                    rows_pe(pe, c + 1)
                    keys_pe(pe, c + 1)

        def num_banks(bank, n):
            return ps[:, bank, 0:4 * n].rearrange("p (h c n) -> p h c n", h=2, c=2)

        def rr_dve(dve, c):
            col, n = chunk_of(c)
            if c:
                dve.wait_ge(d_ready, c)
            nc.vector.tensor_tensor(rr[0:64, :, 0:n],
                                    rows_m[0:64, col:col + n].unsqueeze(1).to_broadcast([64, MH, n]),
                                    pair[0:64, :].unsqueeze(2).to_broadcast([64, MH, n]),
                                    ALU.mult).then_inc(rr_ready, 1)

        def scores_dve(dve, c):
            col, n = chunk_of(c)
            dve.wait_ge(st_ready, c + 1)
            dve.wait_ge(decay_ready, c + 1)
            if c:
                dve.wait_ge(num_ready, c)
            nc.vector.tensor_tensor(sw[0:n, :, 0:n], hview(1, n, n), decay[0:n, :, 0:n], ALU.mult
                                    ).then_inc(sw_ready, 1)

        def keys_dve(dve, c):
            col, n = chunk_of(c)
            cs = slice(col, col + n)
            dve.wait_ge(bc_ready, c + 1)
            if c:
                dve.wait_ge(c_new, 4 * c)
                dve.wait_ge(cup_ready, 4 * c)
            nc.vector.tensor_copy(a_sb[:, :], hview(3, n)[:, :, n - 1])
            nc.vector.tensor_tensor(qs[:, :, 0:n], qk[:, 0:MH, cs], hview(3, n), ALU.mult).then_inc(qs_ready, 1)
            nc.vector.tensor_tensor(kts[0:n, :, :], hview(0, P, n),
                                    decay[0:n, :, n - 1:n].to_broadcast([n, MH, P]), ALU.mult
                                    ).then_inc(kts_ready, 1)

        def states_dve(dve, c):
            dve.wait_ge(qs_ready, c + 1)
            for h in range(MH):
                dve.wait_ge(cup_ready, 4 * c + h + 1)
                if c == 0:
                    ins = nc.vector.tensor_copy(cst_[:, h, :], ps[:, CB[h], 0:VH])
                else:
                    dve.wait_ge(c_new, 4 * c - 3 + h)
                    ins = nc.vector.scalar_tensor_tensor(out=cst_[:, h, :], in0=cst_[:, h, :],
                                                         scalar=a_sb[:, h:h + 1], in1=ps[:, CB[h], 0:VH],
                                                         op0=ALU.mult, op1=ALU.add)
                ins.then_inc(c_new, 1)

        def den_dve(dve, c):
            n = chunk_of(c)[1]
            dve.wait_ge(e_ready, c + 1)
            dve.wait_ge(abs_ready, c + 1)
            nc.vector.tensor_tensor(dd[:, :, 0:n], dd[:, :, 0:n], e_sb[:, :, 0:n], ALU.max).then_inc(dd_step, 1)
            dve.wait_ge(dd_step, 2 * c + 1)
            nc.vector.tensor_tensor(dd[:, :, 0:n], dd[:, :, 0:n], dd[:, :, 0:n], ALU.mult).then_inc(dd_step, 1)

        def root_dve(dve, c):
            n = chunk_of(c)[1]
            dve.wait_ge(dd_step, 2 * c + 2)
            dve.wait_ge(ss_ready, c + 1)
            if c:
                dve.wait_ge(numr_ready, c)
            nc.vector.scalar_tensor_tensor(out=zr[:, :, 0:n], in0=dd[:, :, 0:n], scalar=EPS,
                                           in1=hview(7, n), op0=ALU.mult, op1=ALU.add).then_inc(z_ready, 1)

        def y_dve1(dve, c):
            col, n = chunk_of(c)
            cs = slice(col, col + n)
            dve.wait_ge(r_ready, c + 1)
            if c:
                dve.wait_ge(ylo_ready, c)
            for b in range(2):
                last = nc.vector.tensor_tensor(
                    numr[:, 2 * b:2 * b + 2, :, 0:n], num_banks(5 + b, n),
                    zr[:, 2 * b:2 * b + 2, 0:n].unsqueeze(2).to_broadcast([P, 2, 2, n]), ALU.mult)
            last.then_inc(numr_ready, 1)

        def y_gate_dve(dve, c):
            col, n = chunk_of(c)
            cs = slice(col, col + n)
            dve.wait_ge(numr_ready, c + 1)
            nf = numr[:, :, :, 0:n].rearrange("p h c n -> p (h c) n")
            if c in (0, 1, 1 + NBLK // 2):
                dve.wait_ge(og_in[min(c, 2)], 16)
            nc.vector.tensor_tensor(nf, nf, og[:, :, cs], ALU.mult).then_inc(y_ready, 1)

        def y_dve2(dve, c):
            col, n = chunk_of(c)
            cs = slice(col, col + n)
            dve.wait_ge(yhi_ready, c + 1)
            nc.vector.tensor_tensor(y_lo[:, :, cs], numr[:, :, :, 0:n].rearrange("p h c n -> p (h c) n"),
                                    y_hi[:, :, cs].bitcast(F32), ALU.subtract).then_inc(ylo_ready, 1)

        def chunks_dve(dve):
            rr_dve(dve, 0)
            scores_dve(dve, 0)
            keys_dve(dve, 0)
            rr_dve(dve, 1)
            for c in range(TILES):
                states_dve(dve, c)
                if c:
                    y_dve2(dve, c - 1)
                den_dve(dve, c)
                root_dve(dve, c)
                if c == NBLK:
                    s_rr_dve(dve)
                y_dve1(dve, c)
                if c < NBLK:
                    scores_dve(dve, c + 1)
                    keys_dve(dve, c + 1)
                else:
                    s_scores_dve(dve)
                y_gate_dve(dve, c)
                if c + 1 < NBLK:
                    rr_dve(dve, c + 2)
            y_dve2(dve, TILES - 1)

        def decay_act(act, c):
            n = chunk_of(c)[1]
            act.wait_ge(d_ready, c + 1)
            if c:
                act.wait_ge(kts_ready, c)
            nc.scalar.activation(decay[0:n, :, 0:n], hview(2, n, n), ACT.Exp).then_inc(decay_ready, 1)

        def e_act(act, c):
            n = chunk_of(c)[1]
            act.wait_ge(bc_ready, c + 1)
            if c:
                act.wait_ge(dd_step, 2 * c)
            nc.scalar.activation(e_sb[:, :, 0:n], hview(4, n), ACT.Copy).then_inc(e_ready, 1)

        def outputs_act(act, c):
            n = chunk_of(c)[1]
            act.wait_ge(num_ready, c + 1)
            if c:
                act.wait_ge(ss_ready, c)
                act.wait_ge(z_ready, c)
            nc.scalar.activation(dd[:, :, 0:n], hview(7, n), ACT.Abs).then_inc(abs_ready, 1)
            for b in range(2):
                last = nc.scalar.activation(nsq[:, 2 * b:2 * b + 2, :, 0:n], num_banks(5 + b, n), ACT.Square,
                                            scale=DV ** -0.5)
            last.then_inc(nsq_ready, 1)

        def root_act(act, c):
            n = chunk_of(c)[1]
            act.wait_ge(z_ready, c + 1)
            nc.scalar.activation(zr[:, :, 0:n], zr[:, :, 0:n], ACT.Ln).then_inc(ln_z, 1)
            act.wait_ge(ln_z, c + 1)
            nc.scalar.activation(zr[:, :, 0:n], zr[:, :, 0:n], ACT.Exp, scale=-0.5).then_inc(r_ready, 1)

        def y_act1(act, c):
            col, n = chunk_of(c)
            cs = slice(col, col + n)
            act.wait_ge(y_ready, c + 1)
            nc.scalar.activation(y_hi[:, :, cs], numr[:, :, :, 0:n].rearrange("p h c n -> p (h c) n"), ACT.Copy
                                 ).then_inc(yhi_ready, 1)

        def chunks_act(act):
            decay_act(act, 0)
            e_act(act, 0)
            for c in range(TILES):
                outputs_act(act, c)
                root_act(act, c)
                if c < NBLK:
                    decay_act(act, c + 1)
                if c < NBLK:
                    e_act(act, c + 1)
                else:
                    s_decay_act(act)
                y_act1(act, c)

        def c0_load(sp):
            for b in range(NB):
                sp.wait_ge(cup_ready, 4 * (b + 2))
                sp.dma_start(c0[:, b, :, 0:DV], a["state_C"][0, b].rearrange("h k v -> k h v")).then_inc(c0_in, 16)
            sp.wait_ge(c_new, 4 * TILES)
            sp.dma_start(out[6][0, 0].rearrange("h k v -> k h v"), cst_[:, :, 0:DV]).then_inc(c0_out, 16)

        SC = slice(COL_S, COL_M)
        SN = SAMPLE

        def s_pe(pe):
            pe.wait_ge(c_new, 4 * TILES)
            pe.wait_ge(n_in, 16)
            nc.tensor.transpose(ps[:, 1, 256:256 + NB * MH], n_rows[0:NB * MH, :], ident[0:NB * MH, 0:NB * MH])
            nc.tensor.transpose(ps[0:SN, 1, 384:384 + P], rows_m[:, SC], ident)
            for h in range(MH):
                last = nc.tensor.transpose(ps[0:SN, 0, P * h:P * h + P], qk[:, MH + h, SC], ident)
            for h in range(MH):
                last = nc.tensor.matmul(ps[0:SN, 1, SN * h:SN * h + SN], qk[:, MH + h, SC], qk[:, h, SC],
                                        start=True, stop=True)
            pe.wait_ge(sm_dve, 1)
            nc.tensor.matmul(ps[0:SN, 2, 0:MH * SN], ident[0:SN, 0:SN],
                             own_causal[0:SN, :].unsqueeze(1).to_broadcast([SN, MH, SN]), start=True, stop=False)
            for h in range(MH):
                last = nc.tensor.matmul(ps[0:SN, 2, SN * h:SN * h + SN], rows_u[0:64, SC], rr[0:64, h, 0:SN],
                                        start=False, stop=h == MH - 1)
            last.then_inc(sm_pe, 1)
            for h in range(MH):
                last = nc.tensor.matmul(ps[:, 3, SN * h:SN * h + SN], row_of(64 + h),
                                        rows_m[:, SC], start=True, stop=True)
            last.then_inc(sm_pe, 1)
            pe.wait_ge(sm_dve, 3)
            pe.wait_ge(numr_ready, TILES)
            pe.wait_ge(z_ready, TILES)
            pe.wait_ge(c0_in, 16 * NB)
            for h in range(MH):
                o = ps[0:SN, 4 + h, 0:VH]
                nc.tensor.matmul(o, sw[0:SN, h, 0:SN], v[0:SN, NBLK, h, :], start=True, stop=False)
                for b in range(NB):
                    last = nc.tensor.matmul(o, qz[:, h, b, :], c0[:, b, h, :], start=False, stop=b == NB - 1)
            last.then_inc(sm_pe, 1)
            pe.wait_ge(sm_act, 1)
            pe.wait_ge(sm_dve, 4)
            for b in range(NB):
                if b == 2:
                    pe.wait_ge(sm_dve, 8)
                    for f in range(KC):
                        last = nc.tensor.transpose(ps[:, 4, SN * f:SN * f + SN],
                                                   y_s[:, f // 2, P * (f % 2):P * (f % 2) + P], ident[0:SN, 0:SN])
                    last.then_inc(sm_pe, 1)
                pe.wait_ge(sm_kb, b + 1)
                for h in range(MH):
                    if b:
                        pe.wait_ge(sm_c, 4 * b - 3 + h)
                    nc.tensor.matmul(ps[:, h, 0:VH], kbs[b % 2][:, h, :], v[0:64, NBLK, h, :],
                                     start=True, stop=True).then_inc(sm_cup, 1)
            pe.wait_ge(n_step, 2)
            nc.tensor.transpose(ps[0:NB * MH + MH, 6, 0:P], n_cols[:, :], ident).then_inc(n_t, 1)

        kbs = [at(f"kb{i}", R2 + 16384 + 8192 + 4128 + 32 + 512 + 2048 * i, [64, MH, P]) for i in range(2)]
        kt_s = at("kt_s", R2 + 2048 * 3, [SAMPLE, MH, P])
        qz = at("qz", R2 + 16384, [P, MH, NB, SAMPLE])
        y_s = at("y_s", R2 + 16384 + 4096, [SAMPLE, MH, DV])
        y_f = at("y_f", R2 + 2048 * 5, [P, KC, SAMPLE])
        s_den = at("s_den", R2 + 2048 * 5 + 1024, [SAMPLE, 4, MH])
        sm_kb, sm_cup, sm_c = sem("sm_kb"), sem("sm_cup"), sem("sm_c")
        n_rows = at("n_rows", R2 + 33344, [NB * MH + MH, P])
        n_cols = at("n_cols", R2 + 33344 + 512, [P, NB * MH + MH])
        n_step, n_t = sem("n_step"), sem("n_t")
        qz_zero = sem("qz_zero")

        def s_rr_dve(dve):
            dve.wait_ge(d_ready, TILES)
            nc.vector.tensor_tensor(rr[0:64, :, 0:SN],
                                    rows_m[0:64, SC].unsqueeze(1).to_broadcast([64, MH, SN]),
                                    pair[0:64, :].unsqueeze(2).to_broadcast([64, MH, SN]),
                                    ALU.mult).then_inc(sm_dve, 1)

        def s_scores_dve(dve):
            def inc(ins):
                ins.then_inc(sm_dve, 1)

            nc.vector.memset(qz[:, :, :, :], 0.0)
            for kb in kbs:
                last = nc.vector.memset(kb[SAMPLE:64, :, :], 0.0)
            last.then_inc(qz_zero, 1)
            dve.wait_ge(sm_pe, 1)
            dve.wait_ge(sm_act, 1)
            dve.wait_ge(cup_ready, 4 * TILES)
            nc.vector.tensor_copy(c0[:, :, :, DV:VH], ps[:, 1, 256:256 + NB * MH].rearrange(
                "p (b h a) -> p b h a", b=NB, a=1)).then_inc(n_step, 1)
            nc.vector.tensor_copy(s_den[:, 1, :], ps[0:SN, 1, 384 + 96:384 + 96 + MH])
            inc(nc.vector.tensor_tensor(sw[0:SN, :, 0:SN], hview(1, SN, SN), decay[0:SN, :, 0:SN], ALU.mult))
            dve.wait_ge(sm_pe, 2)
            dve.wait_ge(qz_zero, 1)
            nc.vector.tensor_copy(a_s[:, :, :], hview(3, SN))
            for b in range(NB):
                bs = slice(NS * b, NS * b + NS)
                last = nc.vector.tensor_tensor(qz[:, :, b, bs], qk[:, 0:MH, COL_S + NS * b:COL_S + NS * b + NS],
                                               hview(3, SN)[:, :, bs], ALU.mult)
            inc(last)
            inc(nc.vector.tensor_copy(kt_s[:, :, :], hview(0, P, SN)))

        def s_dve(dve):
            def inc(ins):
                ins.then_inc(sm_dve, 1)

            dve.wait_ge(sm_dve, 4)
            dve.wait_ge(n_step, 1)
            yv = y_s[:, :, :]
            for b in range(NB + 1):
                if b < NB:
                    if b >= 2:
                        dve.wait_ge(sm_cup, 4 * (b - 1))
                    nc.vector.tensor_tensor(kbs[b % 2][0:SAMPLE, :, :], kt_s[:, :, :],
                                            decay[0:SN, :, NS * b + NS - 1:NS * b + NS].to_broadcast([SN, MH, P]),
                                            ALU.mult).then_inc(sm_kb, 1)
                if b == 1:
                    dve.wait_ge(sm_act, 2)
                    inc(nc.vector.tensor_tensor(s_den[:, 0, :], s_den[:, 0, :], s_den[:, 1, :], ALU.max))
                    dve.wait_ge(sm_dve, 5)
                    inc(nc.vector.reciprocal(s_den[:, 2, :], s_den[:, 0, :]))
                    dve.wait_ge(sm_dve, 6)
                    inc(nc.vector.tensor_tensor(yv, ps[0:SN, 4:8, 0:DV],
                                                s_den[:, 2, :].unsqueeze(2).to_broadcast([SN, MH, DV]),
                                                ALU.mult))
                if b == 2:
                    dve.wait_ge(sm_act, 4)
                    inc(nc.vector.tensor_tensor(yv, yv, s_den[:, 3, :].unsqueeze(2).to_broadcast([SN, MH, DV]),
                                                ALU.mult))
                if b == 4:
                    dve.wait_ge(sm_pe, 4)
                    inc(nc.vector.tensor_tensor(y_f[:, :, :], ps[:, 4, 0:KC * SN].rearrange("p (f n) -> p f n", f=KC),
                                                og[:, :, SC], ALU.mult))
                if b == 6:
                    dve.wait_ge(sm_act, 5)
                    inc(nc.vector.tensor_tensor(y_lo[:, :, SC], y_f[:, :, :], y_hi[:, :, SC].bitcast(F32),
                                                ALU.subtract))
                if b:
                    for h in range(MH):
                        dve.wait_ge(sm_cup, 4 * (b - 1) + h + 1)
                        nc.vector.scalar_tensor_tensor(out=c0[:, b - 1, h, :], in0=c0[:, b - 1, h, :],
                                                       scalar=a_s[:, h, NS * b - 1:NS * b],
                                                       in1=ps[:, h, 0:VH], op0=ALU.mult, op1=ALU.add
                                                       ).then_inc(sm_c, 1)
            dve.wait_ge(sm_c, 4 * NB)
            nc.vector.tensor_copy(n_cols[:, 0:NB * MH].rearrange("p (b h a) -> p b h a", b=NB, a=1),
                                  c0[:, :, :, DV:VH])
            nc.vector.tensor_copy(n_cols[:, NB * MH:].unsqueeze(2), cst_[:, :, DV:VH]).then_inc(n_step, 1)
            dve.wait_ge(n_t, 1)
            nc.vector.tensor_copy(n_rows[:, :], ps[0:NB * MH + MH, 6, 0:P]).then_inc(n_step, 1)

        def s_decay_act(act):
            act.wait_ge(sm_pe, 1)
            act.wait_ge(kts_ready, TILES)
            nc.scalar.activation(decay[0:SN, :, 0:SN], hview(2, SN, SN), ACT.Exp).then_inc(sm_act, 1)

        def s_act(act):
            act.wait_ge(sm_pe, 3)
            nc.scalar.activation(s_den[:, 0, :], ps[0:SN, 4:8, DV], ACT.Abs).then_inc(sm_act, 1)
            act.wait_ge(sm_dve, 7)
            for h in range(MH):
                last = nc.scalar.activation(y_sq[:, h, :], y_s[:, h, :], ACT.Square, scale=DV ** -0.5,
                                            accum_out=s_den[:, 3, h:h + 1])
            last.then_inc(sm_act, 1)
            act.wait_ge(sm_act, 3)
            nc.scalar.activation(s_den[:, 3, :], s_den[:, 3, :], ACT.Ln, bias=eps[0:SN, 0:1]).then_inc(ln_z, 1)
            act.wait_ge(ln_z, TILES + 1)
            nc.scalar.activation(s_den[:, 3, :], s_den[:, 3, :], ACT.Exp, scale=-0.5).then_inc(sm_act, 1)
            act.wait_ge(sm_dve, 9)
            nc.scalar.activation(y_hi[:, :, SC], y_f[:, :, :], ACT.Copy).then_inc(sm_act, 1)

        y_sq = at("y_sq", R2 + 2048 * 6, [SAMPLE, MH, DV])

        def s_store(sp):
            for b in range(NB):
                sp.wait_ge(sm_c, 4 * (b + 1))
                sp.dma_start(out[9][0, b].rearrange("h k v -> k h v"), c0[:, b, :, 0:DV]).then_inc(c0_out, 16)
            sp.wait_ge(n_step, 3)
            sp.dma_start(out[10][0].rearrange("b h k -> (b h) k"), n_rows[0:NB * MH, :]).then_inc(c0_out, 16)
            sp.dma_start(out[7][0, 0], n_rows[NB * MH:, :]).then_inc(c0_out, 16)
            sp.wait_ge(sm_dve, 10)
            sp.wait_ge(c0_out, 16 * STATES_OUT)
            for f in range(KC):
                sp.dma_start(x2[:, f, :], scratch["x1"][:, f, :]).then_inc(x2_back, 16)

        STATES_OUT = NB + 3

        def out_pe(pe):
            pe.wait_ge(sm_dve, 10)
            for c in range(KC):
                pe_unit(pe, U_OUT + c, N_OUT + c, y_hi, y_lo)

        y_st = at("y_st", R0, [P, TILES, D])
        y_t, y_act, y_dve, y_out = sem("y_t"), sem("y_by_act"), sem("y_by_dve"), sem("y_out")

        def y_pe(pe):
            pe.wait_ge(out_free, N_MLP1 + 12 * SLICES)
            for i in range(2 * TILES):
                half, t = divmod(i, TILES)
                n = x_rows(t)
                if i >= 8:
                    pe.wait_ge((y_act, y_dve)[i % 2], (i - 8) // 2 + 1)
                for f in range(4):
                    last = nc.tensor.transpose(ps[0:n, i % 8, P * f:P * f + P],
                                               x2[:, 4 * half + f, t * P:t * P + n], ident)
                last.then_inc(y_t, 1)

        def y_take(eng, i):
            half, t = divmod(i, TILES)
            n = x_rows(t)
            eng.wait_ge(y_t, i + 1)
            return y_st[0:n, t, 512 * half:512 * half + 512], ps[0:n, i % 8, :]

        def y_store(sp):
            for i in range(2 * TILES):
                half, t = divmod(i, TILES)
                sp.wait_ge((y_act, y_dve)[i % 2], i // 2 + 1)
                cols = slice(512 * half, 512 * half + 512)
                if t < NBLK:
                    sp.dma_start(out[0][0, t * P:t * P + P, cols], y_st[:, t, cols]).then_inc(y_out, 16)
                else:
                    sp.dma_start(out[1].rearrange("b s d -> (b s) d")[:, cols], y_st[0:SAMPLE, t, cols]
                                 ).then_inc(y_out, 16)
            sp.wait_ge(y_out, 16 * 2 * TILES)

        block = ctx.enter_context(nc.Block())

        @block.sync
        def _(sp):
            load_x(sp)
            for r in range(U_MLP0 // 2):
                if r >= 2:
                    sp.wait_ge(w_lo_ready, 2 * r - 2)
                load_qkv(sp, r) if r < 6 else load_wo(sp, r)
                if r == 1:
                    line_write(sp)
                    sp.wait_ge(x_by_act, TILES)
                    sp.wait_ge(x_by_dve, TILES)
                    sp.dma_start(scratch["x0"], x[:, :, :]).then_inc(x_saved, 16)
                if r == 3:
                    bias_read(sp)
                if r == U_MLP0 // 2 - 2:
                    sample_loads(sp)
                    caches_v(sp)
                    caches_k(sp)
                    reload_x(sp)
            with sp.Fori(0, SLICES) as i:
                mlp_slice_sp(sp, 0, U_MLP0, i)
            for r in range(U_IN // 2, U_MLP1 // 2):
                sp.wait_ge(w_lo_ready, 2 * r - 2)
                if r < U_OUT // 2:
                    load_cols(sp, a["mlstm_w_in"][0], r, 256 * (r - U_IN // 2))
                else:
                    load_cols(sp, a["mlstm_w_out"][0], r, 256 * (r - U_OUT // 2))
                if r == U_OUT // 2 + 1:
                    og_load(sp)
                    c0_load(sp)
                    s_store(sp)
            with sp.Fori(0, SLICES) as i:
                mlp_slice_sp(sp, 1, U_MLP1, i)
            y_store(sp)

        @block.gpsimd
        def _(pool):
            nc.gpsimd.memset(rel_ext[BUCKETS:BUCKETS + 1, :], 1.0).then_inc(rel_one, 1)
            bias_pool(pool)
            for n in range(NG):
                att_scale_pool(pool, n)
            gates_pool(pool)
            gates_out(pool)
            og_pool(pool)
            pool.wait_ge(stored, 16 * 2)

        @block.scalar
        def _(act):
            act.preload_act_table_set("natural_log_exp_and_others")
            act.dma_start(cst[:, :], a["const"]).then_inc(ident_in, 16)
            act.dma_start(gain_rows[0:16, :], a["norm_mix"].rearrange("m (k p) -> (m k) p", p=P)).then_inc(gains_in, 16)
            act.dma_start(gain_rows[16:32, :], a["norm_mlp"].rearrange("m (k p) -> (m k) p", p=P)).then_inc(gains_in, 16)
            act.dma_start(gain_rows[32:40, :], a["mlstm_out_norm"].rearrange("m (k p) -> (m k) p", p=P)).then_inc(gains_in, 16)
            for dst, src in small:
                act.dma_start(dst, src, allow_slow_non_contiguous=True).then_inc(const_in, 16)
            for c in range(TILES):
                o, i = take_x(act, c, 0)
                nc.scalar.activation(o, i, ACT.Copy).then_inc(x_by_act, 1)
            act.wait_ge(x_by_act, TILES)
            act.wait_ge(x_by_dve, TILES)
            act.wait_ge(gains_ready, 1)
            for f in range(KC):
                norm_act(act, 0, f, x, h_hi)
                if f in (1, 2):
                    split_hi_static(act, f - 1)
            qkv_act(act)
            att_act(act)
            sample_act(act)
            project_act(act, U_WO, N_WO, 1, x, h_hi)
            norm_rstd_act(act, 1)
            act.wait_ge(wg_zero, 1)
            for dst, src in wg_cols:
                last = nc.scalar.activation(wg_hi[:, :, dst], wg_raw[:, :, src], ACT.Copy)
            last.then_inc(wg_split_hi, 1)
            with act.Fori(0, SLICES - 1) as i:
                mlp_slice_act(act, 0, U_MLP0, N_MLP0, i)
            mlp_slice_act(act, 0, U_MLP0, N_MLP0, SLICES - 1, norm=(2, x, h_hi))
            norm_rstd_act(act, 2)
            in_act(act)
            act.preload_act_table_set("natural_log_exp_and_others")
            chunks_act(act)
            s_act(act)
            act.wait_ge(c0_out, 16 * STATES_OUT)
            project_act(act, U_OUT, N_OUT, 3, x2, h_hi2)
            norm_rstd_act(act, 3)
            with act.Fori(0, SLICES - 1) as i:
                mlp_slice_act(act, 1, U_MLP1, N_MLP1, i)
            mlp_slice_act(act, 1, U_MLP1, N_MLP1, SLICES - 1, 8 - AHEAD)
            for i in range(0, 2 * TILES, 2):
                o, src = y_take(act, i)
                nc.scalar.activation(o, src, ACT.Copy).then_inc(y_act, 1)

        @block.vector
        def _(dve):
            nc.vector.memset(eps[:, :], EPS)
            nc.vector.memset(x[:, :, T:TP], 0.0)
            dve.wait_ge(line_mm, 1)
            nc.vector.tensor_copy(line[:, :], ps[0:QH, 0, 0:LINE]).then_inc(line_c, 1)
            for c in range(TILES):
                o, i = take_x(dve, c, 1)
                nc.vector.tensor_copy(o, i).then_inc(x_by_dve, 1)
            dve.wait_ge(gains_t, 1)
            nc.vector.tensor_copy(gains[:, :, :].rearrange("p m k -> p (m k)"), ps[:, 7, 0:5 * KC]
                                  ).then_inc(gains_ready, 1)
            dve.wait_ge(gains_ready, 1)
            dve.wait_ge(const_in, 16 * len(small))
            nc.vector.tensor_scalar(nsinks[:, :], sinks[:, :], -1.0, None, ALU.mult)
            nc.vector.tensor_scalar(bg15[:, :], bgate[:, :], 1.0 / CAP, None, ALU.mult)
            dve.wait_ge(x_by_dve, TILES)
            dve.wait_ge(x_by_act, TILES)
            for f in range(KC):
                norm_lo_dve(dve, 0, f, x, h_hi, h_lo)
                if f:
                    norm_acc_dve(dve, 0, f)
                if f in (1, 2):
                    split_lo_static(dve, f - 1)
            qkv_dve(dve)
            dve.wait_ge(qk_normed, 30)
            nc.vector.memset(o_hi[:, :, T:TP].bitcast(F32), 0.0)
            nc.vector.memset(o_lo[:, :, T:TP].bitcast(F32), 0.0)
            att_dve(dve)
            sample_dve2(dve)
            project_dve(dve, U_WO, N_WO, 1, x, h_hi, h_lo, x_back)
            nc.vector.memset(wg_hi[:, :, :].bitcast(F32), 0.0)
            nc.vector.memset(wg_lo[:, :, :].bitcast(F32), 0.0).then_inc(wg_zero, 1)
            dve.wait_ge(wg_split_hi, 1)
            for dst, src in wg_cols:
                last = nc.vector.tensor_tensor(wg_lo[:, :, dst], wg_raw[:, :, src], wg_hi[:, :, dst].bitcast(F32),
                                               ALU.subtract)
            last.then_inc(wg_split, 1)
            dve.wait_ge(norm_rstd, 2)
            with dve.Fori(0, SLICES - 1) as i:
                mlp_slice_dve(dve, 0, U_MLP0, N_MLP0, i, x)
            mlp_slice_dve(dve, 0, U_MLP0, N_MLP0, SLICES - 1, x, norm=(2, x, h_hi, h_lo))
            gates_dve(dve)
            in_dve(dve)
            dve.wait_ge(v2_taken, 24)
            dve.wait_ge(out_free, N_OUT)
            nc.vector.tensor_copy(v_m[:, :, :], v[SAMPLE:LAST, NBLK, :, :]).then_inc(vm_done, 1)
            nc.vector.memset(y_hi[:, :, T:TP].bitcast(F32), 0.0)
            dve.wait_ge(out_ready, N_OUT)
            nc.vector.memset(y_lo[:, :, T:TP].bitcast(F32), 0.0)
            chunks_dve(dve)
            s_dve(dve)
            project_dve(dve, U_OUT, N_OUT, 3, x2, h_hi2, h_lo2, x2_back)
            dve.wait_ge(norm_rstd, 4)
            with dve.Fori(0, SLICES - 1) as i:
                mlp_slice_dve(dve, 1, U_MLP1, N_MLP1, i, x2)
            mlp_slice_dve(dve, 1, U_MLP1, N_MLP1, SLICES - 1, x2, 8 - AHEAD)
            for i in range(1, 2 * TILES, 2):
                o, src = y_take(dve, i)
                nc.vector.tensor_copy(o, src).then_inc(y_dve, 1)

        @block.tensor
        def _(pe):
            pe.wait_ge(line_in, 32)
            pe.wait_ge(rel_one, 1)
            nc.tensor.matmul(ps[0:QH, 0, 0:LINE], rel_ext[:, :], bucket[:, :], start=True, stop=True
                             ).then_inc(line_mm, 1)
            pe.wait_ge(line_c, 1)
            load_pe(pe)
            pe.wait_ge(gains_in, 48)
            pe.wait_ge(x_by_dve, 8)
            nc.tensor.transpose(ps[:, 7, 0:5 * KC], gain_rows[:, :], ident[0:5 * KC, 0:5 * KC]
                                ).then_inc(gains_t, 1)
            qkv_pe(pe)
            att_pe(pe)
            sample_pe(pe)
            wo_pe(pe)
            for g in range(3):
                norm_pe(pe, 1, g)
            with pe.Fori(0, SLICES) as i:
                mlp_slice_pe(pe, 0, U_MLP0, N_MLP0, i, h_hi, h_lo)
            gates_pe(pe)
            in_pe(pe)
            pe.wait_ge(vm_done, 1)
            pe.wait_ge(gate_act, 4)
            pe.wait_ge(out_free, N_OUT)
            chunks_pe(pe)
            s_pe(pe)
            out_pe(pe)
            for g in range(3):
                norm_pe(pe, 3, g)
            with pe.Fori(0, SLICES) as i:
                mlp_slice_pe(pe, 1, U_MLP1, N_MLP1, i, h_hi2, h_lo2)
            y_pe(pe)


_INS = ["x_prompt", "x_sample", "cache_k", "cache_v", "state_C", "state_n", "state_m", "meta_tokens",
        "rel_table", "norm_mix", "norm_mlp", "attn_w_qkv", "attn_q_norm", "attn_k_norm", "attn_sinks",
        "attn_w_o", "mlstm_w_in", "mlstm_w_gate", "mlstm_b_gate", "mlstm_out_norm", "mlstm_w_out",
        "mlp_w_up", "mlp_w_down"]
_OUTS = [(1, SEQ, D), (NB, NS, D),
         (1, 1, WIN, KH, HD), (1, 1, WIN, KH, HD), (1, NB, WIN, KH, HD), (1, NB, WIN, KH, HD),
         (1, 1, MH, DK, DV), (1, 1, MH, DK), (1, 1, MH),
         (1, NB, MH, DK, DV), (1, NB, MH, DK), (1, NB, MH)]
_SCRATCH = {"x0": [P, KC, TP], "x1": [P, KC, TP], "og": [P, KC, TP], "line": [QH, BLK, LINE]}


def kernel(**inputs):
    import concourse.bacc as _bacc
    from concourse.bass_utils import run_bass_kernel_spmd as _run

    nc = _bacc.Bacc("TRN2", target_bir_lowering=False, num_devices=1)
    arrays, args = {}, {}
    for name in _INS:
        arr = np.ascontiguousarray(inputs[name])
        arrays[f"in_{name}"] = arr
        args[name] = nc.dram_tensor(f"in_{name}", arr.shape, F32, kind="ExternalInput").ap()
    consts = {"const": np.concatenate([CONST[k] for k in CONST], axis=1),
              "buckets": bucket_constant(), "keep": scan_constant()}
    for name, arr in consts.items():
        arr = np.ascontiguousarray(arr)
        arrays[f"in_{name}"] = arr
        args[name] = nc.dram_tensor(f"in_{name}", arr.shape, F32, kind="ExternalInput").ap()
    outs = [nc.dram_tensor(f"out_{i}", shape, F32, kind="ExternalOutput").ap() for i, shape in enumerate(_OUTS)]
    scratch = {k: nc.dram_tensor(f"scratch_{k}", s, F32, kind="Internal").ap() for k, s in _SCRATCH.items()}
    build(nc, args, outs, scratch)
    r = _run(nc, [arrays], core_ids=[0])
    return tuple(r.results[0][f"out_{i}"] for i in range(len(_OUTS)))
```
